# Optimizing a Trainium2 kernel written in Bass

```python
import math
import jax, jax.numpy as jnp
from jax import lax
import numpy as np

D_MODEL = 1024
BATCH = 1
SEQ = 1024
DEPTH = 1

MIX_DIM = D_MODEL
RWKV_HEADS = 8
RWKV_HEAD_DIM = 64
RWKV_DIM = RWKV_HEADS * RWKV_HEAD_DIM
LORA_W = 64
LORA_A = 64
LORA_G = 128
DIFF_HEADS = 4
DIFF_HEAD_DIM = 64
DIFF_DIM = DIFF_HEADS * 2 * DIFF_HEAD_DIM
RWKV_COLS = 3 * RWKV_DIM + LORA_W + LORA_A + LORA_G
DIFF_COLS = 3 * DIFF_DIM
IN_COLS = RWKV_COLS + DIFF_COLS
Q_BLOCK = 128
D_FF = 2816
CONV_WIDTH = 3
DECAY_SCALE = math.exp(-0.5)
RWKV_LN_EPS = 64e-5
NORM_EPS = 1e-6
SUBLN_EPS = 1e-5
NEG_INF = -1e30


def rms_norm(x, g, eps=NORM_EPS):
    x32 = x.astype(jnp.float32)
    y = x32 * lax.rsqrt(jnp.mean(x32 * x32, axis=-1, keepdims=True) + eps)
    return (y * g.astype(jnp.float32)).astype(x.dtype)

def alibi_slopes(n):
    return jnp.array([2.0 ** (-8.0 * (i + 1) / n) for i in range(n)], jnp.float32)

def token_shift(p):
    return jnp.pad(p[:, :-1], ((0, 0), (1, 0), (0, 0)))

def rwkv7_mix(p, mu, w_decay_up, w_decay0, w_iclr_up, w_iclr0, w_gate_up,
              k_k, k_a, r_k, ln_x_w, ln_x_b):
    B, S, _ = p.shape
    p = p.astype(jnp.float32)
    xs = p + (token_shift(p) - p) * mu
    cuts = [RWKV_DIM, 2 * RWKV_DIM, 3 * RWKV_DIM, 3 * RWKV_DIM + LORA_W,
            3 * RWKV_DIM + LORA_W + LORA_A]
    r, k, v, w_lo, a_lo, g_lo = jnp.split(xs, cuts, axis=-1)
    decay = jnp.exp(-DECAY_SCALE * jax.nn.sigmoid(w_decay0 + jnp.tanh(w_lo) @ w_decay_up))
    a = jax.nn.sigmoid(w_iclr0 + a_lo @ w_iclr_up)
    g = jax.nn.sigmoid(g_lo) @ w_gate_up
    hs = (B, S, RWKV_HEADS, RWKV_HEAD_DIM)
    kk = (k * k_k).reshape(hs)
    kk = kk / jnp.maximum(jnp.linalg.norm(kk, axis=-1, keepdims=True), 1e-12)
    k = k * (1.0 + (a - 1.0) * k_a)
    r, k, v, decay, a = (t.reshape(hs) for t in (r, k, v, decay, a))

    def step(state, inp):
        r_t, w_t, k_t, v_t, kk_t, a_t = inp
        sa = jnp.einsum('bhvk,bhk->bhv', state, -kk_t)
        state = (state * w_t[:, :, None, :]
                 + sa[..., None] * (kk_t * a_t)[:, :, None, :]
                 + v_t[..., None] * k_t[:, :, None, :])
        return state, jnp.einsum('bhvk,bhk->bhv', state, r_t)

    seq_major = tuple(jnp.moveaxis(t, 1, 0) for t in (r, decay, k, v, kk, a))
    s0 = jnp.zeros((B, RWKV_HEADS, RWKV_HEAD_DIM, RWKV_HEAD_DIM), jnp.float32)
    _, y = lax.scan(step, s0, seq_major)
    y = jnp.moveaxis(y, 0, 1)
    y = y + jnp.sum(r * k * r_k, axis=-1, keepdims=True) * v
    mean = jnp.mean(y, axis=-1, keepdims=True)
    var = jnp.mean(jnp.square(y - mean), axis=-1, keepdims=True)
    y = ((y - mean) * lax.rsqrt(var + RWKV_LN_EPS)).reshape(B, S, RWKV_DIM)
    y = y * ln_x_w + ln_x_b
    return y * g

def diff_attention(q, k, v, lam, slopes):
    B, S, H, _, d = q.shape
    nb = S // Q_BLOCK
    scale = d ** -0.5
    qh = q.transpose(0, 2, 3, 1, 4)
    kh = k.transpose(0, 2, 3, 1, 4).astype(jnp.float32)
    vh = v.transpose(0, 2, 1, 3).astype(jnp.float32)
    qb = qh.reshape(B, H, 2, nb, Q_BLOCK, d).transpose(3, 0, 1, 2, 4, 5)
    kpos = jnp.arange(S)

    def block(args):
        qblk, i = args
        qpos = i * Q_BLOCK + jnp.arange(Q_BLOCK)
        dist = (qpos[:, None] - kpos[None, :]).astype(jnp.float32)
        s = jnp.einsum('bhcqd,bhckd->bhcqk', qblk.astype(jnp.float32), kh) * scale
        s = s - slopes[None, :, None, None, None] * dist
        s = jnp.where(dist >= 0, s, NEG_INF)
        pr = jax.nn.softmax(s, axis=-1)
        attn = pr[:, :, 0] - lam * pr[:, :, 1]
        return jnp.einsum('bhqk,bhkv->bhqv', attn, vh)

    out = lax.map(block, (qb, jnp.arange(nb)))
    return out.transpose(1, 0, 3, 2, 4).reshape(B, S, H, 2 * d)

def causal_dwconv(h, w, b):
    C = h.shape[-1]
    y = lax.conv_general_dilated(h, w[:, None, :].astype(h.dtype), window_strides=(1,),
                                 padding=((CONV_WIDTH - 1, 0),),
                                 dimension_numbers=('NWC', 'WIO', 'NWC'),
                                 feature_group_count=C)
    return y + b.astype(h.dtype)

def first_inputs(seed: int = 0) -> dict:
    key = jax.random.key(seed)
    ks = jax.random.split(key, 32)
    L = DEPTH

    def nrm(k, shape, s):
        return jax.random.normal(k, shape, jnp.float32) * s

    return {
        "x": nrm(ks[0], (BATCH, SEQ, D_MODEL), 1.0),
        "ln_attn_pre": 1.0 + nrm(ks[1], (L, D_MODEL), 0.05),
        "w_in": nrm(ks[2], (L, D_MODEL, IN_COLS), D_MODEL ** -0.5),
        "mu_shift": jax.random.uniform(ks[3], (L, RWKV_COLS), jnp.float32),
        "w_decay_up": nrm(ks[4], (L, LORA_W, RWKV_DIM), LORA_W ** -0.5),
        "w_decay0": nrm(ks[5], (L, RWKV_DIM), 0.5),
        "w_iclr_up": nrm(ks[6], (L, LORA_A, RWKV_DIM), LORA_A ** -0.5),
        "w_iclr0": nrm(ks[7], (L, RWKV_DIM), 0.1),
        "w_gate_up": nrm(ks[8], (L, LORA_G, RWKV_DIM), LORA_G ** -0.5),
        "k_k": 0.85 + nrm(ks[9], (L, RWKV_DIM), 0.05),
        "k_a": 1.0 + nrm(ks[10], (L, RWKV_DIM), 0.05),
        "r_k": nrm(ks[11], (L, RWKV_HEADS, RWKV_HEAD_DIM), 0.1),
        "ln_x_w": 1.0 + nrm(ks[12], (L, RWKV_DIM), 0.05),
        "ln_x_b": nrm(ks[13], (L, RWKV_DIM), 0.02),
        "lambda_q1": nrm(ks[14], (L, DIFF_HEAD_DIM), 0.1),
        "lambda_k1": nrm(ks[15], (L, DIFF_HEAD_DIM), 0.1),
        "lambda_q2": nrm(ks[16], (L, DIFF_HEAD_DIM), 0.1),
        "lambda_k2": nrm(ks[17], (L, DIFF_HEAD_DIM), 0.1),
        "diff_subln": 1.0 + nrm(ks[18], (L, 2 * DIFF_HEAD_DIM), 0.05),
        "w_out": nrm(ks[19], (L, MIX_DIM, D_MODEL), MIX_DIM ** -0.5),
        "ln_attn_post": 1.0 + nrm(ks[20], (L, D_MODEL), 0.05),
        "ln_ffn_pre": 1.0 + nrm(ks[21], (L, D_MODEL), 0.05),
        "w_up": nrm(ks[22], (L, D_MODEL, 2 * D_FF), D_MODEL ** -0.5),
        "conv_w": nrm(ks[23], (L, CONV_WIDTH, 2 * D_FF), CONV_WIDTH ** -0.5),
        "conv_b": nrm(ks[24], (L, 2 * D_FF), 0.02),
        "w_down": nrm(ks[25], (L, D_FF, D_MODEL), D_FF ** -0.5),
        "ln_ffn_post": 1.0 + nrm(ks[26], (L, D_MODEL), 0.05),
    }

def first_block(x, ln_attn_pre, w_in, mu_shift, w_decay_up, w_decay0, w_iclr_up, w_iclr0,
              w_gate_up, k_k, k_a, r_k, ln_x_w, ln_x_b, lambda_q1, lambda_k1, lambda_q2,
              lambda_k2, diff_subln, w_out, ln_attn_post, ln_ffn_pre, w_up, conv_w, conv_b,
              w_down, ln_ffn_post):
    B, S, _ = x.shape
    slopes = alibi_slopes(DIFF_HEADS)
    h = x
    for l in range(DEPTH):
        xn = rms_norm(h, ln_attn_pre[l])
        proj = xn @ w_in[l]
        y_rwkv = rwkv7_mix(proj[..., :RWKV_COLS], mu_shift[l], w_decay_up[l], w_decay0[l],
                           w_iclr_up[l], w_iclr0[l], w_gate_up[l], k_k[l], k_a[l], r_k[l],
                           ln_x_w[l], ln_x_b[l])
        dq, dk, dv = jnp.split(proj[..., RWKV_COLS:], 3, axis=-1)
        dq = dq.reshape(B, S, DIFF_HEADS, 2, DIFF_HEAD_DIM)
        dk = dk.reshape(B, S, DIFF_HEADS, 2, DIFF_HEAD_DIM)
        dv = dv.reshape(B, S, DIFF_HEADS, 2 * DIFF_HEAD_DIM)
        lam_init = 0.8 - 0.6 * math.exp(-0.3 * l)
        lam = (jnp.exp(jnp.sum(lambda_q1[l] * lambda_k1[l]).astype(jnp.float32))
               - jnp.exp(jnp.sum(lambda_q2[l] * lambda_k2[l]).astype(jnp.float32)) + lam_init)
        o = diff_attention(dq, dk, dv, lam, slopes)
        o = rms_norm(o, diff_subln[l], eps=SUBLN_EPS) * (1.0 - lam_init)
        mix = jnp.concatenate([y_rwkv, o.reshape(B, S, DIFF_DIM)], axis=-1).astype(h.dtype)
        h = h + rms_norm(mix @ w_out[l], ln_attn_post[l])
        hn = rms_norm(h, ln_ffn_pre[l])
        u = causal_dwconv(hn @ w_up[l], conv_w[l], conv_b[l])
        gate, val = jnp.split(u, 2, axis=-1)
        f = (jax.nn.gelu(gate, approximate=True) * val) @ w_down[l]
        h = h + rms_norm(f, ln_ffn_post[l])
    return h


CHUNK = 64
HEAD_DIM = 64
H_FOX = 8
H_CHK = 8
W_FOX = H_FOX * HEAD_DIM
W_CHK = H_CHK * HEAD_DIM
LEFT_CHUNKS = 8
MAX_REL = 128
N_REL = 2 * MAX_REL + 1
N_BRANCH = 2
D_FF_2 = 4 * D_MODEL
EPS = 1e-6
NEG = -1e30
N_IN = 3 * W_FOX + H_FOX + 3 * W_CHK + N_BRANCH * D_MODEL
SPLITS = tuple(np.cumsum([W_FOX, W_FOX, W_FOX, H_FOX, W_CHK, W_CHK, W_CHK]).tolist())


def rms_norm_2(x, g):
    xf = x.astype(jnp.float32)
    y = xf * lax.rsqrt(jnp.mean(xf * xf, axis=-1, keepdims=True) + EPS)
    return (y * g.astype(jnp.float32)).astype(x.dtype)

def to_heads(t, h):
    b, s, _ = t.shape
    return t.reshape(b, s, h, HEAD_DIM).transpose(0, 2, 1, 3)

def from_heads(t):
    b, h, s, d = t.shape
    return t.transpose(0, 2, 1, 3).reshape(b, s, h * d)

def forgetting_attention(q, k, v, log_f):
    b, h, s, d = q.shape
    nblk = s // Q_BLOCK
    scale = 1.0 / math.sqrt(d)
    c = jnp.cumsum(log_f, axis=-1)
    qb = q.reshape(b, h, nblk, Q_BLOCK, d).transpose(2, 0, 1, 3, 4)
    cb = c.reshape(b, h, nblk, Q_BLOCK).transpose(2, 0, 1, 3)
    key_pos = jnp.arange(s, dtype=jnp.int32)

    def block(args):
        qi, ci, i = args
        sc = jnp.einsum('bhqd,bhkd->bhqk', qi, k, preferred_element_type=jnp.float32)
        sc = sc * scale + ci[..., None] - c[:, :, None, :]
        tq = i * Q_BLOCK + jnp.arange(Q_BLOCK, dtype=jnp.int32)
        mask = key_pos[None, :] <= tq[:, None]
        sc = jnp.where(mask, sc, NEG)
        p = jax.nn.softmax(sc, axis=-1).astype(v.dtype)
        return jnp.einsum('bhqk,bhkd->bhqd', p, v)

    out = lax.map(block, (qb, cb, jnp.arange(nblk, dtype=jnp.int32)))
    return out.transpose(1, 2, 0, 3, 4).reshape(b, h, s, d)

def chunk_band_attention(q, k, v, rel_bias):
    b, h, s, d = q.shape
    nblk = s // Q_BLOCK
    scale = 1.0 / math.sqrt(d)
    pad = LEFT_CHUNKS * CHUNK
    band = pad + Q_BLOCK
    kp = jnp.pad(k, ((0, 0), (0, 0), (pad, 0), (0, 0)))
    vp = jnp.pad(v, ((0, 0), (0, 0), (pad, 0), (0, 0)))
    qb = q.reshape(b, h, nblk, Q_BLOCK, d).transpose(2, 0, 1, 3, 4)

    def block(args):
        qi, i = args
        p0 = i * Q_BLOCK
        kb = lax.dynamic_slice_in_dim(kp, p0, band, axis=2)
        vb = lax.dynamic_slice_in_dim(vp, p0, band, axis=2)
        tq = p0 + jnp.arange(Q_BLOCK, dtype=jnp.int32)
        sk = p0 - pad + jnp.arange(band, dtype=jnp.int32)
        cq = tq // CHUNK
        ck = sk // CHUNK
        valid = (sk[None, :] >= 0) & (ck[None, :] <= cq[:, None]) & (ck[None, :] >= cq[:, None] - LEFT_CHUNKS)
        rel = jnp.clip(tq[:, None] - sk[None, :], -MAX_REL, MAX_REL) + MAX_REL
        bias = rel_bias[:, rel].astype(jnp.float32)
        sc = jnp.einsum('bhqd,bhkd->bhqk', qi, kb, preferred_element_type=jnp.float32)
        sc = jnp.where(valid, sc * scale + bias[None], NEG)
        p = jax.nn.softmax(sc, axis=-1).astype(vb.dtype)
        return jnp.einsum('bhqk,bhkd->bhqd', p, vb)

    out = lax.map(block, (qb, jnp.arange(nblk, dtype=jnp.int32)))
    return out.transpose(1, 2, 0, 3, 4).reshape(b, h, s, d)

def second_inputs(seed: int = 0) -> dict:
    key = jax.random.key(seed)
    ks = jax.random.split(key, 14)
    nrm = lambda k, shape, fan_in: jax.random.normal(k, shape, jnp.float32) * (fan_in ** -0.5)
    x = jax.random.normal(ks[0], (BATCH, SEQ, D_MODEL), jnp.float32)
    norm1 = 1.0 + 0.02 * jax.random.normal(ks[1], (DEPTH, D_MODEL), jnp.float32)
    w_in = nrm(ks[2], (DEPTH, D_MODEL, N_IN), D_MODEL)
    forget_bias = jnp.linspace(1.0, 6.0, H_FOX, dtype=jnp.float32)[None, :] + 0.1 * jax.random.normal(ks[3], (DEPTH, H_FOX), jnp.float32)
    rel_bias = 0.5 * jax.random.normal(ks[4], (DEPTH, H_CHK, N_REL), jnp.float32)
    w_branch_a = nrm(ks[5], (DEPTH, W_FOX, D_MODEL), W_FOX)
    w_branch_b = nrm(ks[6], (DEPTH, W_CHK, D_MODEL), W_CHK)
    w_out = nrm(ks[7], (DEPTH, D_MODEL, D_MODEL), D_MODEL)
    norm2 = 1.0 + 0.02 * jax.random.normal(ks[8], (DEPTH, D_MODEL), jnp.float32)
    w_up = nrm(ks[9], (DEPTH, D_MODEL, D_FF_2), D_MODEL)
    w_down = nrm(ks[10], (DEPTH, D_FF_2, D_MODEL), D_FF_2)
    final_norm = 1.0 + 0.02 * jax.random.normal(ks[11], (D_MODEL,), jnp.float32)
    return {"x": x, "norm1": norm1, "w_in": w_in, "forget_bias": forget_bias,
            "rel_bias": rel_bias, "w_branch_a": w_branch_a, "w_branch_b": w_branch_b,
            "w_out": w_out, "norm2": norm2, "w_up": w_up, "w_down": w_down,
            "final_norm": final_norm}

def second_block(x, norm1, w_in, forget_bias, rel_bias, w_branch_a, w_branch_b,
              w_out, norm2, w_up, w_down, final_norm):
    for l in range(DEPTH):
        h = rms_norm_2(x, norm1[l])
        proj = h @ w_in[l]
        qa, ka, va, fa, qc, kc, vc, gates = jnp.split(proj, SPLITS, axis=-1)
        log_f = jax.nn.log_sigmoid((fa + forget_bias[l]).astype(jnp.float32))
        log_f = log_f.transpose(0, 2, 1)
        o_a = from_heads(forgetting_attention(to_heads(qa, H_FOX), to_heads(ka, H_FOX),
                                              to_heads(va, H_FOX), log_f))
        o_b = from_heads(chunk_band_attention(to_heads(qc, H_CHK), to_heads(kc, H_CHK),
                                              to_heads(vc, H_CHK), rel_bias[l]))
        g_a, g_b = jnp.split(jax.nn.sigmoid(gates), N_BRANCH, axis=-1)
        merged = g_a * (o_a @ w_branch_a[l]) + g_b * (o_b @ w_branch_b[l])
        x = x + merged @ w_out[l]
        h2 = rms_norm_2(x, norm2[l])
        x = x + jnp.square(jax.nn.relu(h2 @ w_up[l])) @ w_down[l]
    return rms_norm_2(x, final_norm)


def setup_inputs(seed=0):
    out = dict(first_inputs(seed))
    for name, value in second_inputs(seed + 1).items():
        if name != "x":
            out[name + "_2"] = value
    return out


def reference(
    x, ln_attn_pre, w_in, mu_shift, w_decay_up, w_decay0, w_iclr_up, w_iclr0, w_gate_up, k_k,
    k_a, r_k, ln_x_w, ln_x_b, lambda_q1, lambda_k1, lambda_q2, lambda_k2, diff_subln, w_out,
    ln_attn_post, ln_ffn_pre, w_up, conv_w, conv_b, w_down, ln_ffn_post, norm1_2, w_in_2,
    forget_bias_2, rel_bias_2, w_branch_a_2, w_branch_b_2, w_out_2, norm2_2, w_up_2, w_down_2,
    final_norm_2,
):
    x = first_block(
        x, ln_attn_pre, w_in, mu_shift, w_decay_up, w_decay0, w_iclr_up, w_iclr0, w_gate_up,
        k_k, k_a, r_k, ln_x_w, ln_x_b, lambda_q1, lambda_k1, lambda_q2, lambda_k2, diff_subln,
        w_out, ln_attn_post, ln_ffn_pre, w_up, conv_w, conv_b, w_down, ln_ffn_post,
    )
    return second_block(
        x, norm1_2, w_in_2, forget_bias_2, rel_bias_2, w_branch_a_2, w_branch_b_2, w_out_2,
        norm2_2, w_up_2, w_down_2, final_norm_2,
    )


_drawn_inputs = setup_inputs


def setup_inputs(seed=0):
    import zlib

    import numpy as np

    out = dict(_drawn_inputs(seed))
    spreads = {}
    factors = {'k_k': 8.0,
     'ln_x_b': 5.452,
     'lambda_q1': 8.0,
     'conv_b': 3.24,
     'norm1_2': 8.0,
     'rel_bias_2': 3.632,
     'norm2_2': 4.076,
     'final_norm_2': 2.673}
    for name, (base, spread) in spreads.items():
        noise = np.random.default_rng([zlib.crc32(name.encode()), seed]).standard_normal(out[name].shape)
        drawn = base * np.exp(spread * noise) if base else spread * noise
        out[name] = __import__('jax').numpy.asarray(drawn.astype(out[name].dtype))
    for name, factor in factors.items():
        out[name] = (out[name] * factor).astype(out[name].dtype)
    return out
```

```python
import math
from contextlib import ExitStack

import numpy as np

import concourse.bass as bass
from concourse import mybir

F32 = mybir.dt.float32
F32R = mybir.dt.float32r
ALU = mybir.AluOpType
ACT = mybir.ActivationFunctionType
AX_X = mybir.AxisListType.X

P = 128
T = 1024
D = 1024
KT = D // P
TT = T // P
HALF = 512

RWKV_TILES = 4
RWKV_HEAD = 64
LORA = 64
DIFF_HEADS = 4
D_FF = 2816
FF_TILES = D_FF // P
FF2_TILES = 4096 // P
IN_TILES = 26
SHIFTED_TILES = 14
WA_TILE, G_TILE = 12, 13
FOX_HEADS = 8
FA_COL = 1536
Q2_COL = FA_COL + FOX_HEADS
DECAY_SCALE = math.exp(-0.5)
NORM_EPS = 1e-6
SUBLN_EPS = 1e-5
RWKV_LN_EPS = 64e-5
NEG = -1e30
LAM_INIT = 0.8 - 0.6
BAND = 5 * P
N_REL = 2 * P + 1
REL = BAND + P - 1

VECTORS = [
    ("ln_attn_pre", KT), ("mu_shift", SHIFTED_TILES), ("w_decay0", 4), ("w_iclr0", 4), ("k_k", 4), ("k_a", 4),
    ("r_k", 4), ("ln_x_w", 4), ("ln_x_b", 4), ("diff_subln", 1), ("ln_attn_post", KT), ("ln_ffn_pre", KT),
    ("conv_w", 3 * 2 * FF_TILES), ("conv_b", 2 * FF_TILES), ("ln_ffn_post", KT), ("norm1_2", KT),
    ("norm2_2", KT), ("final_norm_2", KT),
]
COL = {}
_at = 0
for _name, _tiles in VECTORS:
    COL[_name] = _at
    _at += _tiles
NCOLS = _at

U_IN = 0
U_OUT = U_IN + IN_TILES
U_UP = U_OUT + KT
U_FA = U_UP + 2 * FF_TILES
U_QKV2 = U_FA + 1
U_BRANCH = U_QKV2 + 40
U_OUT2 = U_BRANCH + KT
U_UP2 = U_OUT2 + KT
U_END = U_UP2 + FF2_TILES
DOWN1 = FF_TILES // 2
DOWN2 = FF2_TILES // 2


CHUNK = 64


class Steps:

    def __init__(self, sem, names):
        self.sem, self.names, self.at = sem, names, 0
        self.index = {name: k for k, name in enumerate(names)}
        assert len(self.index) == len(names)

    def start(self, eng):
        eng.sem_inc(self.sem, len(self.names))

    def done(self, instruction, name):
        assert self.names[self.at % len(self.names)] == name, (name, self.names[self.at % len(self.names)])
        self.at += 1
        instruction.then_inc(self.sem, 1)

    def wait(self, eng, name, j):
        eng.wait_ge(self.sem, j * len(self.names) + (len(self.names) + self.index[name] + 1))

    def wait_last(self, eng, names, j):
        if names:
            self.wait(eng, max(names, key=self.index.get), j)

    def wait_iterations(self, eng, j):
        eng.wait_ge(self.sem, j * len(self.names) + len(self.names))


def build_program(nc, a, out):
    ctx = ExitStack()
    with ctx:
        base = 16512
        KB = 1024

        def at(name, offset_kb, shape, dt=F32):
            return nc.alloc_sbuf_tensor_at(name, shape, dt, offset=base + int(offset_kb * KB))

        def sem(name):
            return ctx.enter_context(nc.semaphore(name))

        def dram(name, shape):
            return nc.dram_tensor(name, shape, F32, kind="Internal").ap()

        xh = at("xh", 0, [P, KT, T], F32R)
        xl = at("xl", 32, [P, KT, T], F32R)
        wh = at("wh", 64, [P, 2, KT, P], F32R)
        wl = at("wl", 72, [P, 2, KT, P], F32R)
        wraw = at("wraw", 80, [P, 2, KT, P])
        cols = at("cols", 204, [P, NCOLS])
        ident = at("ident", 205.25, [P, P])
        ones = at("ones", 205.75, [P, P])
        headones = at("headones", 206.25, [P, P])
        small = at("small", 206.75, [P, 64])
        rstd = at("rstd", 144, [P, T])

        src = at("src", 184, [P, 2, T])
        sq = at("sq", 192, [P, 2, T])
        ss = at("ss", 200, [P, T])
        y = at("y", 112, [P, KT, T])
        xin = at("xin", 112, [P, TT, D])
        shifted = at("shifted", 148, [P, T + 8])
        stage = at("stage", 153, [P, 2, T])
        diff_t = at("diff_t", 161, [P, T])
        fa = at("fa", 166, [FOX_HEADS, T])
        fa_abs = at("fa_abs", 170, [FOX_HEADS, T])
        fa_ones = at("fa_ones", 174, [FOX_HEADS, T])
        cneg = at("cneg", 178, [FOX_HEADS, T])
        hres = at("hres", 148, [P, 2, T])
        draw = at("draw", 104, [P, 2, D])
        dh = at("dh", 88, [P, 2, D], F32R)
        dl = at("dl", 96, [P, 2, D], F32R)
        fh = at("fh", 148, [P, 2, 2, T], F32R)
        fl = at("fl", 164, [P, 2, 2, T], F32R)
        ub = at("ub", 180, [P, 2, T + 8])
        cb = at("cb", 188.25, [P, 2, T])
        xh2 = at("xh2", 88, [P, KT, T], F32R)
        xl2 = at("xl2", 148, [P, KT, T], F32R)
        hres2 = at("hres2", 120, [P, 2, T])
        gates = at("gates", 128, [P, 2, 2, T])
        gated = at("gated", 184, [P, 2, T])
        merged = at("merged", 192, [P, 2, T])
        rel = at("rel", 161, [FOX_HEADS, REL])
        out_tile = at("out_tile", 148, [P, 2, D])
        token_rstd = at("token_rstd", 156, [P, TT])

        ps = ctx.enter_context(nc.psum_tensor("ps", [P, 8, HALF], F32))

        def bank2(slot):
            return ps[:, 2 * slot:2 * slot + 2, :]

        residual = dram("residual", (KT, P, T))
        proj1 = dram("proj1", (IN_TILES, P, T))
        proj2 = dram("proj2", (40, P, T))
        cneg_d = dram("cneg_d", (FOX_HEADS, T))
        rel_d = dram("rel_d", (FOX_HEADS, P, REL))

        wa = at("wa", 88, [P, T])
        gl = at("gl", 92, [P, T])
        chunk_mask = at("chunk_mask", 96, [P, T])
        lora_w = at("lora_w", 100, [P, P])
        gate_w = at("gate_w", 100.5, [P, P])
        causal2 = at("causal2", 101, [P, 2, P])
        strict_t = at("strict_t", 102, [P, P])
        ar = at("ar", 104, [P, TT, 2, P])
        bz = at("bz", 112, [P, 2, T])
        kz = at("kz", 120, [P, 2, T])
        bh_t = at("bh_t", 128, [P, TT, P])
        kh_t = at("kh_t", 132, [P, TT, P])
        v_t = at("v_t", 136, [P, TT, P])
        rkv = at("rkv", 16, [P, 3, T])
        sg = at("sg", 156, [P, T])
        iclr = at("iclr", 160, [P, T])
        css = at("css", 164, [P, T])
        dec = at("dec", 168, [P, T])
        dec_inv = at("dec_inv", 172, [P, T])
        kk = at("kk", 176, [P, T])
        kb = at("kb", 180, [P, T])
        bt = at("bt", 184, [P, T])
        bhc = at("bhc", 188, [P, T])
        ktl = at("ktl", 192, [P, T])
        khc = at("khc", 196, [P, T])
        mm_m = at("mm_m", 144, [P, 2, 2, 4, P])
        mm_n = at("mm_n", 152, [P, 2, 2, 4, P])
        mm_rb = at("mm_rb", 160, [P, 2, 4, P])
        mm_ak = at("mm_ak", 164, [P, 2, 4, P])
        mm_rk = at("mm_rk", 168, [P, 2, 4, P])
        mm_x = at("mm_x", 172, [P, 4, 2, 2, 64])
        mm_g = at("mm_g", 176, [P, 4, P])
        mm_phi = at("mm_phi", 180, [P, 8, P])
        mm_psi = at("mm_psi", 184, [P, 8, P])
        states = at("states", 188, [P, 17, P])
        yb = at("yb", 196.5, [P, TT, 2, 64])
        bonus = at("bonus", 200.75, [P, TT, 2])
        y_stats = at("y_stats", 201, [P, TT, 2, 6])
        y_mv = at("y_mv", 201.5, [P, TT, 2, 2])
        y_rs = at("y_rs", 201.75, [P, TT, 2])
        pc = at("pc", 202, [P, 16])
        y_ln = at("y_ln", 144, [P, T])
        y_mix = at("y_mix", 148, [P, T])

        qraw = at("qraw", 88, [P, 2, T])
        kraw = at("kraw", 96, [P, 2, T])
        vraw = at("vraw", 104, [P, T])
        qs = at("qs", 108, [P, 2, T], F32R)
        kh = at("kh", 116, [P, 2, T], F32R)
        kl = at("kl", 124, [P, 2, T], F32R)
        vt = at("vt", 132, [P, TT, P])
        bias = at("bias", 136, [P, 2, T])
        ssb = at("ssb", 144, [P, 2, 2, T])
        pm = at("pm", 160, [P, 2, 2, T])
        pt = [at("pt0", 176, [P, 2, T]), at("pt1", 195.5, [P, 2, T])]
        osb = at("osb", 184, [P, TT, P])
        ot = at("ot", 188, [P, T])
        tri = at("tri", 192, [P, P])
        negmax = at("negmax", 192.5, [P, TT, 2])
        rowsum = at("rowsum", 192.625, [P, TT, 2])
        weight = at("weight", 192.75, [P, TT, 2])
        osq = at("osq", 192.875, [P, TT])
        lam_row = at("lam_row", 193, [1, 4 * 64])
        lam_tmp = at("lam_tmp", 194, [1, 64])
        lam_dots = at("lam_dots", 194.5, [1, 4])

        cols_ready = sem("cols_ready")
        consts = sem("consts")
        x_loaded = [sem(f"x_loaded{t}") for t in range(2)]
        xt_done = sem("xt_done")
        xt_read = sem("xt_read")
        src_ready = sem("src_ready")
        src_stored = [sem(f"src_stored{s}") for s in range(2)]
        x_hi = sem("x_hi")
        x_sq = sem("x_sq")
        x_lo = sem("x_lo")
        ss_done = sem("ss_done")
        stat_sum = sem("stat_sum")
        stat_root = sem("stat_root")
        rstd_ready = sem("rstd_ready")
        w_loaded = [sem(f"w_loaded{s}") for s in range(2)]
        w_hi = sem("w_hi")
        w_lo = sem("w_lo")
        mm_done = sem("mm_done")
        evac_done = sem("evac_done")
        shift_done = sem("shift_done")
        stage_ready = sem("stage_ready")
        stage_stored = [sem(f"stage_stored{s}") for s in range(2)]
        phase = sem("phase")
        marks = sem("marks")

        def col(name, i, n=1):
            return cols[:, COL[name] + i:COL[name] + i + n]

        def col_at(name, i):
            return cols[:, bass.ds(COL[name] + i, 1)]

        def w_cols(w, col0, rows=D):
            return w[0:rows, bass.ds(col0, P)].rearrange("(k p) c -> p k c", p=P)

        def load_w(sp, n, s, source, first=False):
            if not first:
                sp.wait_ge(w_lo, n - 1)
            sp.dma_start(wraw[:, s, :, :], source).then_inc(w_loaded[s], 16)

        def split_hi(act, n, s, first=False):
            act.wait_ge(w_loaded[s], 8 * (n - s) + 16)
            if not first:
                act.wait_ge(mm_done, n - 1)
            nc.scalar.activation(wh[:, s, :, :], wraw[:, s, :, :], ACT.Copy).then_inc(w_hi, 1)

        def split_lo(pool, n, s, first=False):
            pool.wait_ge(w_hi, n + 1)
            nc.gpsimd.tensor_tensor(wl[:, s, :, :], wraw[:, s, :, :], wh[:, s, :, :].bitcast(F32),
                                    ALU.subtract).then_inc(w_lo, 1)

        def unit_products(pe, n, s, ready=None, first=False, x=None):
            hi, lo = x or (xh, xl)
            pe.wait_ge(w_lo, n + 1)
            if not first:
                pe.wait_ge(evac_done, n - 1)
            for kt in range(KT):
                if ready is not None:
                    pe.wait_ge(x_lo, ready + kt + 1)
                mm = three_products(2 * s, wh[:, s, kt, :], wl[:, s, kt, :], hi[:, kt, :], lo[:, kt, :],
                                    kt == 0, kt == KT - 1)
            mm.then_inc(mm_done, 1)

        def three_products(bank, w_hi_, w_lo_, x_hi_, x_lo_, start, stop):
            for w, x, k in ((w_hi_, x_hi_, 0), (w_hi_, x_lo_, 1), (w_lo_, x_hi_, 2)):
                for h in range(2):
                    mm = nc.tensor.matmul(ps[:, bank + h, :], w, x[:, h * HALF:(h + 1) * HALF],
                                          start=start and k == 0, stop=stop and k == 2)
            return mm

        def square_act(act, q, tile):
            if q >= 2:
                act.wait_ge(ss_done, q - 1)
            nc.scalar.activation(sq[:, q % 2, :], tile, ACT.Square).then_inc(x_sq, 1)

        def square_sum_dve(dve, q):
            dve.wait_ge(x_sq, q + 1)
            if q % KT == 0:
                if q:
                    dve.wait_ge(stat_sum, q // KT)
                nc.vector.tensor_copy(ss[:, :], sq[:, q % 2, :]).then_inc(ss_done, 1)
            else:
                dve.wait_ge(ss_done, q)
                nc.vector.tensor_tensor(ss[:, :], ss[:, :], sq[:, q % 2, :], ALU.add).then_inc(ss_done, 1)

        def prep_act(act, r, q, gain, ready):
            kt, s = r % KT, r % 2
            act.wait_ge(ready[0], ready[1])
            nc.scalar.activation(xh[:, kt, :], src[:, s, :], ACT.Identity, scale=col(gain, kt)).then_inc(x_hi, 1)
            square_act(act, q, src[:, s, :])

        def prep_dve(dve, r, q, gain):
            kt, s = r % KT, r % 2
            dve.wait_ge(x_hi, r + 1)
            nc.vector.scalar_tensor_tensor(out=xl[:, kt, :], in0=src[:, s, :], scalar=col(gain, kt),
                                           in1=xh[:, kt, :].bitcast(F32), op0=ALU.mult, op1=ALU.subtract)\
                .then_inc(x_lo, 1)
            square_sum_dve(dve, q)

        def apart(eng):
            eng.sem_inc(marks, 1)

        def stat_products(pe, sums):
            pe.wait_ge(ss_done, sums)
            for h in range(2):
                mm = nc.tensor.matmul(ps[:, 6 + h, :], ones[:, :], ss[:, h * HALF:(h + 1) * HALF],
                                      start=True, stop=True)
            mm.then_inc(stat_sum, 1)

        def stat_root_act(act, k):
            act.wait_ge(stat_sum, k + 1)
            nc.scalar.activation(rstd[:, :], bank2(3), ACT.Sqrt, bias=small[:, 0:1], scale=1.0 / D)\
                .then_inc(stat_root, 1)

        def stat_reciprocal(dve, k):
            dve.wait_ge(stat_root, k + 1)
            nc.vector.reciprocal(rstd[:, :], rstd[:, :]).then_inc(rstd_ready, 1)
            dve.wait_ge(rstd_ready, k + 1)

        def phase_end(eng, k):
            eng.drain().then_inc(phase, 1)
            eng.wait_ge(phase, 4 * k)

        lora_ready = sem("lora_ready")
        rkv_ready = sem("rkv_ready")
        gate_w_ready = sem("gate_w_ready")
        masks = sem("masks")
        lora_act = sem("lora_act")
        NCH = P // CHUNK
        NHALF = 4 * NCH
        LEVELS = CHUNK.bit_length() - 1
        HH = ((g, hh) for g in range(2) for hh in range(2))

        def level_names(g):
            names = []
            for l in range(LEVELS):
                for hh in range(2):
                    names.append(f"X{g}{l}{hh}")
                    if l < LEVELS - 1:
                        names.append(f"M{g}{l}{hh}")
                    if l < LEVELS - 2:
                        names.append(f"N{g}{l}{hh}")
            return names

        pe_names = ["decay", "iclr", "norm"]
        pe_names += [f"t{k}{h}" for k in ("B", "K", "V") for h in range(2)] + ["bonus"]
        for g in range(2):
            pe_names.append(f"tA{g}")
            for hh in range(2):
                pe_names += [f"SB{g}{hh}0", f"SB{g}{hh}1", f"SN{g}{hh}", f"SK{g}{hh}0", f"SK{g}{hh}1"]
            pe_names += [f"AV{g}0", f"AV{g}1"] + level_names(g)
            pe_names += [f"G{g}"] + [f"Phi{g}{q}" for q in range(NCH)] + [f"Psi{g}{q}" for q in range(NCH)]
            pe_names += [f"S{g}{c}" for c in range(NHALF)] + [f"Y{g}"]
        pe_names += ["tY0", "tY1", "gate0", "gate1"]
        act_names = ["sig_w", "sig_a", "ksq", "root", "P", "Pi", "Pp", "bz0", "bz1", "kz0", "kz1"]
        act_names += [f"t{k}{h}" for k in ("B", "K", "V") for h in range(2)] + ["bonus"]
        for g in range(2):
            act_names.append(f"tA{g}")
            act_names += [n for n in level_names(g) if n[0] == "M"]
        act_names += ["rs", "tY0", "tY1", "hi"]
        dve_names = ["css", "cp", "clamp", "recip", "kk", "A", "kb", "Bt", "Bh", "ka", "km", "Kt", "Kh", "R", "z", "pc", "zero"]
        for g in range(2):
            for hh in range(2):
                dve_names += [f"SB{g}{hh}0m", f"SB{g}{hh}0r", f"SB{g}{hh}1m", f"SB{g}{hh}1r", f"SN{g}{hh}",
                              f"SK{g}{hh}0m", f"SK{g}{hh}0r", f"SK{g}{hh}1m", f"SK{g}{hh}1r"]
            dve_names += [f"AV{g}0", f"AV{g}1"] + [n for n in level_names(g) if n[0] != "M"]
            dve_names += [f"G{g}"] + [f"Phi{g}{q}" for q in range(NCH)]
            dve_names += [f"PhiD{g}{c}" for c in range(NHALF)] + [f"Psi{g}{q}" for q in range(NCH)]
            dve_names += [f"S{g}{c}" for c in range(NHALF)] + [f"Y{g}{b}{hh}" for b in range(4) for hh in range(2)]
        dve_names += [f"bn{b}{hh}" for b in range(TT) for hh in range(2)]
        dve_names += [f"ag{b}{hh}" for b in range(TT) for hh in range(2)]
        dve_names += ["rsr"] + [f"ln{b}{hh}" for b in range(TT) for hh in range(2)] + ["gate0", "gate1", "lo"]
        rw_pe = Steps(sem("rw_pe"), pe_names)
        rw_act = Steps(sem("rw_act"), act_names)
        rw_dve = Steps(sem("rw_dve"), dve_names)

        bank_of, last_reader = {}, {}
        free_at = 0
        readers = {}
        for name in pe_names[3:]:
            bank_of[name] = free_at % 8
            free_at += 1
        def readers_of(name):
            kind = name.rstrip("0123456789")
            if kind in ("tB", "tK", "tV", "bonus", "tA", "M", "tY"):
                return [(rw_act, name)]
            if kind in ("SB", "SK"):
                return [(rw_dve, name + "r")]
            if kind == "Y":
                return [(rw_dve, name + "31")]
            return [(rw_dve, name)]

        def rw_bank(pe, name, j):
            k = pe_names.index(name)
            old = pe_names[k - 8]
            if k - 8 >= 3:
                for steps, reader in readers_of(old):
                    steps.wait(pe, reader, j)
            return bank_of[name]

        block = ctx.enter_context(nc.Block())

        def rwkv_pe(pe, j):
            def done(ins, name):
                rw_pe.done(ins, name)

            mm = nc.tensor.matmul
            rw_act.wait_iterations(pe, j)
            rw_dve.wait_iterations(pe, j)
            pe.wait_ge(rkv_ready, 80 * j + 80)
            for name, lo, bank in (("decay", 0, 0), ("iclr", 64, 2)):
                for h in range(2):
                    ins = mm(ps[:, bank + h, :], lora_w[lo:lo + 64, :], wa[lo:lo + 64, h * HALF:(h + 1) * HALF],
                             start=True, stop=True)
                done(ins, name)
            rw_act.wait(pe, "ksq", j)
            for h in range(2):
                ins = mm(ps[:, 4 + h, :], headones[:, :], kk[:, h * HALF:(h + 1) * HALF], start=True, stop=True)
            done(ins, "norm")
            rw_act.wait(pe, "root", j)

            def transposes(name, source, blocks):
                bank = rw_bank(pe, name, j)
                for i, b in enumerate(blocks):
                    ins = nc.tensor.transpose(ps[:, bank, i * P:(i + 1) * P], source(b), ident[:, :])
                done(ins, name)

            for k, source, ready in (("B", bhc, "Bh"), ("K", khc, "Kh"), ("V", None, "z")):
                rw_dve.wait(pe, ready, j)
                for h in range(2):
                    at_b = (lambda b: rkv[:, 2, b * P:(b + 1) * P]) if source is None else \
                        (lambda b, source=source: source[:, b * P:(b + 1) * P])
                    transposes(f"t{k}{h}", at_b, range(4 * h, 4 * h + 4))
            bank = rw_bank(pe, "bonus", j)
            for b in range(TT):
                ins = mm(ps[:, bank, 2 * b:2 * b + 2], rkv[:, 0, b * P:(b + 1) * P], headones[:, 0:P:64],
                         start=True, stop=True)
            done(ins, "bonus")
            rw_act.wait(pe, "kz1", j)
            for g in range(2):
                blocks = range(4 * g, 4 * g + 4)
                transposes(f"tA{g}", lambda b: ar[:, b, 0, :], blocks)
                for hh in range(2):
                    for q in range(2):
                        name = f"SB{g}{hh}{q}"
                        bank = rw_bank(pe, name, j)
                        for i in range(2):
                            b = 4 * g + 2 * q + i
                            ins = mm(ps[:, bank, i * 256:(i + 1) * 256], bz[:, hh, b * P:(b + 1) * P],
                                     ar[:, b, :, :], start=True, stop=True)
                        done(ins, name)
                    name = f"SN{g}{hh}"
                    bank = rw_bank(pe, name, j)
                    for i, b in enumerate(blocks):
                        ins = mm(ps[:, bank, i * P:(i + 1) * P], ar[:, b, 0, :], bz[:, hh, b * P:(b + 1) * P],
                                 start=True, stop=True)
                    done(ins, name)
                    for q in range(2):
                        name = f"SK{g}{hh}{q}"
                        bank = rw_bank(pe, name, j)
                        for i in range(2):
                            b = 4 * g + 2 * q + i
                            ins = mm(ps[:, bank, i * 256:(i + 1) * 256], kz[:, hh, b * P:(b + 1) * P],
                                     ar[:, b, :, :], start=True, stop=True)
                        done(ins, name)
                rw_act.wait(pe, "tV1", j)
                for hh in range(2):
                    name = f"AV{g}{hh}"
                    bank = rw_bank(pe, name, j)
                    rw_dve.wait(pe, f"SK{g}{hh}1r", j)
                    for i, b in enumerate(blocks):
                        ins = mm(ps[:, bank, i * P:(i + 1) * P], mm_ak[:, hh, i, :], v_t[:, b, :],
                                 start=True, stop=True)
                    done(ins, name)
                rw_act.wait(pe, f"tA{g}", j)
                for l in range(LEVELS):
                    m, n = mm_m[:, l % 2], mm_n[:, l % 2]
                    for hh in range(2):
                        if l == 0:
                            rw_dve.wait(pe, f"AV{g}{hh}", j)
                        else:
                            rw_act.wait(pe, f"M{g}{l - 1}{hh}", j)
                            rw_dve.wait(pe, f"X{g}{l - 1}{hh}", j)
                        name = f"X{g}{l}{hh}"
                        bank = rw_bank(pe, name, j)
                        for i in range(4):
                            ins = mm(ps[:, bank, i * P:(i + 1) * P], m[:, hh, i, :], mm_x[:, i, :, hh, :],
                                     start=True, stop=True)
                        done(ins, name)
                        if l < LEVELS - 1:
                            if l:
                                rw_dve.wait(pe, f"N{g}{l - 1}{hh}", j)
                            name = f"M{g}{l}{hh}"
                            bank = rw_bank(pe, name, j)
                            for i in range(4):
                                ins = mm(ps[:, bank, i * P:(i + 1) * P], n[:, hh, i, :], m[:, hh, i, :],
                                         start=True, stop=True)
                            done(ins, name)
                        if l < LEVELS - 2:
                            name = f"N{g}{l}{hh}"
                            bank = rw_bank(pe, name, j)
                            for i in range(4):
                                ins = mm(ps[:, bank, i * P:(i + 1) * P], m[:, hh, i, :], n[:, hh, i, :],
                                         start=True, stop=True)
                            done(ins, name)
                for hh in range(2):
                    rw_dve.wait(pe, f"X{g}{LEVELS - 1}{hh}", j)
                bank = rw_bank(pe, f"G{g}", j)
                for i in range(4):
                    for hh in range(2):
                        ins = mm(ps[64 * hh:64 * hh + 64, bank, i * P:(i + 1) * P], mm_x[:, i, 0, hh, :],
                                 mm_rb[:, hh, i, :], start=True, stop=True)
                done(ins, f"G{g}")
                for q in range(NCH):
                    bank = rw_bank(pe, f"Phi{g}{q}", j)
                    r = q * CHUNK
                    for i in range(4):
                        ins = mm(ps[:, bank, i * P:(i + 1) * P], mm_x[r:r + CHUNK, i, 0, :, :],
                                 bh_t[r:r + CHUNK, 4 * g + i, :], start=True, stop=True)
                    done(ins, f"Phi{g}{q}")
                for q in range(NCH):
                    bank = rw_bank(pe, f"Psi{g}{q}", j)
                    r = q * CHUNK
                    for i in range(4):
                        mm(ps[:, bank, i * P:(i + 1) * P], bh_t[r:r + CHUNK, 4 * g + i, :],
                           mm_x[r:r + CHUNK, i, 1, :, :], start=True, stop=False)
                        ins = mm(ps[:, bank, i * P:(i + 1) * P], kh_t[r:r + CHUNK, 4 * g + i, :],
                                 v_t[r:r + CHUNK, 4 * g + i, :], start=False, stop=True)
                    done(ins, f"Psi{g}{q}")
                rw_dve.wait(pe, f"Psi{g}{NCH - 1}", j)
                for c in range(NHALF):
                    name = f"S{g}{c}"
                    if c:
                        rw_dve.wait(pe, f"S{g}{c - 1}", j)
                    bank = rw_bank(pe, name, j)
                    ins = mm(ps[:, bank, 0:P], mm_phi[:, c, :], states[:, NHALF * g + c, :], start=True, stop=True)
                    done(ins, name)
                rw_dve.wait(pe, f"S{g}{NHALF - 1}", j)
                bank = rw_bank(pe, f"Y{g}", j)
                for i in range(4):
                    b = 4 * g + i
                    for r in range(NCH):
                        mm(ps[r * CHUNK:(r + 1) * CHUNK, bank, i * P:(i + 1) * P],
                           mm_g[:, i, r * CHUNK:(r + 1) * CHUNK], states[:, NCH * b + r, :],
                           start=(i == 0), stop=False, skip_group_check=True)
                    for hh in range(2):
                        to = ps[:, bank, i * P + 64 * hh:i * P + 64 * hh + 64]
                        mm(to, mm_rb[:, hh, i, :], mm_x[:, i, 1, hh, :], start=False, stop=False,
                           skip_group_check=True)
                        ins = mm(to, mm_rk[:, hh, i, :], v_t[:, b, 64 * hh:64 * hh + 64], start=False,
                                 stop=(i == 3), skip_group_check=True)
                done(ins, f"Y{g}")
            rw_dve.wait(pe, f"ln{TT - 1}1", j)
            for h in range(2):
                transposes(f"tY{h}", lambda b: yb[:, b, :, :], range(4 * h, 4 * h + 4))
            pe.wait_ge(gate_w_ready, 16 * j + 16)
            for h in range(2):
                bank = rw_bank(pe, f"gate{h}", j)
                ins = mm(ps[:, bank, :], gate_w[:, :], gl[:, h * HALF:(h + 1) * HALF], start=True, stop=True)
                done(ins, f"gate{h}")

        def rwkv_act(act, j):
            def done(ins, name):
                rw_act.done(ins, name)

            def vec(name):
                return col_at(name, j)

            fn = nc.scalar.activation
            rw_dve.wait_iterations(act, j)
            rw_pe.wait(act, "decay", j)
            apart(act)
            done(fn(sg[:, :], bank2(0), ACT.Sigmoid, bias=vec("w_decay0")), "sig_w")
            rw_pe.wait(act, "iclr", j)
            apart(act)
            done(fn(iclr[:, :], bank2(1), ACT.Sigmoid, bias=vec("w_iclr0")), "sig_a")
            done(fn(kk[:, :], rkv[:, 1, :], ACT.Square, scale=vec("k_k")), "ksq")
            rw_pe.wait(act, "norm", j)
            done(fn(kb[:, :], bank2(2), ACT.Sqrt), "root")
            rw_dve.wait(act, "css", j)
            done(fn(dec[:, :], css[:, :], ACT.Exp, scale=-DECAY_SCALE), "P")
            done(fn(dec_inv[:, :], css[:, :], ACT.Exp, scale=DECAY_SCALE), "Pi")
            rw_dve.wait(act, "cp", j)
            done(fn(sg[:, :], sg[:, :], ACT.Exp, scale=-DECAY_SCALE), "Pp")
            rw_dve.wait(act, "Bt", j)
            for h in range(2):
                rows = slice(64 * h, 64 * h + 64)
                done(fn(bz[rows, h, :], bt[rows, :], ACT.Copy), f"bz{h}")
            rw_dve.wait(act, "Kt", j)
            for h in range(2):
                rows = slice(64 * h, 64 * h + 64)
                done(fn(kz[rows, h, :], ktl[rows, :], ACT.Copy), f"kz{h}")
            for k, to in (("B", bh_t), ("K", kh_t), ("V", v_t)):
                for h in range(2):
                    name = f"t{k}{h}"
                    rw_pe.wait(act, name, j)
                    done(fn(to[:, 4 * h:4 * h + 4, :], ps[:, bank_of[name], :], ACT.Copy), name)
            rw_pe.wait(act, "bonus", j)
            done(fn(bonus[:, :, :], ps[:, bank_of["bonus"], 0:2 * TT], ACT.Copy), "bonus")
            rw_dve.wait(act, "pc", j)
            for g in range(2):
                if g:
                    rw_pe.wait(act, f"Y{g - 1}", j)
                rw_pe.wait(act, f"tA{g}", j)
                bank = ps[:, bank_of[f"tA{g}"], :].rearrange("p (b c) -> p b c", b=4)
                done(fn(mm_x[:, :, 0, :, :].rearrange("p b h c -> p b (h c)"), bank, ACT.Copy), f"tA{g}")
                for l in range(LEVELS - 1):
                    for hh in range(2):
                        name = f"M{g}{l}{hh}"
                        rw_pe.wait(act, name, j)
                        done(fn(mm_m[:, (l + 1) % 2, hh, :, :], ps[:, bank_of[name], :], ACT.Copy), name)
            rw_dve.wait(act, f"ag{TT - 1}1", j)
            done(fn(y_rs[:, :, :], y_mv[:, :, :, 1], ACT.Sqrt, bias=small[:, 1:2]), "rs")
            for h in range(2):
                rw_pe.wait(act, f"tY{h}", j)
                apart(act)
                done(fn(y_ln[:, h * HALF:(h + 1) * HALF], ps[:, bank_of[f"tY{h}"], :], ACT.Identity,
                        bias=vec("ln_x_b"), scale=vec("ln_x_w")), f"tY{h}")
            rw_dve.wait(act, "gate1", j)
            apart(act)
            done(fn(xh[:, bass.ds(j, 1), :].rearrange("p a n -> p (a n)"), y_mix[:, :], ACT.Copy), "hi")

        def rwkv_dve(dve, j):
            last = [None]

            def done(ins, name):
                rw_dve.done(ins, name)
                last[0] = name

            def after(name=None):
                rw_dve.wait(dve, name or last[0], j)

            def vec(name):
                return col_at(name, j)

            tt, stt = nc.vector.tensor_tensor, nc.vector.scalar_tensor_tensor
            r, k, v = rkv[:, 0, :], rkv[:, 1, :], rkv[:, 2, :]
            rw_dve.wait_iterations(dve, j)
            rw_act.wait(dve, "sig_w", j)
            done(nc.vector.tensor_tensor_scan(css[:, :], chunk_mask[:, :], sg[:, :], 0.0, ALU.mult, ALU.add), "css")
            after()
            done(tt(sg[:, :], css[:, :], sg[:, :], ALU.subtract), "cp")
            rw_act.wait(dve, "root", j)
            done(nc.vector.tensor_scalar(kb[:, :], kb[:, :], 1e-12, None, ALU.max), "clamp")
            after()
            done(nc.vector.reciprocal(kb[:, :], kb[:, :]), "recip")
            after()
            rw_pe.wait(dve, "norm", j)
            done(stt(out=kk[:, :], in0=k, scalar=vec("k_k"), in1=kb[:, :], op0=ALU.mult, op1=ALU.mult), "kk")
            after()
            rw_act.wait(dve, "Pp", j)
            done(stt(out=ar[:, :, 0, :], in0=kk[:, :].rearrange("p (b t) -> p b t", b=TT), scalar=-1.0,
                     in1=sg[:, :].rearrange("p (b t) -> p b t", b=TT), op0=ALU.mult, op1=ALU.mult), "A")
            done(tt(kb[:, :], kk[:, :], iclr[:, :], ALU.mult), "kb")
            after()
            done(tt(bt[:, :], kb[:, :], dec_inv[:, :], ALU.mult), "Bt")
            after()
            ends = dec[:, CHUNK - 1:T:CHUNK].unsqueeze(2).broadcast_to([P, T // CHUNK, CHUNK])

            def chunks(x):
                return x[:, :].rearrange("p (c t) -> p c t", t=CHUNK)

            done(tt(chunks(bhc), chunks(bt), ends, ALU.mult), "Bh")
            done(nc.vector.tensor_scalar(iclr[:, :], iclr[:, :], 1.0, vec("k_a"), ALU.subtract, ALU.mult), "ka")
            after()
            done(stt(out=k, in0=iclr[:, :], scalar=1.0, in1=k, op0=ALU.add, op1=ALU.mult), "km")
            after()
            done(tt(ktl[:, :], k, dec_inv[:, :], ALU.mult), "Kt")
            after()
            done(tt(chunks(khc), chunks(ktl), ends, ALU.mult), "Kh")
            done(tt(ar[:, :, 1, :], rkv[:, 0, :].rearrange("p (b t) -> p b t", b=TT),
                    dec[:, :].rearrange("p (b t) -> p b t", b=TT), ALU.mult), "R")
            after()
            done(stt(out=r, in0=r, scalar=vec("r_k"), in1=k, op0=ALU.mult, op1=ALU.mult), "z")
            done(nc.vector.tensor_copy(pc[:, 0:T // CHUNK], dec[:, CHUNK - 1:T:CHUNK]), "pc")
            after()
            rw_act.wait(dve, "bonus", j)
            done(nc.vector.memset(states[:, 0, :], 0.0), "zero")
            for g in range(2):
                if g:
                    rw_pe.wait(dve, f"Y{g - 1}", j)
                for hh in range(2):
                    for kind, strict_to, full_to in (("SB", mm_m[:, 0], mm_rb), ("SN", None, None),
                                                     ("SK", mm_ak, mm_rk)):
                        if kind == "SN":
                            name = f"SN{g}{hh}"
                            rw_pe.wait(dve, name, j)
                            bank = ps[:, bank_of[name], :].rearrange("p (b c) -> p b c", b=4)
                            done(tt(mm_n[:, 0, hh, :, :], bank,
                                    strict_t[:, :].unsqueeze(1).broadcast_to([P, 4, P]), ALU.mult), name)
                            continue
                        for q in range(2):
                            name = f"{kind}{g}{hh}{q}"
                            rw_pe.wait(dve, name, j)
                            bank = ps[:, bank_of[name], :].rearrange("p (b k c) -> p b k c", b=2, k=2)
                            for which, to, suffix in ((0, strict_to, "m"), (1, full_to, "r")):
                                done(tt(to[:, hh, 2 * q:2 * q + 2, :], bank[:, :, which, :],
                                        causal2[:, which, :].unsqueeze(1).broadcast_to([P, 2, P]), ALU.mult),
                                     name + suffix)
                for hh in range(2):
                    name = f"AV{g}{hh}"
                    rw_pe.wait(dve, name, j)
                    bank = ps[:, bank_of[name], :].rearrange("p (b k c) -> p b k c", b=4, k=2)
                    done(nc.vector.tensor_copy(mm_x[:, :, 1, hh, :], bank[:, :, hh, :]), name)
                rw_act.wait(dve, f"tA{g}", j)
                for l in range(LEVELS):
                    for hh in range(2):
                        name = f"X{g}{l}{hh}"
                        rw_pe.wait(dve, name, j)
                        after(f"AV{g}{hh}" if l == 0 else f"X{g}{l - 1}{hh}")
                        x = mm_x[:, :, :, hh, :]
                        bank = ps[:, bank_of[name], :].rearrange("p (b k c) -> p b k c", b=4, k=2)
                        done(tt(x, bank, x, ALU.add), name)
                        if l < LEVELS - 2:
                            name = f"N{g}{l}{hh}"
                            rw_pe.wait(dve, name, j)
                            done(nc.vector.tensor_copy(mm_n[:, (l + 1) % 2, hh, :, :], ps[:, bank_of[name], :]), name)
                rw_pe.wait(dve, f"G{g}", j)
                done(tt(mm_g[:, :, :], ps[:, bank_of[f"G{g}"], :].rearrange("p (b c) -> p b c", b=4),
                        ar[:, 4 * g:4 * g + 4, 1, :], ALU.add), f"G{g}")
                blocked = headones[:, :].unsqueeze(1).broadcast_to([P, 4, P])
                for q in range(NCH):
                    name = f"Phi{g}{q}"
                    rw_pe.wait(dve, name, j)
                    done(tt(mm_phi[:, q:NHALF:NCH, :], ps[:, bank_of[name], :].rearrange("p (b c) -> p b c", b=4),
                            blocked, ALU.mult), name)
                after()
                for c in range(NHALF):
                    done(stt(out=mm_phi[:, c, :], in0=ident[:, :], scalar=pc[:, NHALF * g + c:NHALF * g + c + 1],
                             in1=mm_phi[:, c, :], op0=ALU.mult, op1=ALU.add), f"PhiD{g}{c}")
                for q in range(NCH):
                    name = f"Psi{g}{q}"
                    rw_pe.wait(dve, name, j)
                    done(tt(mm_psi[:, q:NHALF:NCH, :], ps[:, bank_of[name], :].rearrange("p (b c) -> p b c", b=4),
                            blocked, ALU.mult), name)
                after()
                for c in range(NHALF):
                    name = f"S{g}{c}"
                    rw_pe.wait(dve, name, j)
                    done(tt(states[:, NHALF * g + c + 1, :], ps[:, bank_of[name], 0:P], mm_psi[:, c, :], ALU.add),
                         name)
                rw_pe.wait(dve, f"Y{g}", j)
                for i in range(4):
                    for hh in range(2):
                        b = 4 * g + i
                        done(stt(out=yb[:, b, hh, :], in0=v_t[:, b, 64 * hh:64 * hh + 64],
                                 scalar=bonus[:, b, hh:hh + 1],
                                 in1=ps[:, bank_of[f"Y{g}"], i * P + 64 * hh:i * P + 64 * hh + 64],
                                 op0=ALU.mult, op1=ALU.add), f"Y{g}{i}{hh}")
            after()
            each = [(b, hh) for b in range(TT) for hh in range(2)]
            for b, hh in each:
                done(nc.vector.bn_stats(y_stats[:, b, hh, :], yb[:, b, hh, :]), f"bn{b}{hh}")
            after()
            apart(dve)
            for b, hh in each:
                done(nc.vector.bn_aggr(y_mv[:, b, hh, :], y_stats[:, b, hh, :]), f"ag{b}{hh}")
            rw_act.wait(dve, "rs", j)
            done(nc.vector.reciprocal(y_rs[:, :, :], y_rs[:, :, :]), "rsr")
            after()
            for b, hh in each:
                done(nc.vector.tensor_scalar(yb[:, b, hh, :], yb[:, b, hh, :], y_mv[:, b, hh, 0:1],
                                             y_rs[:, b, hh:hh + 1], ALU.subtract, ALU.mult), f"ln{b}{hh}")
            for h in range(2):
                rw_act.wait(dve, f"tY{h}", j)
                rw_pe.wait(dve, f"gate{h}", j)
                part = slice(h * HALF, (h + 1) * HALF)
                done(tt(y_mix[:, part], ps[:, bank_of[f"gate{h}"], :], y_ln[:, part], ALU.mult), f"gate{h}")
            rw_act.wait(dve, "hi", j)
            done(tt(xl[:, bass.ds(j, 1), :].rearrange("p a n -> p (a n)"), y_mix[:, :],
                    xh[:, bass.ds(j, 1), :].bitcast(F32).rearrange("p a n -> p (a n)"), ALU.subtract), "lo")

        lam_loaded = sem("lam_loaded")
        lam_dve = sem("lam_dve")
        lam_act = sem("lam_act")
        lam_pe = sem("lam_pe")
        class Attention:
            def __init__(self, kind):
                self.kind = kind
                self.diff = kind == "diff"
                self.order = list(range(TT))[::-1] if kind == "fox" else list(range(TT))
                self.maps = 1 if self.diff else 2
                order = self.order
                pe, act, dve = ["tv0", "tv1"], ["vt0", "vt1"], []

                def scores(n):
                    if n < TT:
                        pe.extend(f"s{order[n]}{m}" for m in range(2))

                def maxima(n):
                    if n < TT:
                        for m in range(2):
                            if kind == "fox":
                                dve.append(f"dm{order[n]}{m}")
                            dve.append(f"mx{order[n]}{m}")

                def exps(n):
                    if n < TT:
                        act.extend(f"ex{order[n]}{m}" for m in range(2))

                def outputs(n):
                    if n >= 0:
                        if not self.diff:
                            dve.append(f"rl{order[n]}")
                        dve.extend(f"o{order[n]}{m}" for m in range(self.maps))

                scores(0)
                scores(1)
                maxima(0)
                maxima(1)
                exps(0)
                exps(1)
                for n, i in enumerate(order):
                    scores(n + 2)
                    if self.diff:
                        dve += [f"rl{i}", f"w{i}", f"pa{i}", f"pb{i}"]
                    maxima(n + 2)
                    for m in range(self.maps):
                        for g in self.groups(i):
                            pe.append(f"t{i}{m}{g}")
                            (act if self.copier(m, g) == "act" else dve).append(f"pt{i}{m}{g}")
                    exps(n + 2)
                    pe += [f"o{i}{m}" for m in range(self.maps)]
                    outputs(n - 1)
                    if self.diff and n:
                        act.append(f"sq{order[n - 1]}")
                outputs(TT - 1)
                if self.diff:
                    act += [f"sq{order[-1]}", "root"]
                    dve += ["rr"] + [f"on{i}" for i in range(TT)]
                pe += ["to0", "to1"]
                act += ["ot0", "ot1", "hi"]
                self.pe = Steps(sem(f"{kind}_pe"), pe)
                self.act = Steps(sem(f"{kind}_act"), act)
                self.dve = Steps(sem(f"{kind}_dve"), dve)
                self.pool = Steps(sem(f"{kind}_pool"), ["lo"])
                self.split_act = Steps(sem(f"{kind}_split_act"), ["qh0", "kh0", "qh1", "kh1"])
                self.split_dve = Steps(sem(f"{kind}_split_dve"), {"diff": ["slope"], "fox": [], "band": [
                    "edge0", "edge1", "edge2", "edge3"]}[kind] + ["ql0", "kl0", "ql1", "kl1"])
                self.loaded = sem(f"{kind}_loaded")
                self.bias_loaded = sem(f"{kind}_bias_loaded")
                self.turn, self.before = {}, {}
                uses = []
                for i in order:
                    for m in range(self.maps):
                        for g in self.groups(i):
                            self.turn[i, m, g] = len(uses) % 2
                            self.before[i, m, g] = uses[-2:-1] if len(uses) >= 2 else []
                            uses.append((i, m, g))
                self.last_uses = uses[-2:]

            def blocks(self, i):
                return range(max(0, i - 4) if self.kind == "band" else 0, i + 1)

            def groups(self, i):
                return range((len(self.blocks(i)) + 3) // 4)

            def copier(self, m, g):
                return "act" if (g if self.diff else m) == 0 else "dve"

            def copied(self, eng, uses, j, act=(), dve=()):
                self.act.wait_last(eng, [*act, *(f"pt{i}{m}{g}" for i, m, g in uses if self.copier(m, g) == "act")], j)
                self.dve.wait_last(eng, [*dve, *(f"pt{i}{m}{g}" for i, m, g in uses if self.copier(m, g) == "dve")], j)

            def bias_of(self, i, m):
                n = P * len(self.blocks(i))
                if self.diff:
                    return bias[:, 0, T - n:T]
                if self.kind == "fox":
                    return bias[:, m, 0:n]
                first = (4 - i) * P if i < 4 else 0
                return bias[:, m, first:first + n]

            def multiplied(self, eng, n, m, j):
                if n >= 2:
                    self.pe.wait(eng, f"o{self.order[n - 2]}{m}", j)
                else:
                    self.pe.wait(eng, f"o{self.order[TT - 2 + n]}{m}", j - 1)

        def attention_pe(pe, at_, j):
            mm = nc.tensor.matmul
            order, last = at_.order, at_.order[-1]
            pe.wait_ge(at_.loaded, 9 * 16 * (j + 1))
            at_.act.wait(pe, "ot1", j - 1)
            for h in range(2):
                for b in range(4):
                    ins = nc.tensor.transpose(ps[:, 4 + h, b * P:(b + 1) * P],
                                              vraw[:, (4 * h + b) * P:(4 * h + b + 1) * P], ident[:, :])
                at_.pe.done(ins, f"tv{h}")
            at_.split_dve.wait(pe, "kl1", j)

            def scores(n):
                if n >= TT:
                    return
                i = order[n]
                keys = at_.blocks(i)
                size = P * len(keys)
                for m in range(2):
                    if n:
                        at_.dve.wait(pe, f"mx{order[n - 1]}{m}", j)
                    else:
                        at_.dve.wait(pe, f"mx{last}{m}", j - 1)
                    for lo in range(0, size, HALF):
                        hi = min(size, lo + HALF)
                        k0 = keys[0] * P
                        for part, k in enumerate((kh, kl)):
                            ins = mm(ps[:, 2 * m + lo // HALF, 0:hi - lo], qs[:, m, i * P:(i + 1) * P],
                                     k[:, m, k0 + lo:k0 + hi], start=(part == 0), stop=(part == 1))
                    at_.pe.done(ins, f"s{i}{m}")

            scores(0)
            scores(1)
            for n, i in enumerate(order):
                scores(n + 2)
                for m in range(at_.maps):
                    for g in at_.groups(i):
                        at_.copied(pe, at_.before[i, m, g], j, act=["vt1"] + ([] if at_.diff else [f"ex{i}{m}"]),
                                   dve=[f"pb{i}"] if at_.diff else [])
                        bank = 4 + at_.turn[i, m, g]
                        for k in range(4 * g, min(4 * g + 4, len(at_.blocks(i)))):
                            ins = nc.tensor.transpose(ps[:, bank, (k - 4 * g) * P:(k - 4 * g + 1) * P],
                                                      pm[:, n % 2, m, k * P:(k + 1) * P], ident[:, :])
                        at_.pe.done(ins, f"t{i}{m}{g}")
                if n < 2:
                    at_.dve.wait(pe, f"o{order[TT - 2 + n]}{at_.maps - 1}", j - 1)
                for m in range(at_.maps):
                    keys = at_.blocks(i)
                    at_.copied(pe, [(i, m, g) for g in at_.groups(i)], j,
                               dve=[f"o{order[n - 2]}{at_.maps - 1}"] if n >= 2 else [])
                    for k, b in enumerate(keys):
                        ins = mm(ps[:, 6 + n % 2, m * P:(m + 1) * P], pt[n % 2][:, m, k * P:(k + 1) * P],
                                 vt[:, b, :], start=(k == 0), stop=(k == len(keys) - 1))
                    at_.pe.done(ins, f"o{i}{m}")
            at_.copied(pe, at_.last_uses, j, dve=[f"on{TT - 1}" if at_.diff else f"o{last}1"])
            for h in range(2):
                for b in range(4):
                    ins = nc.tensor.transpose(ps[:, 4 + h, b * P:(b + 1) * P], osb[:, 4 * h + b, :], ident[:, :])
                at_.pe.done(ins, f"to{h}")

        def attention_split_act(act, at_, j):
            fn = nc.scalar.activation
            act.wait_ge(at_.loaded, 9 * 16 * (j + 1))
            at_.pe.wait(act, f"s{at_.order[-1]}1", j - 1)
            for m in range(2):
                at_.split_act.done(fn(qs[:, m, :], qraw[:, m, :], ACT.Copy, scale=0.125), f"qh{m}")
                at_.split_act.done(fn(kh[:, m, :], kraw[:, m, :], ACT.Copy), f"kh{m}")

        def attention_split_dve(dve, at_, j):
            def done(ins, name):
                at_.split_dve.done(ins, name)

            at_.dve.wait(dve, f"mx{at_.order[-1]}1", j - 1)
            if at_.diff:
                done(nc.vector.tensor_scalar(bias[:, 0, :], bias[:, 0, :], 0.25, None, ALU.mult), "slope")
            if at_.kind == "band":
                dve.wait_ge(at_.bias_loaded, 2 * 16 * (j + 1))
                for m in range(2):
                    done(nc.vector.memset(bias[0:64, m, 576:640], NEG), f"edge{2 * m}")
                    done(nc.vector.memset(bias[64:128, m, 0:64], NEG), f"edge{2 * m + 1}")
            for m in range(2):
                at_.split_act.wait(dve, f"qh{m}", j)
                done(nc.vector.scalar_tensor_tensor(out=qs[64:128, m, :], in0=qraw[64:128, m, :], scalar=0.125,
                                                    in1=qs[64:128, m, :].bitcast(F32), op0=ALU.mult,
                                                    op1=ALU.subtract), f"ql{m}")
                at_.split_act.wait(dve, f"kh{m}", j)
                done(nc.vector.tensor_tensor(kl[:, m, :], kraw[:, m, :], kh[:, m, :].bitcast(F32), ALU.subtract),
                     f"kl{m}")

        def attention_act(act, at_, j, to, final=False):
            fn = nc.scalar.activation
            order = at_.order
            for h in range(2):
                at_.pe.wait(act, f"tv{h}", j)
                at_.act.done(fn(vt[:, 4 * h:4 * h + 4, :], ps[:, 4 + h, :], ACT.Copy), f"vt{h}")

            def exps(n):
                if n >= TT:
                    return
                i = order[n]
                size = P * len(at_.blocks(i))
                for m in range(2):
                    at_.dve.wait(act, f"mx{i}{m}", j)
                    if n >= 2:
                        old = order[n - 2]
                        at_.pe.wait(act, f"t{old}{at_.maps - 1}{len(at_.groups(old)) - 1}", j)
                    at_.act.done(fn(pm[:, n % 2, m, 0:size], ssb[:, n % 2, m, 0:size], ACT.Exp, scale=-1.0,
                                    bias=negmax[:, i, m:m + 1], accum_out=rowsum[:, i, m:m + 1]), f"ex{i}{m}")

            def square(i):
                at_.dve.wait(act, f"o{i}0", j)
                at_.act.done(fn(ot[:, i * P:(i + 1) * P], osb[:, i, :], ACT.Square, accum_out=osq[:, i:i + 1]),
                             f"sq{i}")

            exps(0)
            exps(1)
            for n, i in enumerate(order):
                for m in range(at_.maps):
                    for g in at_.groups(i):
                        if at_.copier(m, g) == "act":
                            size = P * min(4, len(at_.blocks(i)) - 4 * g)
                            at_.pe.wait(act, f"t{i}{m}{g}", j)
                            at_.act.done(fn(pt[n % 2][:, m, g * HALF:g * HALF + size],
                                            ps[:, 4 + at_.turn[i, m, g], 0:size], ACT.Copy), f"pt{i}{m}{g}")
                exps(n + 2)
                if n == 1:
                    at_.pool.wait_iterations(act, j)
                if at_.diff and n:
                    square(order[n - 1])
                if n == TT - 2 and not final:
                    attention_split_act(act, at_, j + 1)
            if at_.diff:
                square(order[-1])
                at_.act.wait(act, f"sq{TT - 1}", j)
                at_.act.done(fn(osq[:, :], osq[:, :], ACT.Sqrt, bias=small[:, 3:4], scale=1.0 / P), "root")
            for h in range(2):
                at_.pe.wait(act, f"to{h}", j)
                part = slice(h * HALF, (h + 1) * HALF)
                if at_.diff:
                    at_.act.done(fn(ot[:, part], ps[:, 4 + h, :], ACT.Copy, scale=small[:, 4:5]), f"ot{h}")
                else:
                    at_.act.done(fn(ot[:, part], ps[:, 4 + h, :], ACT.Copy), f"ot{h}")
            at_.act.wait(act, "ot1", j)
            apart(act)
            at_.act.done(fn(xh[:, bass.ds(to + j, 1), :].rearrange("p a n -> p (a n)"), ot[:, :], ACT.Copy), "hi")

        def attention_dve(dve, at_, j, final=False):
            tt, stt = nc.vector.tensor_tensor, nc.vector.scalar_tensor_tensor
            order = at_.order

            def done(ins, name):
                at_.dve.done(ins, name)

            at_.dve.wait_iterations(dve, j)
            at_.split_dve.wait(dve, "kl1", j)
            if at_.kind == "fox":
                dve.wait_ge(at_.bias_loaded, 2 * 16 * (j + 1))
            at_.act.wait(dve, f"ex{order[-1]}1", j - 1)

            def maxima(n):
                if n >= TT:
                    return
                i = order[n]
                size = P * len(at_.blocks(i))
                for m in range(2):
                    if at_.kind == "fox":
                        part = bias[:, m, i * P:(i + 1) * P]
                        done(tt(part, part, tri[:, :], ALU.add), f"dm{i}{m}")
                        at_.dve.wait(dve, f"dm{i}{m}", j)
                    at_.pe.wait(dve, f"s{i}{m}", j)
                    if n >= 2:
                        at_.act.wait(dve, f"ex{order[n - 2]}{m}", j)
                    apart(dve)
                    done(nc.vector.tensor_tensor_reduce(
                        ssb[:, n % 2, m, 0:size], ps[:, 2 * m:2 * m + 2, :].rearrange("p a n -> p (a n)")[:, 0:size],
                        at_.bias_of(i, m), -1.0, 3e38, ALU.add, ALU.min, negmax[:, i, m:m + 1]), f"mx{i}{m}")

            def outputs(n):
                if n < 0:
                    return
                i = order[n]
                if not at_.diff:
                    at_.act.wait(dve, f"ex{i}1", j)
                    done(nc.vector.reciprocal(rowsum[:, i, :], rowsum[:, i, :]), f"rl{i}")
                    at_.dve.wait(dve, f"rl{i}", j)
                if n == 0:
                    at_.pe.wait(dve, "to1", j - 1)
                at_.pe.wait(dve, f"o{i}{at_.maps - 1}", j)
                for m in range(at_.maps):
                    if at_.diff:
                        done(nc.vector.tensor_copy(osb[:, i, :], ps[:, 6 + n % 2, 0:P]), f"o{i}0")
                    else:
                        done(nc.vector.tensor_scalar(osb[:, i, 64 * m:64 * m + 64],
                                                     ps[:, 6 + n % 2, (P + 64) * m:(P + 64) * m + 64],
                                                     rowsum[:, i, m:m + 1],
                                                     None, ALU.mult), f"o{i}{m}")

            maxima(0)
            maxima(1)
            for n, i in enumerate(order):
                size = P * len(at_.blocks(i))
                if at_.diff:
                    at_.act.wait(dve, f"ex{i}1", j)
                    done(nc.vector.reciprocal(rowsum[:, i, :], rowsum[:, i, :]), f"rl{i}")
                    at_.dve.wait(dve, f"rl{i}", j)
                    done(tt(weight[:, i, 0:1], rowsum[:, i, 1:2], small[:, 2:3], ALU.mult), f"w{i}")
                    done(nc.vector.tensor_scalar(pm[:, n % 2, 0, 0:size], pm[:, n % 2, 0, 0:size],
                                                 rowsum[:, i, 0:1], None, ALU.mult), f"pa{i}")
                    at_.dve.wait(dve, f"pa{i}", j)
                    done(stt(out=pm[:, n % 2, 0, 0:size], in0=pm[:, n % 2, 1, 0:size], scalar=weight[:, i, 0:1],
                             in1=pm[:, n % 2, 0, 0:size], op0=ALU.mult, op1=ALU.add), f"pb{i}")
                maxima(n + 2)
                for m in range(at_.maps):
                    for g in at_.groups(i):
                        if at_.copier(m, g) == "dve":
                            part = P * min(4, len(at_.blocks(i)) - 4 * g)
                            at_.pe.wait(dve, f"t{i}{m}{g}", j)
                            done(nc.vector.tensor_copy(pt[n % 2][:, m, g * HALF:g * HALF + part],
                                                       ps[:, 4 + at_.turn[i, m, g], 0:part]), f"pt{i}{m}{g}")
                outputs(n - 1)
                if n == TT - 2 and not final:
                    attention_split_dve(dve, at_, j + 1)
            outputs(TT - 1)
            if at_.diff:
                at_.act.wait(dve, "root", j)
                done(nc.vector.reciprocal(osq[:, :], osq[:, :]), "rr")
                at_.dve.wait(dve, "rr", j)
                for i in range(TT):
                    done(nc.vector.tensor_scalar(osb[:, i, :], osb[:, i, :], osq[:, i:i + 1], None, ALU.mult),
                         f"on{i}")

        def attention_pool(pool, at_, to):
            with pool.Fori(0, 4) as j:
                at_.act.wait(pool, "hi", j)
                at_.pool.done(nc.gpsimd.tensor_tensor(
                    xl[:, bass.ds(to + j, 1), :].rearrange("p a n -> p (a n)"), ot[:, :],
                    xh[:, bass.ds(to + j, 1), :].bitcast(F32).rearrange("p a n -> p (a n)"), ALU.subtract), "lo")

        def attention_loads(sp, at_, source, tiles, bias_loads=None):
            with sp.Fori(0, 4) as j:
                at_.split_act.wait(sp, "kh1", j - 1)
                apart(sp)
                at_.split_dve.wait(sp, "kl1", j - 1)
                apart(sp)
                at_.pe.wait(sp, "tv1", j - 1)
                apart(sp)
                for to, tile0 in ((qraw, tiles[0]), (kraw, tiles[1])):
                    for m in range(2):
                        from_ = source[bass.ds(tile0 + j, 1), 64 * m:64 * m + 64, :].rearrange("a p n -> (a p) n")
                        for half in range(2):
                            sp.dma_start(to[64 * half:64 * half + 64, m, :], from_).then_inc(at_.loaded, 16)
                sp.dma_start(vraw[:, :], source[bass.ds(tiles[2] + j, 1)].rearrange("a p n -> (a p) n"))\
                    .then_inc(at_.loaded, 16)
                if bias_loads is not None:
                    at_.dve.wait(sp, f"mx{at_.order[-1]}1", j - 1)
                    apart(sp)
                    for m in range(2):
                        bias_loads(j, m).then_inc(at_.bias_loaded, 16)

        def attention_loop(eng, body, split, at_, *args):
            if split:
                split(eng, at_, 0)
            with eng.Fori(0, 3) as j:
                body(eng, at_, j, *args)
            body(eng, at_, 3, *args, final=True)

        diff, fox, band = Attention("diff"), Attention("fox"), Attention("band")
        h_loaded = [sem(f"h_loaded{s}") for s in range(2)]
        scaled = sem("scaled")
        added = sem("added")
        d_loaded = sem("d_loaded")
        d_hi = sem("d_hi")
        d_lo = sem("d_lo")
        down_done = sem("down_done")
        down_added = sem("down_added")
        y_zero = sem("y_zero")
        fa_act = sem("fa_act")
        fa_dve = sem("fa_dve")
        fa_loaded = sem("fa_loaded")
        fa_set = sem("fa_set")
        ub_pads = sem("ub_pads")
        fa_stored = sem("fa_stored")
        rel_loaded = sem("rel_loaded")
        rel_filled = sem("rel_filled")
        rel_stored = sem("rel_stored")
        gate_loaded = [sem(f"gate_loaded{s}") for s in range(2)]
        gate_done = sem("gate_done")
        gated_a = sem("gated_a")
        gated_b = sem("gated_b")
        merged_done = sem("merged_done")
        m_hi = sem("m_hi")
        m_lo = sem("m_lo")
        h2_loaded = [sem(f"h2_loaded{s}") for s in range(2)]
        y_loaded = sem("y_loaded")
        squared = sem("squared")
        out_sum = sem("out_sum")
        out_root = sem("out_root")
        gained = sem("gained")
        out_turned = sem("out_turned")
        out_ready = sem("out_ready")
        out_stored = [sem(f"out_stored{s}") for s in range(2)]

        def post_scale(dve, k, kt, gain):
            nc.vector.scalar_tensor_tensor(out=y[:, kt, :], in0=y[:, kt, :], scalar=col(gain, kt), in1=rstd[:, :],
                                           op0=ALU.mult, op1=ALU.mult).then_inc(scaled, 1)

        def post_norm(dve, k, post_gain, r0, q0, pre_gain):
            post_scale(dve, k, 0, post_gain)
            for kt in range(KT):
                if kt + 1 < KT:
                    post_scale(dve, k, kt + 1, post_gain)
                prep_dve(dve, r0 + kt, q0 + kt, pre_gain)

        def post_norm_pool(pool, k, r0, q0):
            for kt in range(KT):
                s = kt % 2
                pool.wait_ge(scaled, KT * k + kt + 1)
                pool.wait_ge(h_loaded[s], 16 * (4 * k + kt // 2 + 1))
                pool.wait_ge(x_lo, r0 + kt - 1)
                pool.wait_ge(x_sq, q0 + kt - 1)
                pool.wait_ge(src_stored[s], 16 * ((r0 + kt) // 2))
                nc.gpsimd.tensor_tensor(src[:, s, :], y[:, kt, :], hres[:, s, :], ALU.add).then_inc(added, 1)

        def post_norm_act(act, k, r0, q0, pre_gain):
            for kt in range(KT):
                prep_act(act, r0 + kt, q0 + kt, pre_gain, (added, KT * k + kt + 1))
                act.dma_start(residual[kt], src[:, kt % 2, :]).then_inc(src_stored[kt % 2], 16)

        def post_norm_loads(sp, k):
            for s in range(2):
                sp.wait_ge(src_stored[s], 16 * 4 * (k + 1))
            for kt in range(KT):
                if kt >= 2:
                    sp.wait_ge(added, KT * k + kt - 1)
                sp.dma_start(hres[:, kt % 2, :], residual[kt]).then_inc(h_loaded[kt % 2], 16)

        def load_down(sp, c, d, w):
            sp.wait_ge(d_lo, d + 1)
            sp.dma_start(draw[:, :, :], w[bass.ds(c * 2 * P, 2 * P), :].rearrange("(k p) n -> p k n", p=P))\
                .then_inc(d_loaded, 16)

        def split_down_hi(act, d):
            act.wait_ge(d_loaded, 16 * d + 16)
            act.wait_ge(down_done, KT * d + 1)
            nc.scalar.activation(dh[:, :, :], draw[:, :, :], ACT.Copy).then_inc(d_hi, 1)

        def split_down_lo(pool, d):
            pool.wait_ge(d_hi, d + 1)
            nc.gpsimd.tensor_tensor(dl[:, :, :], draw[:, :, :], dh[:, :, :].bitcast(F32), ALU.subtract)\
                .then_inc(d_lo, 1)

        def down_products(pe, steps, c, d, par):
            pe.wait_ge(d_lo, d + 2)
            steps.wait(pe, "l1", c)
            for m in range(KT):
                if m != 1:
                    pe.wait_ge(down_added, KT * d + max(m - 1, 0) + 1)
                for kt in range(2):
                    mm = three_products(4 + 2 * (m % 2), dh[:, kt, m * P:(m + 1) * P], dl[:, kt, m * P:(m + 1) * P],
                                        fh[:, par, kt, :], fl[:, par, kt, :], kt == 0, kt == 1)
                mm.then_inc(down_done, 1)

        def down_add(dve, d, squares=None):
            for m in range(KT):
                dve.wait_ge(down_done, KT * d + m + 2)
                nc.vector.tensor_tensor(y[:, m, :], bank2(2 + m % 2), y[:, m, :], ALU.add).then_inc(down_added, 1)
                if squares is not None:
                    if m:
                        square_sum_dve(dve, squares + m - 1)
            if squares is not None:
                square_sum_dve(dve, squares + KT - 1)

        def y_squares_act(act, d, q0):
            for m in range(KT):
                act.wait_ge(down_added, KT * d + m + 2)
                square_act(act, q0 + m, y[:, m, :])

        ff1_act = Steps(sem("ff1_act"), [f"{x}{t}" for t in range(2) for x in ("cg", "cv", "ge", "h")])
        ff1_dve = Steps(sem("ff1_dve"), [f"{x}{t}" for t in range(2) for x in ("ag", "bg", "av", "bv", "m", "l")])
        ff2_act = Steps(sem("ff2_act"), [f"h{t}" for t in range(2)])
        ff2_dve = Steps(sem("ff2_dve"), [f"{x}{t}" for t in range(2) for x in ("u", "r", "l")])

        def ff1_dve_chunk(dve, c, par, d=None):
            for t in range(2):
                if t and d is not None:
                    down_add(dve, d)
                for r, x in enumerate("gv"):
                    k = 2 * t + r
                    n = U_UP + 4 * c + k
                    tile = 2 * c + t + FF_TILES * r
                    dve.wait_ge(mm_done, n + 1)
                    if t:
                        ff1_dve.wait(dve, f"b{x}0", c)
                        ff1_act.wait(dve, f"c{x}0", c)
                    else:
                        ff1_dve.wait_iterations(dve, c)
                        apart(dve)
                        ff1_act.wait_iterations(dve, c)
                    nc.vector.tensor_tensor(ub[:, r, 2:T + 2], bank2(r), rstd[:, :], ALU.mult).then_inc(evac_done, 1)
                    for back, name in ((1, "a"), (2, "b")):
                        if back == 1:
                            ff1_act.wait(dve, f"c{x}{t}", c)
                        else:
                            ff1_dve.wait(dve, f"a{x}{t}", c)
                        ff1_dve.done(nc.vector.scalar_tensor_tensor(
                            out=cb[:, r, :], in0=ub[:, r, 2 - back:T + 2 - back],
                            scalar=col_at("conv_w", (2 - back) * 2 * FF_TILES + tile), in1=cb[:, r, :],
                            op0=ALU.mult, op1=ALU.add), f"{name}{x}{t}")
                ff1_dve.wait(dve, f"bv{t}", c)
                ff1_act.wait(dve, f"ge{t}", c)
                ff1_dve.done(nc.vector.tensor_tensor(cb[:, 1, :], cb[:, 0, :], cb[:, 1, :], ALU.mult), f"m{t}")
                ff1_act.wait(dve, f"h{t}", c)
                ff1_dve.done(nc.vector.tensor_tensor(fl[:, par, t, :], cb[:, 1, :],
                                                     fh[:, par, t, :].bitcast(F32), ALU.subtract), f"l{t}")

        def ff1_act_chunk(act, c, par):
            for t in range(2):
                for r, x in enumerate("gv"):
                    k = 2 * t + r
                    n = U_UP + 4 * c + k
                    tile = 2 * c + t + FF_TILES * r
                    split_hi(act, n + 2, r)
                    act.wait_ge(evac_done, n + 1)
                    if t:
                        ff1_dve.wait(act, "l0", c)
                    else:
                        ff1_dve.wait_iterations(act, c)
                    apart(act)
                    ff1_act.done(nc.scalar.activation(cb[:, r, :], ub[:, r, 2:T + 2], ACT.Identity,
                                                      scale=col_at("conv_w", 2 * 2 * FF_TILES + tile),
                                                      bias=col_at("conv_b", tile)), f"c{x}{t}")
                ff1_dve.wait(act, f"bg{t}", c)
                ff1_act.done(nc.scalar.activation(cb[:, 0, :], cb[:, 0, :], ACT.Gelu_apprx_tanh), f"ge{t}")
                ff1_dve.wait(act, f"m{t}", c)
                if not isinstance(c, int) or c >= 1:
                    act.wait_ge(down_done, KT * (c - 1) + 1)
                ff1_act.done(nc.scalar.activation(fh[:, par, t, :], cb[:, 1, :], ACT.Copy), f"h{t}")

        def ff2_dve_chunk(dve, c, par, d=None):
            for t in range(2):
                if t and d is not None:
                    down_add(dve, d)
                n = U_UP2 + 2 * c + t
                dve.wait_ge(mm_done, n + 1)
                apart(dve)
                if t:
                    ff2_dve.wait(dve, "l0", c)
                else:
                    ff2_dve.wait_iterations(dve, c)
                nc.vector.tensor_tensor(cb[:, 0, :], bank2((U_UP2 + t) % 2), rstd[:, :], ALU.mult)\
                    .then_inc(evac_done, 1)
                dve.wait_ge(evac_done, n + 1)
                ff2_dve.done(nc.vector.tensor_scalar(cb[:, 1, :], cb[:, 0, :], 0.0, None, ALU.max), f"u{t}")
                ff2_dve.wait(dve, f"u{t}", c)
                ff2_dve.done(nc.vector.tensor_tensor(cb[:, 0, :], cb[:, 1, :], cb[:, 1, :], ALU.mult), f"r{t}")
                ff2_act.wait(dve, f"h{t}", c)
                ff2_dve.wait(dve, f"r{t}", c)
                ff2_dve.done(nc.vector.tensor_tensor(fl[:, par, t, :], cb[:, 0, :],
                                                     fh[:, par, t, :].bitcast(F32), ALU.subtract), f"l{t}")

        def ff2_act_chunk(act, c, par, last=False):
            for t in range(2):
                n = U_UP2 + 2 * c + t
                if not last:
                    split_hi(act, n + 2, (U_UP2 + t) % 2)
                ff2_dve.wait(act, f"r{t}", c)
                act.wait_ge(down_done, KT * (DOWN1 - 1 + c) + 1)
                ff2_act.done(nc.scalar.activation(fh[:, par, t, :], cb[:, 0, :], ACT.Copy), f"h{t}")


        @block.sync
        def _(sp):
            sp.dma_start(cols[:, :], a["vectors"]).then_inc(cols_ready, 16)
            for t in range(TT):
                sp.dma_start(xin[:, t, :], a["x"][t * P:(t + 1) * P, :]).then_inc(x_loaded[t % 2], 16)
            for s in range(2):
                load_w(sp, s, s, w_cols(a["w_in"], s * P), first=True)
            with sp.Fori(1, IN_TILES // 2) as i:
                for s in range(2):
                    load_w(sp, 2 * i + s, s, w_cols(a["w_in"], i * (2 * P) + s * P))
            for s in range(2):
                load_w(sp, U_OUT + s, s, w_cols(a["w_out"], s * P))
            for s in range(2):
                sp.wait_ge(stage_stored[s], 8 * IN_TILES + 1)
            sp.wait_ge(phase, 4)
            sp.dma_start(wa[:, :], proj1[WA_TILE]).then_inc(lora_ready, 16)
            sp.dma_start(gl[:, :], proj1[G_TILE]).then_inc(lora_ready, 16)

            def rwkv_loads(j, last):
                if last is not None:
                    rw_dve.wait(sp, "z", last)
                    apart(sp)
                    rw_pe.wait(sp, "bonus", last)
                    apart(sp)
                for k in range(3):
                    sp.dma_start(rkv[:, k, :], proj1[bass.ds(RWKV_TILES * k + j, 1)].rearrange("a p n -> (a p) n"))\
                        .then_inc(rkv_ready, 16)
                sp.dma_start(lora_w[0:64, :], a["w_decay_up"][:, bass.ds(j * P, P)]).then_inc(rkv_ready, 16)
                sp.dma_start(lora_w[64:128, :], a["w_iclr_up"][:, bass.ds(j * P, P)]).then_inc(rkv_ready, 16)
                if last is not None:
                    rw_pe.wait(sp, "gate1", last)
                    apart(sp)
                sp.dma_start(gate_w[:, :], a["w_gate_up"][:, bass.ds(j * P, P)]).then_inc(gate_w_ready, 16)

            rwkv_loads(0, None)
            with sp.Fori(1, RWKV_TILES) as j:
                rwkv_loads(j, j - 1)
            sp.wait_ge(phase, 12)
            sp.dma_start(lam_row[:, :], a["lambdas"].rearrange("(o a) b -> o (a b)", o=1)).then_inc(lam_loaded, 16)
            attention_loads(sp, diff, proj1, (14, 18, 22))
            for kt in range(2, KT):
                load_w(sp, U_OUT + kt, kt % 2, w_cols(a["w_out"], kt * P))
            for s in range(2):
                load_w(sp, U_UP + s, s, w_cols(a["w_up"], s * D_FF))
            sp.wait_ge(phase, 20)
            post_norm_loads(sp, 0)
            with sp.Fori(0, DOWN1 - 1) as c:
                for k in range(2, 6):
                    load_w(sp, U_UP + 4 * c + k, k % 2,
                           w_cols(a["w_up"], c * (2 * P) + (k // 2 * P + k % 2 * D_FF)))
                load_down(sp, c, c, a["w_down"])
            c = DOWN1 - 1
            for k in range(2):
                load_w(sp, U_UP + 4 * c + 2 + k, k, w_cols(a["w_up"], (2 * c + 1) * P + k * D_FF))
            load_w(sp, U_FA, 0, w_cols(a["w_in_2"], FA_COL))
            load_w(sp, U_QKV2, 1, w_cols(a["w_in_2"], 0))
            load_down(sp, c, c, a["w_down"])
            sp.wait_ge(down_done, KT * DOWN1 + 1)
            post_norm_loads(sp, 1)
            sp.wait_ge(x_lo, 17)
            sp.dma_start(small[0:FOX_HEADS, 5:6], a["forget_bias"]).then_inc(fa_loaded, 16)
            sp.dma_start(rel[:, REL - N_REL + 1:REL], a["rel_bias"][:, 0:N_REL - 1]).then_inc(rel_loaded, 16)
            for u in range(1, 12):
                load_w(sp, U_QKV2 + u, (U_QKV2 + u) % 2, w_cols(a["w_in_2"], u * P))
            with sp.Fori(0, 14) as i:
                for k in range(2):
                    load_w(sp, U_QKV2 + 12 + 2 * i + k, (U_QKV2 + k) % 2,
                           w_cols(a["w_in_2"], i * (2 * P) + (Q2_COL + k * P)))
            sp.wait_ge(rel_filled, 1)
            sp.dma_start(rel_d, rel[:, :].rearrange("h (o n) -> h o n", o=1).to_broadcast([FOX_HEADS, P, REL]))\
                .then_inc(rel_stored, 16)
            sp.wait_ge(fa_dve, 4)
            sp.dma_start(cneg_d, cneg[:, :]).then_inc(fa_stored, 16)
            for s in range(2):
                load_w(sp, U_BRANCH + s, (U_BRANCH + s) % 2, w_cols(a["w_branch"], s * P))
            for k in range(2):
                sp.wait_ge(stage_stored[k], 16 * (IN_TILES // 2 + 20) + 1)
            sp.wait_ge(rel_stored, 16)
            sp.wait_ge(fa_stored, 16)
            sp.wait_ge(phase, 28)

            def fox_bias(j, m):
                row = cneg_d[bass.ds(2 * j + m, 1), :]
                return sp.dma_start(bias[:, m, :], bass.AP(tensor=row.tensor, offset=row.offset, ap=[[0, P], [1, T]]))

            def band_bias(j, m):
                rows = rel_d[bass.ds(2 * j + m, 1)]
                return sp.dma_start(bias[:, m, 0:BAND], bass.AP(tensor=rows.tensor, offset=rows.offset + (P - 1),
                                                                ap=[[REL - 1, P], [1, BAND]]))

            attention_loads(sp, fox, proj2, (0, 4, 8), fox_bias)
            sp.wait_ge(phase, 32)
            attention_loads(sp, band, proj2, (12, 16, 20), band_bias)
            sp.wait_ge(phase, 36)
            for m in range(KT):
                if m >= 2:
                    sp.wait_ge(gated_b, m - 1)
                for b in range(2):
                    sp.dma_start(gates[:, m % 2, b, :], proj2[24 + 8 * b + m]).then_inc(gate_loaded[m % 2], 16)
                n = U_BRANCH + m + 2
                w = a["w_branch"] if m + 2 < KT else a["w_out_2"]
                load_w(sp, n, n % 2, w_cols(w, (m + 2) % KT * P))
            for kt in range(KT):
                if kt >= 2:
                    sp.wait_ge(evac_done, U_OUT2 + kt - 1)
                if kt == 0:
                    for s in range(2):
                        sp.wait_ge(src_stored[s], 16 * 12)
                sp.dma_start(hres2[:, kt % 2, :], residual[kt]).then_inc(h2_loaded[kt % 2], 16)
                n = U_OUT2 + kt + 2
                if kt + 2 < KT:
                    load_w(sp, n, n % 2, w_cols(a["w_out_2"], (kt + 2) * P))
                else:
                    load_w(sp, n, n % 2, w_cols(a["w_up_2"], (kt + 2 - KT) * P))
            sp.wait_ge(mm_done, U_UP2)
            for s in range(2):
                sp.wait_ge(src_stored[s], 16 * 16)
            for kt in range(KT):
                sp.dma_start(y[:, kt, :], residual[kt]).then_inc(y_loaded, 16)
            with sp.Fori(0, DOWN2 - 1) as c:
                for k in range(2):
                    load_w(sp, U_UP2 + 2 * c + 2 + k, (U_UP2 + k) % 2,
                           w_cols(a["w_up_2"], c * (2 * P) + (k + 2) * P))
                load_down(sp, c, DOWN1 + c, a["w_down_2"])
            load_down(sp, DOWN2 - 1, DOWN1 + DOWN2 - 1, a["w_down_2"])

        @block.gpsimd
        def _(pool):
            for steps in (diff.pool, fox.pool, band.pool):
                steps.start(pool)
            pool.sem_inc(d_lo, 1)
            nc.gpsimd.memset(ident[:, :], 0.0).then_inc(consts, 1)
            nc.gpsimd.memset(ones[:, :], 1.0).then_inc(consts, 1)
            nc.gpsimd.memset(small[:, 0:1], NORM_EPS).then_inc(consts, 1)
            pool.wait_ge(consts, 3)
            nc.gpsimd.memset(small[:, 1:2], RWKV_LN_EPS).then_inc(consts, 1)
            nc.gpsimd.memset(headones[:, :], 0.0).then_inc(consts, 1)
            pool.wait_ge(consts, 5)
            nc.gpsimd.affine_select(out=ident[:, :], in_=ident[:, :], compare_op=ALU.not_equal, fill=1.0,
                                    base=0, pattern=[[-1, P]], channel_multiplier=1).then_inc(consts, 1)
            for h in range(2):
                pool.wait_ge(consts, 6 + h)
                nc.gpsimd.memset(headones[64 * h:64 * h + 64, 64 * h:64 * h + 64], 1.0).then_inc(consts, 1)
            pool.wait_ge(consts, 8)
            for s in range(2):
                split_lo(pool, s, s)
            with pool.Fori(1, IN_TILES // 2) as i:
                for s in range(2):
                    split_lo(pool, 2 * i + s, s)
            for s in range(2):
                split_lo(pool, U_OUT + s, s)
            phase_end(pool, 1)
            made = [0]

            def mask(ins):
                ins.then_inc(masks, 1)
                made[0] += 1
                pool.wait_ge(masks, made[0])

            mask(nc.gpsimd.memset(chunk_mask[:, :], 1.0))
            mask(nc.gpsimd.memset(chunk_mask[:, 0:T:CHUNK], 0.0))
            mask(nc.gpsimd.memset(causal2[:, :, :], 1.0))
            mask(nc.gpsimd.memset(strict_t[:, :], 1.0))
            for k, op in enumerate((ALU.is_gt, ALU.is_ge)):
                mask(nc.gpsimd.affine_select(out=causal2[:, k, :], in_=causal2[:, k, :], compare_op=op, fill=0.0,
                                             base=0, pattern=[[1, P]], channel_multiplier=-1))
            mask(nc.gpsimd.affine_select(out=strict_t[:, :], in_=strict_t[:, :], compare_op=ALU.is_gt, fill=0.0,
                                         base=0, pattern=[[-1, P]], channel_multiplier=1))
            for c in range(NCH - 1):
                lo, hi = c * CHUNK, (c + 1) * CHUNK
                mask(nc.gpsimd.memset(causal2[lo:hi, :, hi:P], 0.0))
                mask(nc.gpsimd.memset(strict_t[hi:hi + CHUNK, 0:hi], 0.0))
            for h in range(2):
                other = slice(64 - 64 * h, 128 - 64 * h)
                mask(nc.gpsimd.memset(bz[other, h, :], 0.0))
                mask(nc.gpsimd.memset(kz[other, h, :], 0.0))
            phase_end(pool, 2)
            phase_end(pool, 3)
            mask(nc.gpsimd.iota(bias[:, 0, :], pattern=[[1, T]], base=-(T - P), channel_multiplier=-1,
                                allow_small_or_imprecise_dtypes=True))
            mask(nc.gpsimd.affine_select(out=bias[:, 0, :], in_=bias[:, 0, :], compare_op=ALU.is_ge, fill=NEG,
                                         base=T - P, pattern=[[-1, T]], channel_multiplier=1))
            mask(nc.gpsimd.memset(small[:, 3:4], SUBLN_EPS))
            phase_end(pool, 4)
            attention_pool(pool, diff, 4)
            phase_end(pool, 5)
            for n in range(U_OUT + 2, U_UP + 2):
                split_lo(pool, n, n % 2)
            post_norm_pool(pool, 0, 8, 16)
            for kt in range(KT):
                pool.wait_ge(added, kt + 1)
                nc.gpsimd.memset(y[:, kt, :], 0.0).then_inc(y_zero, 1)
            for k in range(2, 6):
                split_lo(pool, U_UP + k, k % 2)
            with pool.Fori(1, DOWN1) as c:
                split_down_lo(pool, c - 1)
                for k in range(2, 6):
                    split_lo(pool, U_UP + 4 * c + k, k % 2)
            split_down_lo(pool, DOWN1 - 1)
            post_norm_pool(pool, 1, 16, 32)
            split_lo(pool, U_QKV2 + 1, (U_QKV2 + 1) % 2)
            pool.wait_ge(x_lo, 24)
            nc.gpsimd.memset(fa_ones[:, :], 1.0).then_inc(fa_set, 1)
            pool.wait_ge(rel_loaded, 16)
            nc.gpsimd.memset(rel[:, 0:REL - N_REL + 1], 0.0).then_inc(fa_set, 1)
            pool.wait_ge(fa_set, 2)
            first = REL - N_REL + 1
            nc.gpsimd.tensor_scalar(rel[:, 0:first], rel[:, 0:first], rel[:, first:first + 1], None, ALU.add)\
                .then_inc(rel_filled, 1)
            with pool.Fori(0, 20) as i:
                for k in range(2):
                    split_lo(pool, U_QKV2 + 2 + 2 * i + k, (U_QKV2 + k) % 2)
            phase_end(pool, 6)
            mask(nc.gpsimd.memset(tri[:, :], 0.0))
            mask(nc.gpsimd.affine_select(out=tri[:, :], in_=tri[:, :], compare_op=ALU.is_ge, fill=NEG,
                                         base=0, pattern=[[-1, P]], channel_multiplier=1))
            phase_end(pool, 7)
            attention_pool(pool, fox, 0)
            phase_end(pool, 8)
            attention_pool(pool, band, 4)
            phase_end(pool, 9)
            for n in range(U_BRANCH + 2, U_UP2 + 2):
                split_lo(pool, n, n % 2)
            for k in range(2, 4):
                split_lo(pool, U_UP2 + k, (U_UP2 + k) % 2)
            with pool.Fori(1, DOWN2 - 1) as c:
                split_down_lo(pool, DOWN1 + c - 1)
                for k in range(2, 4):
                    split_lo(pool, U_UP2 + 2 * c + k, (U_UP2 + k) % 2)
            for c in (DOWN2 - 2, DOWN2 - 1):
                split_down_lo(pool, DOWN1 + c)

        @block.scalar
        def _(act):
            for steps in (rw_act, diff.act, fox.act, band.act, diff.split_act, fox.split_act, band.split_act, ff1_act,
                          ff2_act):
                steps.start(act)
            act.wait_ge(cols_ready, 16)
            for s in range(2):
                split_hi(act, s, s, first=True)
            for kt in range(KT):
                s = kt % 2
                act.wait_ge(xt_done, kt + 1)
                if kt >= 2:
                    act.wait_ge(x_lo, kt - 1)
                    act.wait_ge(x_sq, kt - 1)
                    act.wait_ge(src_stored[s], 16 * (kt // 2))
                nc.scalar.activation(src[:, s, :], bank2(s), ACT.Copy).then_inc(src_ready, 1)
                prep_act(act, kt, kt, "ln_attn_pre", (src_ready, kt + 1))
                act.dma_start(residual[kt], src[:, s, :]).then_inc(src_stored[s], 16)
            act.wait_ge(consts, 8)
            stat_root_act(act, 0)

            def store_stage(n, s, staged):
                act.wait_ge(staged[0], n + staged[1])
                act.dma_start(proj1[bass.ds(n, 1)].rearrange("a p n -> (a p) n"), stage[:, s, :])\
                    .then_inc(stage_stored[s], 16)

            for lo, hi, staged in ((0, SHIFTED_TILES // 2, (stage_ready, 2)),
                                   (SHIFTED_TILES // 2, IN_TILES // 2, (evac_done, 1))):
                with act.Fori(lo, hi) as i:
                    for s in range(2):
                        split_hi(act, 2 * i + 2 + s, s)
                        store_stage(2 * i + s, s, staged)
            phase_end(act, 1)
            act.wait_ge(lora_ready, 32)
            nc.scalar.activation(wa[0:64, :], wa[0:64, :], ACT.Tanh).then_inc(lora_act, 1)
            nc.scalar.activation(gl[:, :], gl[:, :], ACT.Sigmoid).then_inc(lora_act, 1)
            phase_end(act, 2)
            with act.Fori(0, RWKV_TILES) as j:
                rwkv_act(act, j)
            phase_end(act, 3)
            act.wait_ge(lam_dve, 2)
            nc.scalar.activation(lam_dots[:, 0:2], lam_dots[:, 0:2], ACT.Exp).then_inc(lam_act, 1)
            nc.scalar.activation(small[:, 4:5], col("diff_subln", 0), ACT.Copy, scale=1.0 - LAM_INIT)\
                .then_inc(lam_act, 1)
            phase_end(act, 4)
            attention_loop(act, attention_act, attention_split_act, diff, 4)
            phase_end(act, 5)
            for kt in range(KT):
                n = U_OUT + kt
                split_hi(act, n + 2, n % 2)
                act.wait_ge(mm_done, n + 1)
                nc.scalar.activation(y[:, kt, :], bank2(n % 2), ACT.Copy).then_inc(evac_done, 1)
                act.wait_ge(evac_done, n + 1)
                square_act(act, 8 + kt, y[:, kt, :])
            stat_root_act(act, 1)
            post_norm_act(act, 0, 8, 16, "ln_ffn_pre")
            stat_root_act(act, 2)
            ff1_act_chunk(act, 0, 0)
            with act.Fori(0, DOWN1 // 2) as i:
                for h in range(2):
                    c = 2 * i + 1 + h
                    split_down_hi(act, c - 1)
                    ff1_act_chunk(act, c, (1 + h) % 2)
            split_down_hi(act, DOWN1 - 1)
            y_squares_act(act, DOWN1 - 1, 24)
            stat_root_act(act, 3)
            post_norm_act(act, 1, 16, 32, "norm1_2")
            split_hi(act, U_FA + 2, U_FA % 2)
            stat_root_act(act, 4)
            act.wait_ge(fa_dve, 2)
            nc.scalar.activation(fa_abs[:, :], fa[:, :], ACT.Abs).then_inc(fa_act, 1)
            act.wait_ge(fa_act, 1)
            nc.scalar.activation(fa_abs[:, :], fa_abs[:, :], ACT.Exp, scale=-1.0).then_inc(fa_act, 1)
            act.wait_ge(fa_act, 2)
            nc.scalar.activation(fa_abs[:, :], fa_abs[:, :], ACT.Ln, bias=ones[0:FOX_HEADS, 0:1]).then_inc(fa_act, 1)
            with act.Fori(0, 20) as i:
                for k in range(2):
                    u = 2 * i + k
                    split_hi(act, U_QKV2 + 2 + u, (U_QKV2 + k) % 2)
                    act.wait_ge(evac_done, U_QKV2 + 1 + u)
                    act.dma_start(proj2[bass.ds(u, 1)].rearrange("a p n -> (a p) n"), stage[:, k, :])\
                        .then_inc(stage_stored[k], 16)
            phase_end(act, 6)
            phase_end(act, 7)
            attention_loop(act, attention_act, attention_split_act, fox, 0)
            phase_end(act, 8)
            attention_loop(act, attention_act, attention_split_act, band, 4)
            phase_end(act, 9)
            for m in range(KT):
                n = U_BRANCH + m
                act.wait_ge(gate_loaded[m % 2], 32 * (m // 2 + 1))
                nc.scalar.activation(gates[:, m % 2, :, :], gates[:, m % 2, :, :], ACT.Sigmoid)\
                    .then_inc(gate_done, 1)
                split_hi(act, n + 2, n % 2)
                act.wait_ge(merged_done, m + 1)
                nc.scalar.activation(xh2[:, m, :], merged[:, m % 2, :], ACT.Copy).then_inc(m_hi, 1)
            for kt in range(KT):
                n = U_OUT2 + kt
                split_hi(act, n + 2, n % 2)
                prep_act(act, 24 + kt, 40 + kt, "norm2_2", (evac_done, n + 1))
                act.dma_start(residual[kt], src[:, kt % 2, :]).then_inc(src_stored[kt % 2], 16)
            stat_root_act(act, 5)
            ff2_act_chunk(act, 0, 0)
            with act.Fori(0, DOWN2 // 2 - 1) as i:
                for h in range(2):
                    c = 2 * i + 1 + h
                    split_down_hi(act, DOWN1 - 1 + c)
                    ff2_act_chunk(act, c, (1 + h) % 2)
            split_down_hi(act, DOWN1 + DOWN2 - 2)
            ff2_act_chunk(act, DOWN2 - 1, 1, last=True)
            split_down_hi(act, DOWN1 + DOWN2 - 1)
            y_squares_act(act, DOWN1 + DOWN2 - 1, 48)
            act.wait_ge(out_sum, 1)
            nc.scalar.activation(token_rstd[:, :], ps[:, 6, 0:TT], ACT.Sqrt, bias=small[:, 0:1], scale=1.0 / D)\
                .then_inc(out_root, 1)
            act.wait_ge(out_root, 2)
            for t in range(TT):
                s = t % 2
                act.wait_ge(out_turned, t + 1)
                if t >= 2:
                    act.wait_ge(out_stored[s], 16 * (t // 2))
                nc.scalar.activation(out_tile[:, s, :], bank2(s), ACT.Copy, scale=token_rstd[:, t:t + 1])\
                    .then_inc(out_ready, 1)
                act.wait_ge(out_ready, t + 1)
                act.dma_start(out[t * P:(t + 1) * P, :], out_tile[:, s, :]).then_inc(out_stored[s], 16)
            for s in range(2):
                act.wait_ge(out_stored[s], 16 * TT // 2)

        @block.tensor
        def _(pe):
            for steps in (rw_pe, diff.pe, fox.pe, band.pe):
                steps.start(pe)
            pe.sem_inc(down_done, 1)
            pe.wait_ge(consts, 8)
            for s in range(2):
                pe.wait_ge(x_loaded[s], 16 * TT // 2)
            for kt in range(KT):
                s = kt % 2
                if kt >= 2:
                    pe.wait_ge(src_ready, kt - 1)
                for t in range(TT):
                    mm = nc.tensor.transpose(ps[:, 2 * s + t // 4, t % 4 * P:t % 4 * P + P],
                                             xin[:, t, kt * P:(kt + 1) * P], ident[:, :])
                mm.then_inc(xt_done, 1)
            stat_products(pe, KT)
            pe.wait_ge(src_ready, KT)
            for s in range(2):
                unit_products(pe, s, s, 0, first=True)
            with pe.Fori(1, IN_TILES // 2) as i:
                for s in range(2):
                    unit_products(pe, 2 * i + s, s, 0)
            phase_end(pe, 1)
            phase_end(pe, 2)
            with pe.Fori(0, RWKV_TILES) as j:
                rwkv_pe(pe, j)
            phase_end(pe, 3)
            pe.wait_ge(lam_dve, 3)
            nc.tensor.matmul(ps[:, 0, 0:1], ones[0:1, :], lam_dots[:, 2:3], start=True, stop=True).then_inc(lam_pe, 1)
            phase_end(pe, 4)
            with pe.Fori(0, DIFF_HEADS) as j:
                attention_pe(pe, diff, j)
            phase_end(pe, 5)
            for n in range(U_OUT, U_UP):
                unit_products(pe, n, n % 2)
            stat_products(pe, 16)
            unit_products(pe, U_UP, 0, 8)
            stat_products(pe, 24)
            for k in range(1, 4):
                unit_products(pe, U_UP + k, k % 2)
            with pe.Fori(0, DOWN1 // 2) as i:
                for h in range(2):
                    c = 2 * i + 1 + h
                    for k in range(4):
                        if k == 2:
                            down_products(pe, ff1_dve, c - 1, c - 1, h)
                        unit_products(pe, U_UP + 4 * c + k, k % 2)
            down_products(pe, ff1_dve, DOWN1 - 1, DOWN1 - 1, (DOWN1 - 1) % 2)
            stat_products(pe, 32)
            unit_products(pe, U_FA, 0, 16)
            stat_products(pe, 40)
            with pe.Fori(0, 20) as i:
                for k in range(2):
                    unit_products(pe, U_QKV2 + 2 * i + k, (U_QKV2 + k) % 2)
            phase_end(pe, 6)
            phase_end(pe, 7)
            with pe.Fori(0, 4) as j:
                attention_pe(pe, fox, j)
            phase_end(pe, 8)
            with pe.Fori(0, 4) as j:
                attention_pe(pe, band, j)
            phase_end(pe, 9)
            for m in range(KT):
                n = U_BRANCH + m
                s = n % 2
                pe.wait_ge(w_lo, n + 1)
                pe.wait_ge(evac_done, n - 1)
                for kt in range(KT):
                    b = kt // 4
                    mm = three_products(4 * b + 2 * s, wh[:, s, kt, :], wl[:, s, kt, :], xh[:, kt, :], xl[:, kt, :],
                                        kt % 4 == 0, kt % 4 == 3)
                mm.then_inc(mm_done, 1)
            pe.wait_ge(m_lo, KT)
            for n in range(U_OUT2, U_UP2):
                unit_products(pe, n, n % 2, x=(xh2, xl2))
            unit_products(pe, U_UP2, U_UP2 % 2, 24)
            stat_products(pe, 48)
            unit_products(pe, U_UP2 + 1, (U_UP2 + 1) % 2)
            with pe.Fori(0, DOWN2 // 2 - 1) as i:
                for h in range(2):
                    c = 2 * i + 1 + h
                    for k in range(2):
                        if k:
                            down_products(pe, ff2_dve, c - 1, DOWN1 - 1 + c, h)
                        unit_products(pe, U_UP2 + 2 * c + k, (U_UP2 + k) % 2)
            c = DOWN2 - 1
            for k in range(2):
                unit_products(pe, U_UP2 + 2 * c + k, (U_UP2 + k) % 2)
                down_products(pe, ff2_dve, c - 1 + k, DOWN1 - 1 + c + k, (c - 1 + k) % 2)
            pe.wait_ge(ss_done, 56)
            for t in range(TT):
                mm = nc.tensor.matmul(ps[:, 6, t:t + 1], ss[:, t * P:(t + 1) * P], ones[:, 0:1], start=True,
                                      stop=True)
            mm.then_inc(out_sum, 1)
            pe.wait_ge(gained, KT)
            for t in range(TT):
                if t >= 2:
                    pe.wait_ge(out_ready, t - 1)
                for kt in range(KT):
                    mm = nc.tensor.transpose(ps[:, 2 * (t % 2) + kt // 4, kt % 4 * P:kt % 4 * P + P],
                                             y[:, kt, t * P:(t + 1) * P], ident[:, :])
                mm.then_inc(out_turned, 1)

        @block.vector
        def _(dve):
            for steps in (rw_dve, diff.dve, fox.dve, band.dve, diff.split_dve, fox.split_dve, band.split_dve, ff1_dve,
                          ff2_dve):
                steps.start(dve)
            for counted in (stage_ready, down_added, *stage_stored):
                dve.sem_inc(counted, 1)
            nc.vector.memset(shifted[:, 0:1], 0.0).then_inc(shift_done, 1)
            dve.wait_ge(cols_ready, 16)
            for kt in range(KT):
                prep_dve(dve, kt, kt, "ln_attn_pre")
            stat_reciprocal(dve, 0)

            with dve.Fori(0, SHIFTED_TILES // 2) as i:
                for s in range(2):
                    n = 2 * i + s
                    dve.wait_ge(mm_done, n + 1)
                    dve.wait_ge(stage_ready, n + 1)
                    dve.wait_ge(shift_done, 1)
                    nc.vector.tensor_tensor(shifted[:, 1:T + 1], bank2(s), rstd[:, :], ALU.mult)\
                        .then_inc(evac_done, 1)
                    dve.wait_ge(evac_done, n + 1)
                    nc.vector.tensor_tensor(diff_t[:, :], shifted[:, 0:T], shifted[:, 1:T + 1], ALU.subtract)\
                        .then_inc(shift_done, 1)
                    dve.wait_ge(shift_done, n + 2)
                    dve.wait_ge(stage_stored[s], 16 * i + 1)
                    nc.vector.scalar_tensor_tensor(out=stage[:, s, :], in0=diff_t[:, :],
                                                   scalar=col_at("mu_shift", n), in1=shifted[:, 1:T + 1],
                                                   op0=ALU.mult, op1=ALU.add).then_inc(stage_ready, 1)
            with dve.Fori(SHIFTED_TILES // 2, IN_TILES // 2) as i:
                for s in range(2):
                    n = 2 * i + s
                    dve.wait_ge(mm_done, n + 1)
                    dve.wait_ge(stage_stored[s], 16 * i + 1)
                    nc.vector.tensor_tensor(stage[:, s, :], bank2(s), rstd[:, :], ALU.mult)\
                        .then_inc(evac_done, 1)
            phase_end(dve, 1)
            phase_end(dve, 2)
            with dve.Fori(0, RWKV_TILES) as j:
                rwkv_dve(dve, j)
            phase_end(dve, 3)
            dve.wait_ge(lam_loaded, 16)
            for k in range(2):
                if k:
                    dve.wait_ge(lam_dve, k)
                nc.vector.tensor_tensor_reduce(lam_tmp[:, :], lam_row[:, 128 * k:128 * k + 64],
                                               lam_row[:, 128 * k + 64:128 * k + 128], 1.0, 0.0, ALU.mult, ALU.add,
                                               lam_dots[:, k:k + 1]).then_inc(lam_dve, 1)
            dve.wait_ge(lam_act, 1)
            nc.vector.scalar_tensor_tensor(out=lam_dots[:, 2:3], in0=lam_dots[:, 1:2], scalar=-LAM_INIT,
                                           in1=lam_dots[:, 0:1], op0=ALU.add, op1=ALU.subtract).then_inc(lam_dve, 1)
            dve.wait_ge(lam_pe, 1)
            nc.vector.tensor_copy(small[:, 2:3], ps[:, 0, 0:1]).then_inc(lam_dve, 1)
            phase_end(dve, 4)
            attention_loop(dve, attention_dve, attention_split_dve, diff)
            phase_end(dve, 5)
            for kt in range(KT):
                square_sum_dve(dve, 8 + kt)
            stat_reciprocal(dve, 1)
            post_norm(dve, 0, "ln_attn_post", 8, 16, "ln_ffn_pre")
            stat_reciprocal(dve, 2)
            for s in range(2):
                dve.wait_ge(src_stored[s], 16 * 8)
                nc.vector.memset(ub[:, s, 0:2], 0.0).then_inc(ub_pads, 1)
            dve.wait_ge(ub_pads, 2)
            ff1_dve_chunk(dve, 0, 0)
            dve.wait_ge(y_zero, KT)
            with dve.Fori(0, DOWN1 // 2) as i:
                for h in range(2):
                    c = 2 * i + 1 + h
                    ff1_dve_chunk(dve, c, (1 + h) % 2, c - 1)
            down_add(dve, DOWN1 - 1, 24)
            stat_reciprocal(dve, 3)
            post_norm(dve, 1, "ln_ffn_post", 16, 32, "norm1_2")
            stat_reciprocal(dve, 4)
            dve.wait_ge(mm_done, U_FA + 1)
            for s in range(2):
                dve.wait_ge(src_stored[s], 16 * 12)
            nc.vector.tensor_tensor(fa[:, :], ps[0:FOX_HEADS, 0:2, :].rearrange("p a n -> p (a n)"),
                                    rstd[0:FOX_HEADS, :], ALU.mult).then_inc(evac_done, 1)
            dve.wait_ge(fa_loaded, 16)
            dve.wait_ge(evac_done, U_FA + 1)
            nc.vector.tensor_scalar(fa[:, :], fa[:, :], small[0:FOX_HEADS, 5:6], None, ALU.add).then_inc(fa_dve, 1)
            dve.wait_ge(fa_dve, 1)
            nc.vector.tensor_scalar(cneg[:, :], fa[:, :], 0.0, None, ALU.min).then_inc(fa_dve, 1)
            dve.wait_ge(fa_act, 3)
            dve.wait_ge(fa_dve, 2)
            nc.vector.tensor_tensor(fa[:, :], fa_abs[:, :], cneg[:, :], ALU.subtract).then_inc(fa_dve, 1)
            dve.wait_ge(fa_dve, 3)
            dve.wait_ge(fa_set, 1)
            nc.vector.tensor_tensor_scan(cneg[:, :], fa_ones[:, :], fa[:, :], 0.0, ALU.mult, ALU.add)\
                .then_inc(fa_dve, 1)
            with dve.Fori(0, 20) as i:
                for k in range(2):
                    n = U_QKV2 + 2 * i + k
                    dve.wait_ge(mm_done, n + 1)
                    dve.wait_ge(stage_stored[k], 16 * (IN_TILES // 2) + 16 * i + 1)
                    nc.vector.tensor_tensor(stage[:, k, :], bank2((U_QKV2 + k) % 2), rstd[:, :], ALU.mult)\
                        .then_inc(evac_done, 1)
            phase_end(dve, 6)
            phase_end(dve, 7)
            attention_loop(dve, attention_dve, attention_split_dve, fox)
            phase_end(dve, 8)
            attention_loop(dve, attention_dve, attention_split_dve, band)
            phase_end(dve, 9)
            for m in range(KT):
                n = U_BRANCH + m
                s = n % 2
                dve.wait_ge(mm_done, n + 1)
                dve.wait_ge(gate_done, m + 1)
                nc.vector.tensor_tensor(gated[:, m % 2, :], bank2(s), gates[:, m % 2, 0, :], ALU.mult)\
                    .then_inc(gated_a, 1)
                if m >= 2:
                    dve.wait_ge(m_lo, m - 1)
                nc.vector.tensor_tensor(merged[:, m % 2, :], bank2(2 + s), gates[:, m % 2, 1, :], ALU.mult)\
                    .then_inc(gated_b, 1)
                dve.wait_ge(gated_a, m + 1)
                dve.wait_ge(gated_b, m + 1)
                nc.vector.tensor_tensor(merged[:, m % 2, :], merged[:, m % 2, :], gated[:, m % 2, :], ALU.add)\
                    .then_inc(merged_done, 1)
                dve.wait_ge(merged_done, m + 1)
                dve.drain().then_inc(evac_done, 1)
                dve.wait_ge(m_hi, m + 1)
                nc.vector.tensor_tensor(xl2[:, m, :], merged[:, m % 2, :], xh2[:, m, :].bitcast(F32),
                                        ALU.subtract).then_inc(m_lo, 1)
            for kt in range(KT):
                n, r, s = U_OUT2 + kt, 24 + kt, kt % 2
                dve.wait_ge(mm_done, n + 1)
                dve.wait_ge(h2_loaded[s], 16 * (kt // 2 + 1))
                dve.wait_ge(src_stored[s], 16 * (r // 2))
                if kt >= 2:
                    dve.wait_ge(x_sq, 40 + kt - 1)
                    dve.wait_ge(x_lo, r - 1)
                nc.vector.tensor_tensor(src[:, s, :], bank2(n % 2), hres2[:, s, :], ALU.add).then_inc(evac_done, 1)
                prep_dve(dve, r, 40 + kt, "norm2_2")
            stat_reciprocal(dve, 5)
            for s in range(2):
                dve.wait_ge(src_stored[s], 16 * 16)
            ff2_dve_chunk(dve, 0, 0)
            dve.wait_ge(y_loaded, 16 * KT)
            with dve.Fori(0, DOWN2 // 2 - 1) as i:
                for h in range(2):
                    c = 2 * i + 1 + h
                    ff2_dve_chunk(dve, c, (1 + h) % 2, DOWN1 - 1 + c)
            ff2_dve_chunk(dve, DOWN2 - 1, 1, DOWN1 + DOWN2 - 2)
            down_add(dve, DOWN1 + DOWN2 - 1, 48)
            dve.wait_ge(out_root, 1)
            nc.vector.reciprocal(token_rstd[:, :], token_rstd[:, :]).then_inc(out_root, 1)
            for kt in range(KT):
                nc.vector.tensor_scalar(y[:, kt, :], y[:, kt, :], col("final_norm_2", kt), None, ALU.mult)\
                    .then_inc(gained, 1)


_NAMES = ["x", "w_in", "w_decay_up", "w_iclr_up", "w_gate_up", "w_out", "w_up", "w_down", "w_in_2",
          "w_out_2", "w_up_2", "w_down_2"]


def kernel(**inputs):
    from concourse import bacc
    from concourse.bass_utils import run_bass_kernel_spmd

    arrays = {}
    for name in _NAMES:
        w = np.asarray(inputs[name])
        arrays[name] = np.ascontiguousarray(w.reshape(w.shape[-2:]))
    packed = [np.asarray(inputs[name]).reshape(tiles, P) for name, tiles in VECTORS]
    arrays["vectors"] = np.ascontiguousarray(np.concatenate(packed).T)
    arrays["lambdas"] = np.stack([np.asarray(inputs[f"lambda_{k}"]).reshape(-1) for k in ("q1", "k1", "q2", "k2")])
    arrays["forget_bias"] = np.asarray(inputs["forget_bias_2"]).reshape(FOX_HEADS, 1)
    arrays["w_branch"] = np.concatenate([np.asarray(inputs[f"w_branch_{k}_2"])[0] for k in "ab"])
    arrays["rel_bias"] = np.ascontiguousarray(np.asarray(inputs["rel_bias_2"])[0, :, ::-1])
    nc = bacc.Bacc("TRN2", target_bir_lowering=False, num_devices=1)
    aps = {n: nc.dram_tensor(f"in_{n}", v.shape, F32, kind="ExternalInput").ap() for n, v in arrays.items()}
    out = nc.dram_tensor("out", (T, D), F32, kind="ExternalOutput").ap()
    build_program(nc, aps, out)
    r = run_bass_kernel_spmd(nc, [{f"in_{n}": v for n, v in arrays.items()}], core_ids=[0])
    return np.asarray(r.results[0]["out"]).reshape(1, T, D)
```

```python
import math
from contextlib import ExitStack

import numpy as np

import concourse.bass as bass
from concourse import mybir

F32 = mybir.dt.float32
F32R = mybir.dt.float32r
ALU = mybir.AluOpType
ACT = mybir.ActivationFunctionType
AX_X = mybir.AxisListType.X

P = 128
T = 1024
D = 1024
KT = D // P
TT = T // P
HALF = 512

RWKV_TILES = 4
RWKV_HEAD = 64
LORA = 64
DIFF_HEADS = 4
D_FF = 2816
FF_TILES = D_FF // P
FF2_TILES = 4096 // P
IN_TILES = 26
SHIFTED_TILES = 14
WA_TILE, G_TILE = 12, 13
FOX_HEADS = 8
FA_COL = 1536
Q2_COL = FA_COL + FOX_HEADS
DECAY_SCALE = math.exp(-0.5)
NORM_EPS = 1e-6
SUBLN_EPS = 1e-5
RWKV_LN_EPS = 64e-5
NEG = -1e30
LAM_INIT = 0.8 - 0.6
BAND = 5 * P
N_REL = 2 * P + 1
REL = BAND + P - 1

VECTORS = [
    ("ln_attn_pre", KT), ("mu_shift", SHIFTED_TILES), ("w_decay0", 4), ("w_iclr0", 4), ("k_k", 4), ("k_a", 4),
    ("r_k", 4), ("ln_x_w", 4), ("ln_x_b", 4), ("diff_subln", 1), ("ln_attn_post", KT), ("ln_ffn_pre", KT),
    ("conv_w", 3 * 2 * FF_TILES), ("conv_b", 2 * FF_TILES), ("ln_ffn_post", KT), ("norm1_2", KT),
    ("norm2_2", KT), ("final_norm_2", KT),
]
COL = {}
_at = 0
for _name, _tiles in VECTORS:
    COL[_name] = _at
    _at += _tiles
NCOLS = _at

U_IN = 0
U_OUT = U_IN + IN_TILES
U_UP = U_OUT + KT
U_FA = U_UP + 2 * FF_TILES
U_QKV2 = U_FA + 1
U_BRANCH = U_QKV2 + 40
U_OUT2 = U_BRANCH + KT
U_UP2 = U_OUT2 + KT
U_END = U_UP2 + FF2_TILES
DOWN1 = FF_TILES // 2
DOWN2 = FF2_TILES // 2


CHUNK = 64


class Steps:

    def __init__(self, sem, names):
        self.sem, self.names, self.at = sem, names, 0
        self.index = {name: k for k, name in enumerate(names)}
        assert len(self.index) == len(names)

    def start(self, eng):
        eng.sem_inc(self.sem, len(self.names))

    def done(self, instruction, name):
        assert self.names[self.at % len(self.names)] == name, (name, self.names[self.at % len(self.names)])
        self.at += 1
        instruction.then_inc(self.sem, 1)

    def wait(self, eng, name, j):
        eng.wait_ge(self.sem, j * len(self.names) + (len(self.names) + self.index[name] + 1))

    def wait_last(self, eng, names, j):
        if names:
            self.wait(eng, max(names, key=self.index.get), j)

    def wait_iterations(self, eng, j):
        eng.wait_ge(self.sem, j * len(self.names) + len(self.names))


def build_program(nc, a, out):
    ctx = ExitStack()
    with ctx:
        base = 16512
        KB = 1024

        def at(name, offset_kb, shape, dt=F32):
            return nc.alloc_sbuf_tensor_at(name, shape, dt, offset=base + int(offset_kb * KB))

        def sem(name):
            return ctx.enter_context(nc.semaphore(name))

        def dram(name, shape):
            return nc.dram_tensor(name, shape, F32, kind="Internal").ap()

        xh = at("xh", 0, [P, KT, T], F32R)
        xl = at("xl", 32, [P, KT, T], F32R)
        wh = at("wh", 64, [P, 2, KT, P], F32R)
        wl = at("wl", 72, [P, 2, KT, P], F32R)
        wraw = at("wraw", 80, [P, 2, KT, P])
        cols = at("cols", 204, [P, NCOLS])
        ident = at("ident", 205.25, [P, P])
        ones = at("ones", 205.75, [P, P])
        headones = at("headones", 206.25, [P, P])
        small = at("small", 206.75, [P, 64])
        rstd = at("rstd", 144, [P, T])

        src = at("src", 184, [P, 2, T])
        sq = at("sq", 192, [P, 2, T])
        ss = at("ss", 200, [P, T])
        y = at("y", 112, [P, KT, T])
        xin = at("xin", 112, [P, TT, D])
        shifted = at("shifted", 148, [P, T + 8])
        stage = at("stage", 153, [P, 2, T])
        diff_t = at("diff_t", 161, [P, T])
        fa = at("fa", 166, [FOX_HEADS, T])
        fa_abs = at("fa_abs", 170, [FOX_HEADS, T])
        fa_ones = at("fa_ones", 174, [FOX_HEADS, T])
        cneg = at("cneg", 178, [FOX_HEADS, T])
        hres = at("hres", 148, [P, 2, T])
        draw = at("draw", 104, [P, 2, D])
        dh = at("dh", 88, [P, 2, D], F32R)
        dl = at("dl", 96, [P, 2, D], F32R)
        fh = at("fh", 148, [P, 2, 2, T], F32R)
        fl = at("fl", 164, [P, 2, 2, T], F32R)
        ub = at("ub", 180, [P, 2, T + 8])
        cb = at("cb", 188.25, [P, 2, T])
        xh2 = at("xh2", 88, [P, KT, T], F32R)
        xl2 = at("xl2", 148, [P, KT, T], F32R)
        hres2 = at("hres2", 120, [P, 2, T])
        gates = at("gates", 128, [P, 2, 2, T])
        gated = at("gated", 184, [P, 2, T])
        merged = at("merged", 192, [P, 2, T])
        rel = at("rel", 161, [FOX_HEADS, REL])
        out_tile = at("out_tile", 148, [P, 2, D])
        token_rstd = at("token_rstd", 156, [P, TT])

        ps = ctx.enter_context(nc.psum_tensor("ps", [P, 8, HALF], F32))

        def bank2(slot):
            return ps[:, 2 * slot:2 * slot + 2, :]

        residual = dram("residual", (KT, P, T))
        proj1 = dram("proj1", (IN_TILES, P, T))
        proj2 = dram("proj2", (40, P, T))
        cneg_d = dram("cneg_d", (FOX_HEADS, T))
        rel_d = dram("rel_d", (FOX_HEADS, P, REL))

        wa = at("wa", 88, [P, T])
        gl = at("gl", 92, [P, T])
        chunk_mask = at("chunk_mask", 96, [P, T])
        lora_w = at("lora_w", 100, [P, P])
        gate_w = at("gate_w", 100.5, [P, P])
        causal2 = at("causal2", 101, [P, 2, P])
        strict_t = at("strict_t", 102, [P, P])
        ar = at("ar", 104, [P, TT, 2, P])
        bz = at("bz", 112, [P, 2, T])
        kz = at("kz", 120, [P, 2, T])
        bh_t = at("bh_t", 128, [P, TT, P])
        kh_t = at("kh_t", 132, [P, TT, P])
        v_t = at("v_t", 136, [P, TT, P])
        rkv = at("rkv", 16, [P, 3, T])
        sg = at("sg", 156, [P, T])
        iclr = at("iclr", 160, [P, T])
        css = at("css", 164, [P, T])
        dec = at("dec", 168, [P, T])
        dec_inv = at("dec_inv", 172, [P, T])
        kk = at("kk", 176, [P, T])
        kb = at("kb", 180, [P, T])
        bt = at("bt", 184, [P, T])
        bhc = at("bhc", 188, [P, T])
        ktl = at("ktl", 192, [P, T])
        khc = at("khc", 196, [P, T])
        mm_m = at("mm_m", 144, [P, 2, 2, 4, P])
        mm_n = at("mm_n", 48, [P, 2, 2, 4, P])
        mm_rb = at("mm_rb", 56, [P, 2, 4, P])
        mm_ak = at("mm_ak", 60, [P, 2, 4, P])
        mm_rk = at("mm_rk", 28, [P, 2, 4, P])
        mm_x = at("mm_x", 152, [P, 4, 2, 2, 64])
        mm_g = at("mm_g", 48, [P, 4, P])
        mm_phi = at("mm_phi", 52, [P, 8, P])
        mm_psi = at("mm_psi", 184, [P, 8, P])
        states = at("states", 188, [P, 17, P])
        yb = at("yb", 196.5, [P, TT, 2, 64])
        bonus = at("bonus", 200.75, [P, TT, 2])
        y_stats = at("y_stats", 201, [P, TT, 2, 6])
        y_mv = at("y_mv", 201.5, [P, TT, 2, 2])
        y_rs = at("y_rs", 201.75, [P, TT, 2])
        pc = at("pc", 202, [P, 16])
        y_mix = at("y_mix", 140, [P, T])

        qraw = at("qraw", 88, [P, 2, T])
        kraw = at("kraw", 96, [P, 2, T])
        vraw = at("vraw", 104, [P, T])
        qs = at("qs", 108, [P, 2, T], F32R)
        kh = at("kh", 116, [P, 2, T], F32R)
        kl = at("kl", 124, [P, 2, T], F32R)
        vt = at("vt", 132, [P, TT, P])
        bias = at("bias", 136, [P, 2, T])
        ssb = at("ssb", 144, [P, 2, 2, T])
        pm = at("pm", 160, [P, 2, 2, T])
        pt = [at("pt0", 176, [P, 2, T]), at("pt1", 195.5, [P, 2, T])]
        osb = at("osb", 184, [P, TT, P])
        ot = at("ot", 188, [P, T])
        tri = at("tri", 192, [P, P])
        negmax = at("negmax", 192.5, [P, TT, 2])
        rowsum = at("rowsum", 192.625, [P, TT, 2])
        weight = at("weight", 192.75, [P, TT, 2])
        osq = at("osq", 192.875, [P, TT])
        lam_row = at("lam_row", 193, [1, 4 * 64])
        lam_tmp = at("lam_tmp", 194, [1, 64])
        lam_dots = at("lam_dots", 194.5, [1, 4])

        cols_ready = sem("cols_ready")
        consts = sem("consts")
        x_loaded = [sem(f"x_loaded{t}") for t in range(2)]
        xt_done = sem("xt_done")
        xt_read = sem("xt_read")
        src_ready = sem("src_ready")
        src_stored = [sem(f"src_stored{s}") for s in range(2)]
        x_hi = sem("x_hi")
        x_sq = sem("x_sq")
        x_lo = sem("x_lo")
        ss_done = sem("ss_done")
        stat_sum = sem("stat_sum")
        stat_root = sem("stat_root")
        rstd_ready = sem("rstd_ready")
        w_loaded = [sem(f"w_loaded{s}") for s in range(2)]
        w_hi = sem("w_hi")
        w_lo = sem("w_lo")
        mm_done = sem("mm_done")
        evac_done = sem("evac_done")
        shift_done = sem("shift_done")
        stage_ready = sem("stage_ready")
        stage_stored = [sem(f"stage_stored{s}") for s in range(2)]
        phase = sem("phase")
        marks = sem("marks")

        def col(name, i, n=1):
            return cols[:, COL[name] + i:COL[name] + i + n]

        def col_at(name, i):
            return cols[:, bass.ds(COL[name] + i, 1)]

        def w_cols(w, col0, rows=D):
            return w[0:rows, bass.ds(col0, P)].rearrange("(k p) c -> p k c", p=P)

        def load_w(sp, n, s, source, first=False):
            if not first:
                sp.wait_ge(w_lo, n - 1)
            sp.dma_start(wraw[:, s, :, :], source).then_inc(w_loaded[s], 16)

        def split_hi(act, n, s, first=False):
            act.wait_ge(w_loaded[s], 8 * (n - s) + 16)
            if not first:
                act.wait_ge(mm_done, n - 1)
            nc.scalar.activation(wh[:, s, :, :], wraw[:, s, :, :], ACT.Copy).then_inc(w_hi, 1)

        def split_lo(pool, n, s, first=False):
            pool.wait_ge(w_hi, n + 1)
            nc.gpsimd.tensor_tensor(wl[:, s, :, :], wraw[:, s, :, :], wh[:, s, :, :].bitcast(F32),
                                    ALU.subtract).then_inc(w_lo, 1)

        def unit_products(pe, n, s, ready=None, first=False, x=None, before=None):
            hi, lo = x or (xh, xl)
            pe.wait_ge(w_lo, n + 1)
            if not first:
                pe.wait_ge(evac_done, n - 1)
            for kt in range(KT):
                if before is not None:
                    before(kt)
                if ready is not None:
                    pe.wait_ge(x_lo, ready + kt + 1)
                mm = three_products(2 * s, wh[:, s, kt, :], wl[:, s, kt, :], hi[:, kt, :], lo[:, kt, :],
                                    kt == 0, kt == KT - 1)
            mm.then_inc(mm_done, 1)

        def three_products(bank, w_hi_, w_lo_, x_hi_, x_lo_, start, stop):
            for w, x, k in ((w_hi_, x_hi_, 0), (w_hi_, x_lo_, 1), (w_lo_, x_hi_, 2)):
                for h in range(2):
                    mm = nc.tensor.matmul(ps[:, bank + h, :], w, x[:, h * HALF:(h + 1) * HALF],
                                          start=start and k == 0, stop=stop and k == 2)
            return mm

        def square_act(act, q, tile):
            if q >= 2:
                act.wait_ge(ss_done, q - 1)
            nc.scalar.activation(sq[:, q % 2, :], tile, ACT.Square).then_inc(x_sq, 1)

        def square_sum_pe(pe, q):
            if q and q % KT == 0:
                pe.wait_ge(stat_root, q // KT)
            pe.wait_ge(x_sq, q + 1)
            for h in range(2):
                mm = nc.tensor.matmul(ps[:, 6 + h, :], ones[:, :], sq[:, q % 2, h * HALF:(h + 1) * HALF],
                                      start=q % KT == 0, stop=q % KT == KT - 1)
            mm.then_inc(ss_done, 1)

        def square_sum_dve(dve, q):
            dve.wait_ge(x_sq, q + 1)
            if q % KT == 0:
                if q:
                    dve.wait_ge(stat_root, q // KT)
                nc.vector.tensor_copy(ss[:, :], sq[:, q % 2, :]).then_inc(ss_done, 1)
            else:
                dve.wait_ge(ss_done, q)
                nc.vector.tensor_tensor(ss[:, :], ss[:, :], sq[:, q % 2, :], ALU.add).then_inc(ss_done, 1)

        def prep_act(act, r, q, gain, ready):
            kt, s = r % KT, r % 2
            act.wait_ge(ready[0], ready[1])
            nc.scalar.activation(xh[:, kt, :], src[:, s, :], ACT.Identity, scale=col(gain, kt)).then_inc(x_hi, 1)
            square_act(act, q, src[:, s, :])

        def prep_dve(dve, r, q, gain, sums=False):
            kt, s = r % KT, r % 2
            dve.wait_ge(x_hi, r + 1)
            nc.vector.scalar_tensor_tensor(out=xl[:, kt, :], in0=src[:, s, :], scalar=col(gain, kt),
                                           in1=xh[:, kt, :].bitcast(F32), op0=ALU.mult, op1=ALU.subtract)\
                .then_inc(x_lo, 1)
            if sums:
                square_sum_dve(dve, q)

        def apart(eng):
            eng.sem_inc(marks, 1)

        def stat_products(pe, sums):
            pe.wait_ge(ss_done, sums)
            for h in range(2):
                mm = nc.tensor.matmul(ps[:, 6 + h, :], ones[:, :], ss[:, h * HALF:(h + 1) * HALF],
                                      start=True, stop=True)
            mm.then_inc(stat_sum, 1)

        def stat_root_act(act, k, sums=None):
            act.wait_ge(*((ss_done, KT * (k + 1)) if sums is None else (stat_sum, sums)))
            nc.scalar.activation(rstd[:, :], bank2(3), ACT.Sqrt, bias=small[:, 0:1], scale=1.0 / D)\
                .then_inc(stat_root, 1)

        def stat_reciprocal(dve, k):
            dve.wait_ge(stat_root, k + 1)
            nc.vector.reciprocal(rstd[:, :], rstd[:, :]).then_inc(rstd_ready, 1)
            dve.wait_ge(rstd_ready, k + 1)

        def phase_end(eng, k):
            eng.drain().then_inc(phase, 1)
            eng.wait_ge(phase, 4 * k)

        lora_ready = sem("lora_ready")
        lora_w_ready = sem("lora_w_ready")
        rkv_ready = sem("rkv_ready")
        gate_w_ready = sem("gate_w_ready")
        masks = sem("masks")
        lora_act = sem("lora_act")
        NCH = P // CHUNK
        NHALF = 4 * NCH
        LEVELS = CHUNK.bit_length() - 1

        def level_names(g):
            names = []
            for l in range(LEVELS):
                for hh in range(2):
                    names.append(f"X{g}{l}{hh}")
                    if l < LEVELS - 1:
                        names.append(f"M{g}{l}{hh}")
                    if l < LEVELS - 2:
                        names.append(f"N{g}{l}{hh}")
            return names

        def score_names(g):
            return [n for hh in range(2) for n in (f"SB{g}{hh}0", f"SB{g}{hh}1", f"SN{g}{hh}")] + \
                [f"SK{g}{hh}{q}" for hh in range(2) for q in range(2)]

        transposed = [f"t{k}{h}" for k in ("B", "K", "V") for h in range(2)] + ["bonus"]

        def normed(g):
            return [f"rsr{g}"] + [f"ln{b}{hh}" for b in range(4 * g, 4 * g + 4) for hh in range(2)]

        pe_turns = []
        for g in range(2):
            pe_turns.append(f"tA{g}")
            pe_turns += score_names(g)
            if g == 0:
                pe_turns += transposed
            pe_turns += [f"AV{g}0", f"AV{g}1"] + level_names(g)
            if g:
                pe_turns += ["tY0", "gate0"]
            pe_turns += [f"G{g}"] + [f"Phi{g}{q}" for q in range(NCH)] + [f"Psi{g}{q}" for q in range(NCH)]
            if g == 0:
                pe_turns += ["+d0", "+d1", "+i0", "+i1"]
            pe_turns += [f"S{g}{c}" for c in range(NHALF)]
            if g == 0:
                pe_turns += ["+n0", "+n1"]
            pe_turns.append(f"Y{g}")
        pe_turns += ["tY1", "gate1"]
        act_names = ["bz0", "bz1", "kz0", "kz1"]
        for g in range(2):
            act_names.append(f"tA{g}")
            if g == 0:
                act_names += transposed
            act_names += (["rs0"] if g else []) + [n for n in level_names(g) if n[0] == "M"]
        act_names += ["tY0", "rs1", "tY1", "hi"]
        dve_names = ["A", "R", "Bt", "Kt", "Bh", "Kh", "z", "pc"]
        for g in range(2):
            for n in score_names(g):
                dve_names += [n] if n[:2] == "SN" else [n + "m", n + "r"]
            dve_names += [f"AV{g}0", f"AV{g}1"] + (normed(0) if g else [])
            dve_names += [n for n in level_names(g) if n[0] != "M"] + (["gate0"] if g else [])
            dve_names += [f"G{g}"] + [f"Phi{g}{q}" for q in range(NCH)]
            dve_names += [f"PhiD{g}{c}" for c in range(NHALF)] + (["zero"] if g == 0 else [])
            dve_names += [f"Psi{g}{q}" for q in range(NCH)]
            dve_names += [f"S{g}{c}" for c in range(NHALF)] + [f"Y{g}{b}{hh}" for b in range(4) for hh in range(2)]
            dve_names += [f"{x}{b}{hh}" for x in ("bn", "ag") for b in range(4 * g, 4 * g + 4) for hh in range(2)]
        dve_names += normed(1) + ["gate1"]
        pe_names = [n for n in pe_turns if n[0] != "+"]
        rw_pe = Steps(sem("rw_pe"), pe_names)
        rw_act = Steps(sem("rw_act"), act_names)
        rw_dve = Steps(sem("rw_dve"), dve_names)

        rw_pool = Steps(sem("rw_pool"), ["lo"])
        pre_pe = Steps(sem("pre_pe"), ["d0", "d1", "i0", "i1", "n0", "n1"])
        pre_act = Steps(sem("pre_act"), ["w0", "w1", "a0", "a1", "ksq", "r0", "r1", "P", "Pi", "Pp"])
        pre_dve = Steps(sem("pre_dve"), ["css", "cp", "clamp", "rc0", "rc1", "rc2", "rc3", "kk", "kb", "ka", "km"])

        bank_of = {name: k % 8 for k, name in enumerate(pe_turns)}
        read_in = {"d": "w", "i": "a", "n": "r"}

        def reader_of(name, j):
            if name[0] == "+":
                return pre_act, read_in[name[1]] + name[2], j + 1
            kind = name.rstrip("0123456789")
            if kind in ("tB", "tK", "tV", "bonus", "tA", "M", "tY"):
                return rw_act, name, j
            return rw_dve, name + {"SB": "r", "SK": "r", "Y": "31"}.get(kind, ""), j

        def rw_bank(pe, name, j, final):
            k = pe_turns.index(name)
            earlier = [n for n in pe_turns[:k] if bank_of[n] == k % 8 and not (final and n[0] == "+")]
            if earlier:
                steps, reader, at_j = reader_of(earlier[-1], j)
            else:
                steps, reader, at_j = reader_of([n for n in pe_turns if bank_of[n] == k % 8][-1], j - 1)
            steps.wait(pe, reader, at_j)
            return bank_of[name]

        block = ctx.enter_context(nc.Block())

        def prepare_pe(pe, j, what, banks=None):
            if what == "lora":
                pe.wait_ge(lora_w_ready, 32 * j + 32)
                names = ["d0", "d1", "i0", "i1"]
            else:
                pre_act.wait(pe, "ksq", j)
                names = ["n0", "n1"]
            for name in names:
                if banks is not None:
                    rw_bank(pe, "+" + name, banks, False)
                half = slice(int(name[1]) * HALF, (int(name[1]) + 1) * HALF)
                rows = slice(64, 128) if name[0] == "i" else slice(0, 64)
                if what == "lora":
                    ins = nc.tensor.matmul(ps[:, bank_of["+" + name], :], lora_w[rows, :], wa[rows, half],
                                           start=True, stop=True)
                else:
                    ins = nc.tensor.matmul(ps[:, bank_of["+" + name], :], headones[:, :], kk[:, half],
                                           start=True, stop=True)
                pre_pe.done(ins, name)

        def prepare_act(act, j, what):
            fn = nc.scalar.activation
            if what == "lora":
                rw_dve.wait(act, "pc", j - 1)
                for n, k, to, bias_ in (("w", "d", sg, "w_decay0"), ("a", "i", iclr, "w_iclr0")):
                    for h in range(2):
                        pre_pe.wait(act, f"{k}{h}", j)
                        apart(act)
                        pre_act.done(fn(to[:, h * HALF:(h + 1) * HALF], ps[:, bank_of[f"+{k}{h}"], :], ACT.Sigmoid,
                                        bias=col_at(bias_, j)), f"{n}{h}")
                act.wait_ge(rkv_ready, 48 * j + 48)
                apart(act)
                pre_act.done(fn(kk[:, :], rkv[:, 1, :], ACT.Square, scale=col_at("k_k", j)), "ksq")
            elif what == "root":
                for h in range(2):
                    pre_pe.wait(act, f"n{h}", j)
                    pre_act.done(fn(kb[:, h * HALF:(h + 1) * HALF], ps[:, bank_of[f"+n{h}"], :], ACT.Sqrt), f"r{h}")
            elif what == "decays":
                pre_dve.wait(act, "css", j)
                pre_act.done(fn(dec[:, :], css[:, :], ACT.Exp, scale=-DECAY_SCALE), "P")
                pre_act.done(fn(dec_inv[:, :], css[:, :], ACT.Exp, scale=DECAY_SCALE), "Pi")
                pre_dve.wait(act, "cp", j)
                pre_act.done(fn(sg[:, :], sg[:, :], ACT.Exp, scale=-DECAY_SCALE), "Pp")

        def prepare_dve(dve, j, what):
            tt, stt = nc.vector.tensor_tensor, nc.vector.scalar_tensor_tensor
            done = pre_dve.done
            k = rkv[:, 1, :]
            if what == "sum":
                pre_act.wait(dve, "w1", j)
                done(nc.vector.tensor_tensor_scan(css[:, :], chunk_mask[:, :], sg[:, :], 0.0, ALU.mult, ALU.add), "css")
                pre_dve.wait(dve, "css", j)
                done(tt(sg[:, :], css[:, :], sg[:, :], ALU.subtract), "cp")
            elif what == "clamp":
                pre_act.wait(dve, "r1", j)
                done(nc.vector.tensor_scalar(kb[:, :], kb[:, :], 1e-12, None, ALU.max), "clamp")
            elif what in ("norm0", "norm1"):
                for q in range(2):
                    q += 2 * int(what[-1])
                    part = kb[:, q * (T // 4):(q + 1) * (T // 4)]
                    pre_dve.wait(dve, "clamp", j)
                    done(nc.vector.reciprocal(part, part), f"rc{q}")
            elif what == "kk":
                pre_dve.wait(dve, "rc3", j)
                apart(dve)
                pre_pe.wait(dve, "n1", j)
                done(stt(out=kk[:, :], in0=k, scalar=col_at("k_k", j), in1=kb[:, :], op0=ALU.mult, op1=ALU.mult), "kk")
                pre_dve.wait(dve, "kk", j)
                apart(dve)
                pre_act.wait(dve, "a1", j)
                done(tt(kb[:, :], kk[:, :], iclr[:, :], ALU.mult), "kb")
            elif what == "km":
                pre_dve.wait(dve, "kb", j)
                done(nc.vector.tensor_scalar(iclr[:, :], iclr[:, :], 1.0, col_at("k_a", j), ALU.subtract, ALU.mult),
                     "ka")
                pre_dve.wait(dve, "ka", j)
                done(stt(out=k, in0=iclr[:, :], scalar=1.0, in1=k, op0=ALU.add, op1=ALU.mult), "km")

        def rwkv_pe(pe, j, final=False):
            def done(ins, name):
                rw_pe.done(ins, name)

            mm = nc.tensor.matmul

            def transposes(name, source, blocks):
                bank = rw_bank(pe, name, j, final)
                for i, b in enumerate(blocks):
                    ins = nc.tensor.transpose(ps[:, bank, i * P:(i + 1) * P], source(b), ident[:, :])
                done(ins, name)

            def outputs(h):
                rw_dve.wait(pe, f"ln{4 * h + 3}1", j)
                apart(pe)
                transposes(f"tY{h}", lambda b: yb[:, b, :, :], range(4 * h, 4 * h + 4))
                pe.wait_ge(gate_w_ready, 16 * j + 16)
                bank = rw_bank(pe, f"gate{h}", j, final)
                ins = mm(ps[:, bank, :], gate_w[:, :], gl[:, h * HALF:(h + 1) * HALF], start=True, stop=True)
                done(ins, f"gate{h}")

            for g in range(2):
                blocks = range(4 * g, 4 * g + 4)
                if g == 0:
                    rw_dve.wait(pe, "A", j)
                    apart(pe)
                transposes(f"tA{g}", lambda b: ar[:, b, 0, :], blocks)
                rw_act.wait(pe, "bz1", j)
                for name in score_names(g):
                    kind, hh = name[:2], int(name[3])
                    if name == f"SK{g}00":
                        rw_act.wait(pe, "kz1", j)
                        apart(pe)
                    elif name == f"SB{g}00":
                        rw_dve.wait(pe, "R", j)
                        apart(pe)
                    bank = rw_bank(pe, name, j, final)
                    if kind == "SN":
                        for i, b in enumerate(blocks):
                            ins = mm(ps[:, bank, i * P:(i + 1) * P], ar[:, b, 0, :], bz[:, hh, b * P:(b + 1) * P],
                                     start=True, stop=True)
                    else:
                        side = bz if kind == "SB" else kz
                        for i in range(2):
                            b = 4 * g + 2 * int(name[4]) + i
                            ins = mm(ps[:, bank, i * 256:(i + 1) * 256], side[:, hh, b * P:(b + 1) * P],
                                     ar[:, b, :, :], start=True, stop=True)
                    done(ins, name)
                if g == 0:
                    for k, source, ready in (("B", bhc, "Bh"), ("K", khc, "Kh"), ("V", None, "z")):
                        rw_dve.wait(pe, ready, j)
                        apart(pe)
                        for h in range(2):
                            at_b = (lambda b: rkv[:, 2, b * P:(b + 1) * P]) if source is None else \
                                (lambda b, source=source: source[:, b * P:(b + 1) * P])
                            transposes(f"t{k}{h}", at_b, range(4 * h, 4 * h + 4))
                    bank = rw_bank(pe, "bonus", j, final)
                    for b in range(TT):
                        ins = mm(ps[:, bank, 2 * b:2 * b + 2], rkv[:, 0, b * P:(b + 1) * P], headones[:, 0:P:64],
                                 start=True, stop=True)
                    done(ins, "bonus")
                rw_act.wait(pe, "tV1", j)
                for hh in range(2):
                    name = f"AV{g}{hh}"
                    bank = rw_bank(pe, name, j, final)
                    rw_dve.wait(pe, f"SK{g}{hh}1r", j)
                    for i, b in enumerate(blocks):
                        ins = mm(ps[:, bank, i * P:(i + 1) * P], mm_ak[:, hh, i, :], v_t[:, b, :],
                                 start=True, stop=True)
                    done(ins, name)
                rw_act.wait(pe, f"tA{g}", j)
                for l in range(LEVELS):
                    m, n = mm_m[:, l % 2], mm_n[:, l % 2]
                    for hh in range(2):
                        if l == 0:
                            rw_dve.wait(pe, f"AV{g}{hh}", j)
                        else:
                            rw_act.wait(pe, f"M{g}{l - 1}{hh}", j)
                            rw_dve.wait(pe, f"X{g}{l - 1}{hh}", j)
                        name = f"X{g}{l}{hh}"
                        bank = rw_bank(pe, name, j, final)
                        for i in range(4):
                            ins = mm(ps[:, bank, i * P:(i + 1) * P], m[:, hh, i, :], mm_x[:, i, :, hh, :],
                                     start=True, stop=True)
                        done(ins, name)
                        if l < LEVELS - 1:
                            if l:
                                rw_dve.wait(pe, f"N{g}{l - 1}{hh}", j)
                            name = f"M{g}{l}{hh}"
                            bank = rw_bank(pe, name, j, final)
                            for i in range(4):
                                ins = mm(ps[:, bank, i * P:(i + 1) * P], n[:, hh, i, :], m[:, hh, i, :],
                                         start=True, stop=True)
                            done(ins, name)
                        if l < LEVELS - 2:
                            name = f"N{g}{l}{hh}"
                            bank = rw_bank(pe, name, j, final)
                            for i in range(4):
                                ins = mm(ps[:, bank, i * P:(i + 1) * P], m[:, hh, i, :], n[:, hh, i, :],
                                         start=True, stop=True)
                            done(ins, name)
                if g:
                    outputs(0)
                for hh in range(2):
                    rw_dve.wait(pe, f"X{g}{LEVELS - 1}{hh}", j)
                bank = rw_bank(pe, f"G{g}", j, final)
                for i in range(4):
                    for hh in range(2):
                        ins = mm(ps[64 * hh:64 * hh + 64, bank, i * P:(i + 1) * P], mm_x[:, i, 0, hh, :],
                                 mm_rb[:, hh, i, :], start=True, stop=True)
                done(ins, f"G{g}")
                for q in range(NCH):
                    bank = rw_bank(pe, f"Phi{g}{q}", j, final)
                    r = q * CHUNK
                    for i in range(4):
                        ins = mm(ps[:, bank, i * P:(i + 1) * P], mm_x[r:r + CHUNK, i, 0, :, :],
                                 bh_t[r:r + CHUNK, 4 * g + i, :], start=True, stop=True)
                    done(ins, f"Phi{g}{q}")
                for q in range(NCH):
                    bank = rw_bank(pe, f"Psi{g}{q}", j, final)
                    r = q * CHUNK
                    for i in range(4):
                        mm(ps[:, bank, i * P:(i + 1) * P], bh_t[r:r + CHUNK, 4 * g + i, :],
                           mm_x[r:r + CHUNK, i, 1, :, :], start=True, stop=False)
                        ins = mm(ps[:, bank, i * P:(i + 1) * P], kh_t[r:r + CHUNK, 4 * g + i, :],
                                 v_t[r:r + CHUNK, 4 * g + i, :], start=False, stop=True)
                    done(ins, f"Psi{g}{q}")
                if g == 0 and not final:
                    prepare_pe(pe, j + 1, "lora", j)
                rw_dve.wait(pe, f"Psi{g}{NCH - 1}", j)
                for c in range(NHALF):
                    name = f"S{g}{c}"
                    if c:
                        rw_dve.wait(pe, f"S{g}{c - 1}", j)
                    bank = rw_bank(pe, name, j, final)
                    ins = mm(ps[:, bank, 0:P], mm_phi[:, c, :], states[:, NHALF * g + c, :], start=True, stop=True)
                    done(ins, name)
                if g == 0 and not final:
                    prepare_pe(pe, j + 1, "norm", j)
                rw_dve.wait(pe, f"S{g}{NHALF - 1}", j)
                bank = rw_bank(pe, f"Y{g}", j, final)
                for i in range(4):
                    b = 4 * g + i
                    for r in range(NCH):
                        mm(ps[r * CHUNK:(r + 1) * CHUNK, bank, i * P:(i + 1) * P],
                           mm_g[:, i, r * CHUNK:(r + 1) * CHUNK], states[:, NCH * b + r, :],
                           start=(i == 0), stop=False, skip_group_check=True)
                    for hh in range(2):
                        to = ps[:, bank, i * P + 64 * hh:i * P + 64 * hh + 64]
                        mm(to, mm_rb[:, hh, i, :], mm_x[:, i, 1, hh, :], start=False, stop=False,
                           skip_group_check=True)
                        ins = mm(to, mm_rk[:, hh, i, :], v_t[:, b, 64 * hh:64 * hh + 64], start=False,
                                 stop=(i == 3), skip_group_check=True)
                done(ins, f"Y{g}")
            outputs(1)

        def rwkv_act(act, j, final=False):
            def done(ins, name):
                rw_act.done(ins, name)

            def vec(name):
                return col_at(name, j)

            fn = nc.scalar.activation

            def root(h):
                rw_dve.wait(act, f"ag{4 * h + 3}1", j)
                part = slice(4 * h, 4 * h + 4)
                done(fn(y_rs[:, part, :], y_mv[:, part, :, 1], ACT.Sqrt, bias=small[:, 1:2]), f"rs{h}")

            def output(h):
                rw_pe.wait(act, f"tY{h}", j)
                apart(act)
                done(fn(y_mix[:, h * HALF:(h + 1) * HALF], ps[:, bank_of[f"tY{h}"], :], ACT.Identity,
                        bias=vec("ln_x_b"), scale=vec("ln_x_w")), f"tY{h}")

            for source, to, k in ((bt, bz, "b"), (ktl, kz, "k")):
                rw_dve.wait(act, "Bt" if k == "b" else "Kt", j)
                for h in range(2):
                    rows = slice(64 * h, 64 * h + 64)
                    done(fn(to[rows, h, :], source[rows, :], ACT.Copy), f"{k}z{h}")
            for g in range(2):
                if g:
                    rw_pe.wait(act, f"Y{g - 1}", j)
                rw_pe.wait(act, f"tA{g}", j)
                bank = ps[:, bank_of[f"tA{g}"], :].rearrange("p (b c) -> p b c", b=4)
                done(fn(mm_x[:, :, 0, :, :].rearrange("p b h c -> p b (h c)"), bank, ACT.Copy), f"tA{g}")
                if g == 0:
                    for k, to in (("B", bh_t), ("K", kh_t), ("V", v_t)):
                        for h in range(2):
                            name = f"t{k}{h}"
                            rw_pe.wait(act, name, j)
                            done(fn(to[:, 4 * h:4 * h + 4, :], ps[:, bank_of[name], :], ACT.Copy), name)
                    rw_pe.wait(act, "bonus", j)
                    done(fn(bonus[:, :, :], ps[:, bank_of["bonus"], 0:2 * TT], ACT.Copy), "bonus")
                if g:
                    root(0)
                for l in range(LEVELS - 1):
                    for hh in range(2):
                        name = f"M{g}{l}{hh}"
                        rw_pe.wait(act, name, j)
                        done(fn(mm_m[:, (l + 1) % 2, hh, :, :], ps[:, bank_of[name], :], ACT.Copy), name)
                    if g and not final and l == 1:
                        prepare_act(act, j + 1, "decays")
                if g:
                    rw_pool.wait_iterations(act, j)
                    output(0)
                if g == 0 and not final:
                    prepare_act(act, j + 1, "lora")
                    prepare_act(act, j + 1, "root")
            root(1)
            output(1)
            rw_dve.wait(act, "gate1", j)
            apart(act)
            done(fn(xh[:, bass.ds(j, 1), :].rearrange("p a n -> p (a n)"), y_mix[:, :], ACT.Copy), "hi")

        def rwkv_dve(dve, j, final=False):
            last = [None]

            def done(ins, name):
                rw_dve.done(ins, name)
                last[0] = name

            def after(name=None):
                rw_dve.wait(dve, name or last[0], j)

            def vec(name):
                return col_at(name, j)

            tt, stt = nc.vector.tensor_tensor, nc.vector.scalar_tensor_tensor
            r, k, v = rkv[:, 0, :], rkv[:, 1, :], rkv[:, 2, :]
            rw_dve.wait_iterations(dve, j)
            pre_dve.wait(dve, "km", j)
            pre_act.wait(dve, "Pp", j)

            def blocks(x):
                return x.rearrange("p (b t) -> p b t", b=TT)

            def chunks(x):
                return x[:, :].rearrange("p (c t) -> p c t", t=CHUNK)

            ends = dec[:, CHUNK - 1:T:CHUNK].unsqueeze(2).broadcast_to([P, T // CHUNK, CHUNK])
            done(stt(out=ar[:, :, 0, :], in0=blocks(kk[:, :]), scalar=-1.0, in1=blocks(sg[:, :]), op0=ALU.mult,
                     op1=ALU.mult), "A")
            done(tt(ar[:, :, 1, :], blocks(rkv[:, 0, :]), blocks(dec[:, :]), ALU.mult), "R")
            done(tt(bt[:, :], kb[:, :], dec_inv[:, :], ALU.mult), "Bt")
            done(tt(ktl[:, :], k, dec_inv[:, :], ALU.mult), "Kt")
            after("Bt")
            done(tt(chunks(bhc), chunks(bt), ends, ALU.mult), "Bh")
            after("Kt")
            done(tt(chunks(khc), chunks(ktl), ends, ALU.mult), "Kh")
            after("R")
            done(stt(out=r, in0=r, scalar=vec("r_k"), in1=k, op0=ALU.mult, op1=ALU.mult), "z")
            done(nc.vector.tensor_copy(pc[:, 0:T // CHUNK], dec[:, CHUNK - 1:T:CHUNK]), "pc")
            after()

            def norm(h):
                rw_act.wait(dve, f"rs{h}", j)
                part = y_rs[:, 4 * h:4 * h + 4, :]
                done(nc.vector.reciprocal(part, part), f"rsr{h}")
                after()
                for b in range(4 * h, 4 * h + 4):
                    for hh in range(2):
                        done(nc.vector.tensor_scalar(yb[:, b, hh, :], yb[:, b, hh, :], y_mv[:, b, hh, 0:1],
                                                     y_rs[:, b, hh:hh + 1], ALU.subtract, ALU.mult), f"ln{b}{hh}")

            def gate(h):
                rw_act.wait(dve, f"tY{h}", j)
                rw_pe.wait(dve, f"gate{h}", j)
                part = slice(h * HALF, (h + 1) * HALF)
                done(tt(y_mix[:, part], ps[:, bank_of[f"gate{h}"], :], y_mix[:, part], ALU.mult), f"gate{h}")

            for g in range(2):
                if g:
                    rw_pe.wait(dve, f"Y{g - 1}", j)
                for name in score_names(g):
                    hh = int(name[3])
                    rw_pe.wait(dve, name, j)
                    if name[:2] == "SN":
                        bank = ps[:, bank_of[name], :].rearrange("p (b c) -> p b c", b=4)
                        done(tt(mm_n[:, 0, hh, :, :], bank, strict_t[:, :].unsqueeze(1).broadcast_to([P, 4, P]),
                                ALU.mult), name)
                        continue
                    q = int(name[4])
                    strict_to, full_to = (mm_m[:, 0], mm_rb) if name[:2] == "SB" else (mm_ak, mm_rk)
                    bank = ps[:, bank_of[name], :].rearrange("p (b k c) -> p b k c", b=2, k=2)
                    for which, to, suffix in ((0, strict_to, "m"), (1, full_to, "r")):
                        done(tt(to[:, hh, 2 * q:2 * q + 2, :], bank[:, :, which, :],
                                causal2[:, which, :].unsqueeze(1).broadcast_to([P, 2, P]), ALU.mult), name + suffix)
                for hh in range(2):
                    name = f"AV{g}{hh}"
                    rw_pe.wait(dve, name, j)
                    bank = ps[:, bank_of[name], :].rearrange("p (b k c) -> p b k c", b=4, k=2)
                    done(nc.vector.tensor_copy(mm_x[:, :, 1, hh, :], bank[:, :, hh, :]), name)
                if g:
                    norm(0)
                rw_act.wait(dve, f"tA{g}", j)
                for l in range(LEVELS):
                    for hh in range(2):
                        name = f"X{g}{l}{hh}"
                        rw_pe.wait(dve, name, j)
                        after(f"AV{g}{hh}" if l == 0 else f"X{g}{l - 1}{hh}")
                        x = mm_x[:, :, :, hh, :]
                        bank = ps[:, bank_of[name], :].rearrange("p (b k c) -> p b k c", b=4, k=2)
                        done(tt(x, bank, x, ALU.add), name)
                        if l < LEVELS - 2:
                            name = f"N{g}{l}{hh}"
                            rw_pe.wait(dve, name, j)
                            done(nc.vector.tensor_copy(mm_n[:, (l + 1) % 2, hh, :, :], ps[:, bank_of[name], :]), name)
                    if g and not final:
                        for what in (("sum",), ("clamp",), ("norm0",), ("norm1",), ("kk",), ("km",))[l]:
                            prepare_dve(dve, j + 1, what)
                if g:
                    gate(0)
                rw_pe.wait(dve, f"G{g}", j)
                done(tt(mm_g[:, :, :], ps[:, bank_of[f"G{g}"], :].rearrange("p (b c) -> p b c", b=4),
                        ar[:, 4 * g:4 * g + 4, 1, :], ALU.add), f"G{g}")
                blocked = headones[:, :].unsqueeze(1).broadcast_to([P, 4, P])
                for q in range(NCH):
                    name = f"Phi{g}{q}"
                    rw_pe.wait(dve, name, j)
                    done(tt(mm_phi[:, q:NHALF:NCH, :], ps[:, bank_of[name], :].rearrange("p (b c) -> p b c", b=4),
                            blocked, ALU.mult), name)
                after()
                for c in range(NHALF):
                    done(stt(out=mm_phi[:, c, :], in0=ident[:, :], scalar=pc[:, NHALF * g + c:NHALF * g + c + 1],
                             in1=mm_phi[:, c, :], op0=ALU.mult, op1=ALU.add), f"PhiD{g}{c}")
                if g == 0:
                    rw_act.wait(dve, "bonus", j)
                    done(nc.vector.memset(states[:, 0, :], 0.0), "zero")
                for q in range(NCH):
                    name = f"Psi{g}{q}"
                    rw_pe.wait(dve, name, j)
                    done(tt(mm_psi[:, q:NHALF:NCH, :], ps[:, bank_of[name], :].rearrange("p (b c) -> p b c", b=4),
                            blocked, ALU.mult), name)
                after()
                for c in range(NHALF):
                    name = f"S{g}{c}"
                    rw_pe.wait(dve, name, j)
                    done(tt(states[:, NHALF * g + c + 1, :], ps[:, bank_of[name], 0:P], mm_psi[:, c, :], ALU.add),
                         name)
                rw_pe.wait(dve, f"Y{g}", j)
                for i in range(4):
                    for hh in range(2):
                        b = 4 * g + i
                        done(stt(out=yb[:, b, hh, :], in0=v_t[:, b, 64 * hh:64 * hh + 64],
                                 scalar=bonus[:, b, hh:hh + 1],
                                 in1=ps[:, bank_of[f"Y{g}"], i * P + 64 * hh:i * P + 64 * hh + 64],
                                 op0=ALU.mult, op1=ALU.add), f"Y{g}{i}{hh}")
                each = [(b, hh) for b in range(4 * g, 4 * g + 4) for hh in range(2)]
                after()
                for b, hh in each:
                    done(nc.vector.bn_stats(y_stats[:, b, hh, :], yb[:, b, hh, :]), f"bn{b}{hh}")
                after()
                apart(dve)
                for b, hh in each:
                    done(nc.vector.bn_aggr(y_mv[:, b, hh, :], y_stats[:, b, hh, :]), f"ag{b}{hh}")
            norm(1)
            gate(1)

        def rwkv_pool(pool):
            with pool.Fori(0, RWKV_TILES) as j:
                rw_act.wait(pool, "hi", j)
                rw_pool.done(nc.gpsimd.tensor_tensor(
                    xl[:, bass.ds(j, 1), :].rearrange("p a n -> p (a n)"), y_mix[:, :],
                    xh[:, bass.ds(j, 1), :].bitcast(F32).rearrange("p a n -> p (a n)"), ALU.subtract), "lo")

        lam_loaded = sem("lam_loaded")
        lam_dve = sem("lam_dve")
        lam_act = sem("lam_act")
        lam_pe = sem("lam_pe")
        class Attention:
            def __init__(self, kind):
                self.kind = kind
                self.diff = kind == "diff"
                self.order = list(range(TT))[::-1] if kind == "fox" else list(range(TT))
                self.maps = 1 if self.diff else 2
                order = self.order
                pe, act, dve = ["tv0", "tv1"], ["vt0", "vt1"], []

                def scores(n):
                    if n < TT:
                        pe.extend(f"s{order[n]}{m}" for m in range(2))

                def maxima(n):
                    if n < TT:
                        for m in range(2):
                            if kind == "fox":
                                dve.append(f"dm{order[n]}{m}")
                            dve.append(f"mx{order[n]}{m}")

                def exps(n):
                    if n < TT:
                        act.extend(f"ex{order[n]}{m}" for m in range(2))

                def outputs(n):
                    if n >= 0:
                        if not self.diff:
                            dve.append(f"rl{order[n]}")
                        dve.extend(f"o{order[n]}{m}" for m in range(self.maps))

                scores(0)
                scores(1)
                maxima(0)
                maxima(1)
                exps(0)
                exps(1)
                for n, i in enumerate(order):
                    scores(n + 2)
                    if self.diff:
                        dve += [f"rl{i}", f"w{i}", f"pa{i}", f"pb{i}"]
                    maxima(n + 2)
                    for m in range(self.maps):
                        for g in self.groups(i):
                            pe.append(f"t{i}{m}{g}")
                            (act if self.copier(m, g) == "act" else dve).append(f"pt{i}{m}{g}")
                    exps(n + 2)
                    pe += [f"o{i}{m}" for m in range(self.maps)]
                    outputs(n - 1)
                    if self.diff and n:
                        act.append(f"sq{order[n - 1]}")
                outputs(TT - 1)
                if self.diff:
                    act += [f"sq{order[-1]}", "root"]
                    dve += ["rr"] + [f"on{i}" for i in range(TT)]
                pe += ["to0", "to1"]
                act += ["ot0", "ot1", "hi"]
                self.pe = Steps(sem(f"{kind}_pe"), pe)
                self.act = Steps(sem(f"{kind}_act"), act)
                self.dve = Steps(sem(f"{kind}_dve"), dve)
                self.pool = Steps(sem(f"{kind}_pool"), ["lo"])
                self.split_act = Steps(sem(f"{kind}_split_act"), ["qh0", "kh0", "qh1", "kh1"])
                self.split_dve = Steps(sem(f"{kind}_split_dve"), {"diff": ["slope"], "fox": [], "band": [
                    "edge0", "edge1", "edge2", "edge3"]}[kind] + ["ql0", "kl0", "ql1", "kl1"])
                self.loaded = sem(f"{kind}_loaded")
                self.bias_loaded = sem(f"{kind}_bias_loaded")
                self.turn, self.before = {}, {}
                uses = []
                for i in order:
                    for m in range(self.maps):
                        for g in self.groups(i):
                            self.turn[i, m, g] = len(uses) % 2
                            self.before[i, m, g] = uses[-2:-1] if len(uses) >= 2 else []
                            uses.append((i, m, g))
                self.last_uses = uses[-2:]

            def blocks(self, i):
                return range(max(0, i - 4) if self.kind == "band" else 0, i + 1)

            def groups(self, i):
                return range((len(self.blocks(i)) + 3) // 4)

            def copier(self, m, g):
                return "act" if (g if self.diff else m) == 0 else "dve"

            def copied(self, eng, uses, j, act=(), dve=()):
                self.act.wait_last(eng, [*act, *(f"pt{i}{m}{g}" for i, m, g in uses if self.copier(m, g) == "act")], j)
                self.dve.wait_last(eng, [*dve, *(f"pt{i}{m}{g}" for i, m, g in uses if self.copier(m, g) == "dve")], j)

            def bias_of(self, i, m):
                n = P * len(self.blocks(i))
                if self.diff:
                    return bias[:, 0, T - n:T]
                if self.kind == "fox":
                    return bias[:, m, 0:n]
                first = (4 - i) * P if i < 4 else 0
                return bias[:, m, first:first + n]

            def multiplied(self, eng, n, m, j):
                if n >= 2:
                    self.pe.wait(eng, f"o{self.order[n - 2]}{m}", j)
                else:
                    self.pe.wait(eng, f"o{self.order[TT - 2 + n]}{m}", j - 1)

        def attention_pe(pe, at_, j):
            mm = nc.tensor.matmul
            order, last = at_.order, at_.order[-1]
            pe.wait_ge(at_.loaded, 9 * 16 * (j + 1))
            at_.act.wait(pe, "ot1", j - 1)
            for h in range(2):
                for b in range(4):
                    ins = nc.tensor.transpose(ps[:, 4 + h, b * P:(b + 1) * P],
                                              vraw[:, (4 * h + b) * P:(4 * h + b + 1) * P], ident[:, :])
                at_.pe.done(ins, f"tv{h}")
            at_.split_dve.wait(pe, "kl1", j)

            def scores(n):
                if n >= TT:
                    return
                i = order[n]
                keys = at_.blocks(i)
                size = P * len(keys)
                for m in range(2):
                    if n:
                        at_.dve.wait(pe, f"mx{order[n - 1]}{m}", j)
                    else:
                        at_.dve.wait(pe, f"mx{last}{m}", j - 1)
                    for lo in range(0, size, HALF):
                        hi = min(size, lo + HALF)
                        k0 = keys[0] * P
                        for part, k in enumerate((kh, kl)):
                            ins = mm(ps[:, 2 * m + lo // HALF, 0:hi - lo], qs[:, m, i * P:(i + 1) * P],
                                     k[:, m, k0 + lo:k0 + hi], start=(part == 0), stop=(part == 1))
                    at_.pe.done(ins, f"s{i}{m}")

            scores(0)
            scores(1)
            for n, i in enumerate(order):
                scores(n + 2)
                for m in range(at_.maps):
                    for g in at_.groups(i):
                        at_.copied(pe, at_.before[i, m, g], j, act=["vt1"] + ([] if at_.diff else [f"ex{i}{m}"]),
                                   dve=[f"pb{i}"] if at_.diff else [])
                        bank = 4 + at_.turn[i, m, g]
                        for k in range(4 * g, min(4 * g + 4, len(at_.blocks(i)))):
                            ins = nc.tensor.transpose(ps[:, bank, (k - 4 * g) * P:(k - 4 * g + 1) * P],
                                                      pm[:, n % 2, m, k * P:(k + 1) * P], ident[:, :])
                        at_.pe.done(ins, f"t{i}{m}{g}")
                if n < 2:
                    at_.dve.wait(pe, f"o{order[TT - 2 + n]}{at_.maps - 1}", j - 1)
                for m in range(at_.maps):
                    keys = at_.blocks(i)
                    at_.copied(pe, [(i, m, g) for g in at_.groups(i)], j,
                               dve=[f"o{order[n - 2]}{at_.maps - 1}"] if n >= 2 else [])
                    for k, b in enumerate(keys):
                        ins = mm(ps[:, 6 + n % 2, m * P:(m + 1) * P], pt[n % 2][:, m, k * P:(k + 1) * P],
                                 vt[:, b, :], start=(k == 0), stop=(k == len(keys) - 1))
                    at_.pe.done(ins, f"o{i}{m}")
            at_.copied(pe, at_.last_uses, j, dve=[f"on{TT - 1}" if at_.diff else f"o{last}1"])
            for h in range(2):
                for b in range(4):
                    ins = nc.tensor.transpose(ps[:, 4 + h, b * P:(b + 1) * P], osb[:, 4 * h + b, :], ident[:, :])
                at_.pe.done(ins, f"to{h}")

        def attention_split_act(act, at_, j):
            fn = nc.scalar.activation
            act.wait_ge(at_.loaded, 9 * 16 * (j + 1))
            at_.pe.wait(act, f"s{at_.order[-1]}1", j - 1)
            for m in range(2):
                at_.split_act.done(fn(qs[:, m, :], qraw[:, m, :], ACT.Copy, scale=0.125), f"qh{m}")
                at_.split_act.done(fn(kh[:, m, :], kraw[:, m, :], ACT.Copy), f"kh{m}")

        def attention_split_dve(dve, at_, j):
            def done(ins, name):
                at_.split_dve.done(ins, name)

            at_.dve.wait(dve, f"mx{at_.order[-1]}1", j - 1)
            if at_.diff:
                done(nc.vector.tensor_scalar(bias[:, 0, :], bias[:, 0, :], 0.25, None, ALU.mult), "slope")
            if at_.kind == "band":
                dve.wait_ge(at_.bias_loaded, 2 * 16 * (j + 1))
                for m in range(2):
                    done(nc.vector.memset(bias[0:64, m, 576:640], NEG), f"edge{2 * m}")
                    done(nc.vector.memset(bias[64:128, m, 0:64], NEG), f"edge{2 * m + 1}")
            for m in range(2):
                at_.split_act.wait(dve, f"qh{m}", j)
                done(nc.vector.scalar_tensor_tensor(out=qs[64:128, m, :], in0=qraw[64:128, m, :], scalar=0.125,
                                                    in1=qs[64:128, m, :].bitcast(F32), op0=ALU.mult,
                                                    op1=ALU.subtract), f"ql{m}")
                at_.split_act.wait(dve, f"kh{m}", j)
                done(nc.vector.tensor_tensor(kl[:, m, :], kraw[:, m, :], kh[:, m, :].bitcast(F32), ALU.subtract),
                     f"kl{m}")

        def attention_act(act, at_, j, to, final=False):
            fn = nc.scalar.activation
            order = at_.order
            for h in range(2):
                at_.pe.wait(act, f"tv{h}", j)
                at_.act.done(fn(vt[:, 4 * h:4 * h + 4, :], ps[:, 4 + h, :], ACT.Copy), f"vt{h}")

            def exps(n):
                if n >= TT:
                    return
                i = order[n]
                size = P * len(at_.blocks(i))
                for m in range(2):
                    at_.dve.wait(act, f"mx{i}{m}", j)
                    if n >= 2:
                        old = order[n - 2]
                        at_.pe.wait(act, f"t{old}{at_.maps - 1}{len(at_.groups(old)) - 1}", j)
                    at_.act.done(fn(pm[:, n % 2, m, 0:size], ssb[:, n % 2, m, 0:size], ACT.Exp, scale=-1.0,
                                    bias=negmax[:, i, m:m + 1], accum_out=rowsum[:, i, m:m + 1]), f"ex{i}{m}")

            def square(i):
                at_.dve.wait(act, f"o{i}0", j)
                at_.act.done(fn(ot[:, i * P:(i + 1) * P], osb[:, i, :], ACT.Square, accum_out=osq[:, i:i + 1]),
                             f"sq{i}")

            exps(0)
            exps(1)
            for n, i in enumerate(order):
                for m in range(at_.maps):
                    for g in at_.groups(i):
                        if at_.copier(m, g) == "act":
                            size = P * min(4, len(at_.blocks(i)) - 4 * g)
                            at_.pe.wait(act, f"t{i}{m}{g}", j)
                            at_.act.done(fn(pt[n % 2][:, m, g * HALF:g * HALF + size],
                                            ps[:, 4 + at_.turn[i, m, g], 0:size], ACT.Copy), f"pt{i}{m}{g}")
                exps(n + 2)
                if n == 1:
                    at_.pool.wait_iterations(act, j)
                if at_.diff and n:
                    square(order[n - 1])
                if n == TT - 2 and not final:
                    attention_split_act(act, at_, j + 1)
            if at_.diff:
                square(order[-1])
                at_.act.wait(act, f"sq{TT - 1}", j)
                at_.act.done(fn(osq[:, :], osq[:, :], ACT.Sqrt, bias=small[:, 3:4], scale=1.0 / P), "root")
            for h in range(2):
                at_.pe.wait(act, f"to{h}", j)
                part = slice(h * HALF, (h + 1) * HALF)
                if at_.diff:
                    at_.act.done(fn(ot[:, part], ps[:, 4 + h, :], ACT.Copy, scale=small[:, 4:5]), f"ot{h}")
                else:
                    at_.act.done(fn(ot[:, part], ps[:, 4 + h, :], ACT.Copy), f"ot{h}")
            at_.act.wait(act, "ot1", j)
            apart(act)
            at_.act.done(fn(xh[:, bass.ds(to + j, 1), :].rearrange("p a n -> p (a n)"), ot[:, :], ACT.Copy), "hi")

        def attention_dve(dve, at_, j, final=False):
            tt, stt = nc.vector.tensor_tensor, nc.vector.scalar_tensor_tensor
            order = at_.order

            def done(ins, name):
                at_.dve.done(ins, name)

            at_.dve.wait_iterations(dve, j)
            at_.split_dve.wait(dve, "kl1", j)
            if at_.kind == "fox":
                dve.wait_ge(at_.bias_loaded, 2 * 16 * (j + 1))
            at_.act.wait(dve, f"ex{order[-1]}1", j - 1)

            def maxima(n):
                if n >= TT:
                    return
                i = order[n]
                size = P * len(at_.blocks(i))
                for m in range(2):
                    if at_.kind == "fox":
                        part = bias[:, m, i * P:(i + 1) * P]
                        done(tt(part, part, tri[:, :], ALU.add), f"dm{i}{m}")
                        at_.dve.wait(dve, f"dm{i}{m}", j)
                    at_.pe.wait(dve, f"s{i}{m}", j)
                    if n >= 2:
                        at_.act.wait(dve, f"ex{order[n - 2]}{m}", j)
                    apart(dve)
                    done(nc.vector.tensor_tensor_reduce(
                        ssb[:, n % 2, m, 0:size], ps[:, 2 * m:2 * m + 2, :].rearrange("p a n -> p (a n)")[:, 0:size],
                        at_.bias_of(i, m), -1.0, 3e38, ALU.add, ALU.min, negmax[:, i, m:m + 1]), f"mx{i}{m}")

            def outputs(n):
                if n < 0:
                    return
                i = order[n]
                if not at_.diff:
                    at_.act.wait(dve, f"ex{i}1", j)
                    done(nc.vector.reciprocal(rowsum[:, i, :], rowsum[:, i, :]), f"rl{i}")
                    at_.dve.wait(dve, f"rl{i}", j)
                if n == 0:
                    at_.pe.wait(dve, "to1", j - 1)
                at_.pe.wait(dve, f"o{i}{at_.maps - 1}", j)
                for m in range(at_.maps):
                    if at_.diff:
                        done(nc.vector.tensor_copy(osb[:, i, :], ps[:, 6 + n % 2, 0:P]), f"o{i}0")
                    else:
                        done(nc.vector.tensor_scalar(osb[:, i, 64 * m:64 * m + 64],
                                                     ps[:, 6 + n % 2, (P + 64) * m:(P + 64) * m + 64],
                                                     rowsum[:, i, m:m + 1],
                                                     None, ALU.mult), f"o{i}{m}")

            maxima(0)
            maxima(1)
            for n, i in enumerate(order):
                size = P * len(at_.blocks(i))
                if at_.diff:
                    at_.act.wait(dve, f"ex{i}1", j)
                    done(nc.vector.reciprocal(rowsum[:, i, :], rowsum[:, i, :]), f"rl{i}")
                    at_.dve.wait(dve, f"rl{i}", j)
                    done(tt(weight[:, i, 0:1], rowsum[:, i, 1:2], small[:, 2:3], ALU.mult), f"w{i}")
                    done(nc.vector.tensor_scalar(pm[:, n % 2, 0, 0:size], pm[:, n % 2, 0, 0:size],
                                                 rowsum[:, i, 0:1], None, ALU.mult), f"pa{i}")
                    at_.dve.wait(dve, f"pa{i}", j)
                    done(stt(out=pm[:, n % 2, 0, 0:size], in0=pm[:, n % 2, 1, 0:size], scalar=weight[:, i, 0:1],
                             in1=pm[:, n % 2, 0, 0:size], op0=ALU.mult, op1=ALU.add), f"pb{i}")
                maxima(n + 2)
                for m in range(at_.maps):
                    for g in at_.groups(i):
                        if at_.copier(m, g) == "dve":
                            part = P * min(4, len(at_.blocks(i)) - 4 * g)
                            at_.pe.wait(dve, f"t{i}{m}{g}", j)
                            done(nc.vector.tensor_copy(pt[n % 2][:, m, g * HALF:g * HALF + part],
                                                       ps[:, 4 + at_.turn[i, m, g], 0:part]), f"pt{i}{m}{g}")
                outputs(n - 1)
                if n == TT - 2 and not final:
                    attention_split_dve(dve, at_, j + 1)
            outputs(TT - 1)
            if at_.diff:
                at_.act.wait(dve, "root", j)
                done(nc.vector.reciprocal(osq[:, :], osq[:, :]), "rr")
                at_.dve.wait(dve, "rr", j)
                for i in range(TT):
                    done(nc.vector.tensor_scalar(osb[:, i, :], osb[:, i, :], osq[:, i:i + 1], None, ALU.mult),
                         f"on{i}")

        def attention_pool(pool, at_, to):
            with pool.Fori(0, 4) as j:
                at_.act.wait(pool, "hi", j)
                at_.pool.done(nc.gpsimd.tensor_tensor(
                    xl[:, bass.ds(to + j, 1), :].rearrange("p a n -> p (a n)"), ot[:, :],
                    xh[:, bass.ds(to + j, 1), :].bitcast(F32).rearrange("p a n -> p (a n)"), ALU.subtract), "lo")

        def attention_loads(sp, at_, source, tiles, bias_loads=None, before=None):
            def load(j, of, last):
                of.split_act.wait(sp, "kh1", last)
                apart(sp)
                of.split_dve.wait(sp, "kl1", last)
                apart(sp)
                of.pe.wait(sp, "tv1", last)
                apart(sp)
                for to, tile0 in ((qraw, tiles[0]), (kraw, tiles[1])):
                    for m in range(2):
                        from_ = source[bass.ds(tile0 + j, 1), 64 * m:64 * m + 64, :].rearrange("a p n -> (a p) n")
                        for half in range(2):
                            sp.dma_start(to[64 * half:64 * half + 64, m, :], from_).then_inc(at_.loaded, 16)
                sp.dma_start(vraw[:, :], source[bass.ds(tiles[2] + j, 1)].rearrange("a p n -> (a p) n"))\
                    .then_inc(at_.loaded, 16)
                if bias_loads is not None:
                    of.dve.wait(sp, f"mx{of.order[-1]}1", last)
                    apart(sp)
                    for m in range(2):
                        bias_loads(j, m).then_inc(at_.bias_loaded, 16)

            if before is None:
                load(0, at_, -1)
            else:
                load(0, before, 3)
            with sp.Fori(1, 4) as j:
                load(j, at_, j - 1)

        def last_outputs(pe, at_, kt):
            if kt >= 4:
                at_.pool.wait_iterations(pe, kt - 3)

        def attention_loop(eng, body, split, at_, *args):
            if split:
                split(eng, at_, 0)
            with eng.Fori(0, 3) as j:
                body(eng, at_, j, *args)
            body(eng, at_, 3, *args, final=True)

        diff, fox, band = Attention("diff"), Attention("fox"), Attention("band")
        h_loaded = [sem(f"h_loaded{s}") for s in range(2)]
        scaled = sem("scaled")
        added = sem("added")
        d_loaded = sem("d_loaded")
        d_hi = sem("d_hi")
        d_lo = sem("d_lo")
        down_done = sem("down_done")
        down_added = sem("down_added")
        y_zero = sem("y_zero")
        fa_act = sem("fa_act")
        fa_dve = sem("fa_dve")
        fa_loaded = sem("fa_loaded")
        fa_set = sem("fa_set")
        ub_pads = sem("ub_pads")
        fa_stored = sem("fa_stored")
        rel_loaded = sem("rel_loaded")
        rel_filled = sem("rel_filled")
        rel_stored = sem("rel_stored")
        gate_loaded = [sem(f"gate_loaded{s}") for s in range(2)]
        gate_done = sem("gate_done")
        gated_a = sem("gated_a")
        gated_b = sem("gated_b")
        merged_done = sem("merged_done")
        m_hi = sem("m_hi")
        m_lo = sem("m_lo")
        h2_loaded = [sem(f"h2_loaded{s}") for s in range(2)]
        y_loaded = sem("y_loaded")
        squared = sem("squared")
        out_sum = sem("out_sum")
        out_root = sem("out_root")
        gained = sem("gained")
        out_turned = sem("out_turned")
        out_ready = sem("out_ready")
        out_stored = [sem(f"out_stored{s}") for s in range(2)]

        def post_scale(dve, kt, gain):
            nc.vector.scalar_tensor_tensor(out=y[:, kt, :], in0=y[:, kt, :], scalar=col(gain, kt), in1=rstd[:, :],
                                           op0=ALU.mult, op1=ALU.mult).then_inc(scaled, 1)

        def post_norm(dve, post_gain, r0, q0, pre_gain):
            post_scale(dve, 0, post_gain)
            for kt in range(KT):
                if kt + 1 < KT:
                    post_scale(dve, kt + 1, post_gain)
                prep_dve(dve, r0 + kt, q0 + kt, pre_gain)

        def post_norm_pool(pool, k, r0, q0):
            for kt in range(KT):
                s = kt % 2
                pool.wait_ge(scaled, KT * k + kt + 1)
                pool.wait_ge(h_loaded[s], 16 * (4 * k + kt // 2 + 1))
                pool.wait_ge(x_lo, r0 + kt - 1)
                pool.wait_ge(x_sq, q0 + kt - 1)
                pool.wait_ge(src_stored[s], 16 * ((r0 + kt) // 2))
                nc.gpsimd.tensor_tensor(src[:, s, :], y[:, kt, :], hres[:, s, :], ALU.add).then_inc(added, 1)

        def post_norm_act(act, k, r0, q0, pre_gain):
            for kt in range(KT):
                prep_act(act, r0 + kt, q0 + kt, pre_gain, (added, KT * k + kt + 1))
                act.dma_start(residual[kt], src[:, kt % 2, :]).then_inc(src_stored[kt % 2], 16)

        def post_norm_loads(sp, k):
            for s in range(2):
                sp.wait_ge(src_stored[s], 16 * 4 * (k + 1))
            for kt in range(KT):
                if kt >= 2:
                    sp.wait_ge(added, KT * k + kt - 1)
                sp.dma_start(hres[:, kt % 2, :], residual[kt]).then_inc(h_loaded[kt % 2], 16)

        def load_down(sp, c, d, w):
            sp.wait_ge(d_lo, d + 1)
            sp.dma_start(draw[:, :, :], w[bass.ds(c * 2 * P, 2 * P), :].rearrange("(k p) n -> p k n", p=P))\
                .then_inc(d_loaded, 16)

        def split_down_hi(act, d):
            act.wait_ge(d_loaded, 16 * d + 16)
            act.wait_ge(down_done, KT * d + 1)
            nc.scalar.activation(dh[:, :, :], draw[:, :, :], ACT.Copy).then_inc(d_hi, 1)

        def split_down_lo(pool, d):
            pool.wait_ge(d_hi, d + 1)
            nc.gpsimd.tensor_tensor(dl[:, :, :], draw[:, :, :], dh[:, :, :].bitcast(F32), ALU.subtract)\
                .then_inc(d_lo, 1)

        def down_products(pe, steps, c, d, par):
            pe.wait_ge(d_lo, d + 2)
            steps.wait(pe, "l1", c)
            for m in range(KT):
                if m != 1:
                    pe.wait_ge(down_added, KT * d + max(m - 1, 0) + 1)
                for kt in range(2):
                    mm = three_products(4 + 2 * (m % 2), dh[:, kt, m * P:(m + 1) * P], dl[:, kt, m * P:(m + 1) * P],
                                        fh[:, par, kt, :], fl[:, par, kt, :], kt == 0, kt == 1)
                mm.then_inc(down_done, 1)

        def down_add(dve, d, squares=None):
            for m in range(KT):
                dve.wait_ge(down_done, KT * d + m + 2)
                nc.vector.tensor_tensor(y[:, m, :], bank2(2 + m % 2), y[:, m, :], ALU.add).then_inc(down_added, 1)
                if squares is not None:
                    if m:
                        square_sum_dve(dve, squares + m - 1)
            if squares is not None:
                square_sum_dve(dve, squares + KT - 1)

        def y_squares_act(act, d, q0):
            for m in range(KT):
                act.wait_ge(down_added, KT * d + m + 2)
                square_act(act, q0 + m, y[:, m, :])

        ff1_act = Steps(sem("ff1_act"), [f"{x}{t}" for t in range(2) for x in ("cg", "cv", "ge", "h")])
        ff1_dve = Steps(sem("ff1_dve"), [f"{x}{t}" for t in range(2) for x in ("ag", "bg", "av", "bv", "m", "l")])
        ff2_act = Steps(sem("ff2_act"), [f"h{t}" for t in range(2)])
        ff2_dve = Steps(sem("ff2_dve"), [f"{x}{t}" for t in range(2) for x in ("u", "r", "l")])

        def ff1_dve_chunk(dve, c, par, d=None):
            for t in range(2):
                for r, x in enumerate("gv"):
                    k = 2 * t + r
                    n = U_UP + 4 * c + k
                    tile = 2 * c + t + FF_TILES * r
                    dve.wait_ge(mm_done, n + 1)
                    if t:
                        ff1_dve.wait(dve, f"b{x}0", c)
                        ff1_act.wait(dve, f"c{x}0", c)
                    else:
                        ff1_dve.wait_iterations(dve, c)
                        apart(dve)
                        ff1_act.wait_iterations(dve, c)
                    nc.vector.tensor_tensor(ub[:, r, 2:T + 2], bank2(r), rstd[:, :], ALU.mult).then_inc(evac_done, 1)
                    for back, name in ((1, "a"), (2, "b")):
                        if back == 1:
                            ff1_act.wait(dve, f"c{x}{t}", c)
                        else:
                            ff1_dve.wait(dve, f"a{x}{t}", c)
                        ff1_dve.done(nc.vector.scalar_tensor_tensor(
                            out=cb[:, r, :], in0=ub[:, r, 2 - back:T + 2 - back],
                            scalar=col_at("conv_w", (2 - back) * 2 * FF_TILES + tile), in1=cb[:, r, :],
                            op0=ALU.mult, op1=ALU.add), f"{name}{x}{t}")
                if t == 0 and d is not None:
                    down_add(dve, d)
                ff1_dve.wait(dve, f"bv{t}", c)
                ff1_act.wait(dve, f"ge{t}", c)
                ff1_dve.done(nc.vector.tensor_tensor(cb[:, 1, :], cb[:, 0, :], cb[:, 1, :], ALU.mult), f"m{t}")
                ff1_act.wait(dve, f"h{t}", c)
                ff1_dve.done(nc.vector.tensor_tensor(fl[:, par, t, :], cb[:, 1, :],
                                                     fh[:, par, t, :].bitcast(F32), ALU.subtract), f"l{t}")

        def ff1_act_chunk(act, c, par):
            for t in range(2):
                if t:
                    split_down_hi(act, c)
                for r, x in enumerate("gv"):
                    k = 2 * t + r
                    n = U_UP + 4 * c + k
                    tile = 2 * c + t + FF_TILES * r
                    split_hi(act, n + 2, r)
                    act.wait_ge(evac_done, n + 1)
                    if t:
                        ff1_dve.wait(act, "l0", c)
                    else:
                        ff1_dve.wait_iterations(act, c)
                    apart(act)
                    ff1_act.done(nc.scalar.activation(cb[:, r, :], ub[:, r, 2:T + 2], ACT.Identity,
                                                      scale=col_at("conv_w", 2 * 2 * FF_TILES + tile),
                                                      bias=col_at("conv_b", tile)), f"c{x}{t}")
                ff1_dve.wait(act, f"bg{t}", c)
                ff1_act.done(nc.scalar.activation(cb[:, 0, :], cb[:, 0, :], ACT.Gelu_apprx_tanh), f"ge{t}")
                ff1_dve.wait(act, f"m{t}", c)
                if not isinstance(c, int) or c >= 1:
                    act.wait_ge(down_done, KT * (c - 1) + 1)
                ff1_act.done(nc.scalar.activation(fh[:, par, t, :], cb[:, 1, :], ACT.Copy), f"h{t}")

        def ff2_dve_chunk(dve, c, par, d=None):
            for t in range(2):
                n = U_UP2 + 2 * c + t
                dve.wait_ge(mm_done, n + 1)
                apart(dve)
                if t:
                    ff2_dve.wait(dve, "l0", c)
                else:
                    ff2_dve.wait_iterations(dve, c)
                nc.vector.tensor_tensor(cb[:, 0, :], bank2((U_UP2 + t) % 2), rstd[:, :], ALU.mult)\
                    .then_inc(evac_done, 1)
                dve.wait_ge(evac_done, n + 1)
                ff2_dve.done(nc.vector.tensor_scalar(cb[:, 1, :], cb[:, 0, :], 0.0, None, ALU.max), f"u{t}")
                ff2_dve.wait(dve, f"u{t}", c)
                ff2_dve.done(nc.vector.tensor_tensor(cb[:, 0, :], cb[:, 1, :], cb[:, 1, :], ALU.mult), f"r{t}")
                if t == 0 and d is not None:
                    down_add(dve, d)
                ff2_act.wait(dve, f"h{t}", c)
                ff2_dve.wait(dve, f"r{t}", c)
                ff2_dve.done(nc.vector.tensor_tensor(fl[:, par, t, :], cb[:, 0, :],
                                                     fh[:, par, t, :].bitcast(F32), ALU.subtract), f"l{t}")

        def ff2_act_chunk(act, c, par, last=False):
            for t in range(2):
                n = U_UP2 + 2 * c + t
                if t:
                    split_down_hi(act, DOWN1 + c)
                if not last:
                    split_hi(act, n + 2, (U_UP2 + t) % 2)
                ff2_dve.wait(act, f"r{t}", c)
                act.wait_ge(down_done, KT * (DOWN1 - 1 + c) + 1)
                ff2_act.done(nc.scalar.activation(fh[:, par, t, :], cb[:, 0, :], ACT.Copy), f"h{t}")


        @block.sync
        def _(sp):
            sp.dma_start(cols[:, :], a["vectors"]).then_inc(cols_ready, 16)
            for t in range(TT):
                sp.dma_start(xin[:, t, :], a["x"][t * P:(t + 1) * P, :]).then_inc(x_loaded[t % 2], 16)
            for s in range(2):
                load_w(sp, s, s, w_cols(a["w_in"], s * P), first=True)
            with sp.Fori(1, IN_TILES // 2) as i:
                for s in range(2):
                    load_w(sp, 2 * i + s, s, w_cols(a["w_in"], i * (2 * P) + s * P))
            for s in range(2):
                load_w(sp, U_OUT + s, s, w_cols(a["w_out"], s * P))
            for s in range(2):
                sp.wait_ge(stage_stored[s], 16 * (G_TILE // 2 + 1) + 1)
            sp.dma_start(wa[:, :], proj1[WA_TILE]).then_inc(lora_ready, 16)
            sp.dma_start(gl[:, :], proj1[G_TILE]).then_inc(lora_ready, 16)

            def rwkv_weights(j, last):
                if last is not None:
                    pre_pe.wait(sp, "i1", last)
                    apart(sp)
                sp.dma_start(lora_w[0:64, :], a["w_decay_up"][:, bass.ds(j * P, P)]).then_inc(lora_w_ready, 16)
                sp.dma_start(lora_w[64:128, :], a["w_iclr_up"][:, bass.ds(j * P, P)]).then_inc(lora_w_ready, 16)
                if last is not None:
                    rw_pe.wait(sp, "gate1", last)
                    apart(sp)
                sp.dma_start(gate_w[:, :], a["w_gate_up"][:, bass.ds(j * P, P)]).then_inc(gate_w_ready, 16)

            def rwkv_loads(j, last):
                if last is not None:
                    rw_dve.wait(sp, "z", last)
                    apart(sp)
                    rw_pe.wait(sp, "bonus", last)
                    apart(sp)
                for k in range(3):
                    sp.dma_start(rkv[:, k, :], proj1[bass.ds(RWKV_TILES * k + j, 1)].rearrange("a p n -> (a p) n"))\
                        .then_inc(rkv_ready, 16)

            rwkv_weights(0, None)
            for s in range(2):
                sp.wait_ge(stage_stored[s], 8 * IN_TILES + 1)
            sp.wait_ge(phase, 4)
            rwkv_loads(0, None)
            with sp.Fori(1, RWKV_TILES) as j:
                rwkv_loads(j, j - 1)
                rwkv_weights(j, j - 1)
            sp.wait_ge(phase, 8)
            sp.dma_start(lam_row[:, :], a["lambdas"].rearrange("(o a) b -> o (a b)", o=1)).then_inc(lam_loaded, 16)
            attention_loads(sp, diff, proj1, (14, 18, 22))
            for kt in range(2, KT):
                load_w(sp, U_OUT + kt, kt % 2, w_cols(a["w_out"], kt * P))
            for s in range(2):
                load_w(sp, U_UP + s, s, w_cols(a["w_up"], s * D_FF))
            sp.wait_ge(phase, 16)
            post_norm_loads(sp, 0)
            with sp.Fori(0, DOWN1 - 1) as c:
                load_down(sp, c, c, a["w_down"])
                for k in range(2, 6):
                    load_w(sp, U_UP + 4 * c + k, k % 2,
                           w_cols(a["w_up"], c * (2 * P) + (k // 2 * P + k % 2 * D_FF)))
            c = DOWN1 - 1
            load_down(sp, c, c, a["w_down"])
            for k in range(2):
                load_w(sp, U_UP + 4 * c + 2 + k, k, w_cols(a["w_up"], (2 * c + 1) * P + k * D_FF))
            load_w(sp, U_FA, 0, w_cols(a["w_in_2"], FA_COL))
            load_w(sp, U_QKV2, 1, w_cols(a["w_in_2"], 0))
            sp.wait_ge(down_done, KT * DOWN1 + 1)
            post_norm_loads(sp, 1)
            sp.wait_ge(x_lo, 17)
            sp.dma_start(small[0:FOX_HEADS, 5:6], a["forget_bias"]).then_inc(fa_loaded, 16)
            sp.dma_start(rel[:, REL - N_REL + 1:REL], a["rel_bias"][:, 0:N_REL - 1]).then_inc(rel_loaded, 16)
            for u in range(1, 12):
                load_w(sp, U_QKV2 + u, (U_QKV2 + u) % 2, w_cols(a["w_in_2"], u * P))
            with sp.Fori(0, 14) as i:
                for k in range(2):
                    load_w(sp, U_QKV2 + 12 + 2 * i + k, (U_QKV2 + k) % 2,
                           w_cols(a["w_in_2"], i * (2 * P) + (Q2_COL + k * P)))
            sp.wait_ge(rel_filled, 1)
            sp.dma_start(rel_d, rel[:, :].rearrange("h (o n) -> h o n", o=1).to_broadcast([FOX_HEADS, P, REL]))\
                .then_inc(rel_stored, 16)
            sp.wait_ge(fa_dve, 4)
            sp.dma_start(cneg_d, cneg[:, :]).then_inc(fa_stored, 16)
            for s in range(2):
                load_w(sp, U_BRANCH + s, (U_BRANCH + s) % 2, w_cols(a["w_branch"], s * P))
            for k in range(2):
                sp.wait_ge(stage_stored[k], 16 * (IN_TILES // 2 + 12) + 1)
            sp.wait_ge(fa_stored, 16)
            sp.wait_ge(x_lo, 24)

            def fox_bias(j, m):
                row = cneg_d[bass.ds(2 * j + m, 1), :]
                return sp.dma_start(bias[:, m, :], bass.AP(tensor=row.tensor, offset=row.offset, ap=[[0, P], [1, T]]))

            def band_bias(j, m):
                rows = rel_d[bass.ds(2 * j + m, 1)]
                return sp.dma_start(bias[:, m, 0:BAND], bass.AP(tensor=rows.tensor, offset=rows.offset + (P - 1),
                                                                ap=[[REL - 1, P], [1, BAND]]))

            attention_loads(sp, fox, proj2, (0, 4, 8), fox_bias)
            for k in range(2):
                sp.wait_ge(stage_stored[k], 16 * (IN_TILES // 2 + 20) + 1)
            sp.wait_ge(rel_stored, 16)
            attention_loads(sp, band, proj2, (12, 16, 20), band_bias, before=fox)
            sp.wait_ge(phase, 28)
            for m in range(KT):
                if m >= 2:
                    sp.wait_ge(gated_b, m - 1)
                for b in range(2):
                    sp.dma_start(gates[:, m % 2, b, :], proj2[24 + 8 * b + m]).then_inc(gate_loaded[m % 2], 16)
                n = U_BRANCH + m + 2
                w = a["w_branch"] if m + 2 < KT else a["w_out_2"]
                load_w(sp, n, n % 2, w_cols(w, (m + 2) % KT * P))
            for kt in range(KT):
                if kt >= 2:
                    sp.wait_ge(evac_done, U_OUT2 + kt - 1)
                if kt == 0:
                    for s in range(2):
                        sp.wait_ge(src_stored[s], 16 * 12)
                sp.dma_start(hres2[:, kt % 2, :], residual[kt]).then_inc(h2_loaded[kt % 2], 16)
                n = U_OUT2 + kt + 2
                if kt + 2 < KT:
                    load_w(sp, n, n % 2, w_cols(a["w_out_2"], (kt + 2) * P))
                else:
                    load_w(sp, n, n % 2, w_cols(a["w_up_2"], (kt + 2 - KT) * P))
            sp.wait_ge(mm_done, U_UP2)
            for s in range(2):
                sp.wait_ge(src_stored[s], 16 * 16)
            for kt in range(KT):
                sp.dma_start(y[:, kt, :], residual[kt]).then_inc(y_loaded, 16)
            with sp.Fori(0, DOWN2 - 1) as c:
                load_down(sp, c, DOWN1 + c, a["w_down_2"])
                for k in range(2):
                    load_w(sp, U_UP2 + 2 * c + 2 + k, (U_UP2 + k) % 2,
                           w_cols(a["w_up_2"], c * (2 * P) + (k + 2) * P))
            load_down(sp, DOWN2 - 1, DOWN1 + DOWN2 - 1, a["w_down_2"])

        @block.gpsimd
        def _(pool):
            for steps in (rw_pool, diff.pool, fox.pool, band.pool):
                steps.start(pool)
            pool.sem_inc(d_lo, 1)
            nc.gpsimd.memset(ident[:, :], 0.0).then_inc(consts, 1)
            nc.gpsimd.memset(ones[:, :], 1.0).then_inc(consts, 1)
            nc.gpsimd.memset(small[:, 0:1], NORM_EPS).then_inc(consts, 1)
            pool.wait_ge(consts, 3)
            nc.gpsimd.memset(small[:, 1:2], RWKV_LN_EPS).then_inc(consts, 1)
            nc.gpsimd.memset(headones[:, :], 0.0).then_inc(consts, 1)
            pool.wait_ge(consts, 5)
            nc.gpsimd.affine_select(out=ident[:, :], in_=ident[:, :], compare_op=ALU.not_equal, fill=1.0,
                                    base=0, pattern=[[-1, P]], channel_multiplier=1).then_inc(consts, 1)
            for h in range(2):
                pool.wait_ge(consts, 6 + h)
                nc.gpsimd.memset(headones[64 * h:64 * h + 64, 64 * h:64 * h + 64], 1.0).then_inc(consts, 1)
            pool.wait_ge(consts, 8)
            made = [0]

            def mask(ins):
                ins.then_inc(masks, 1)
                made[0] += 1
                pool.wait_ge(masks, made[0])

            mask(nc.gpsimd.memset(chunk_mask[:, :], 1.0))
            mask(nc.gpsimd.memset(chunk_mask[:, 0:T:CHUNK], 0.0))
            mask(nc.gpsimd.memset(causal2[:, :, :], 1.0))
            mask(nc.gpsimd.memset(strict_t[:, :], 1.0))
            for k, op in enumerate((ALU.is_gt, ALU.is_ge)):
                mask(nc.gpsimd.affine_select(out=causal2[:, k, :], in_=causal2[:, k, :], compare_op=op, fill=0.0,
                                             base=0, pattern=[[1, P]], channel_multiplier=-1))
            mask(nc.gpsimd.affine_select(out=strict_t[:, :], in_=strict_t[:, :], compare_op=ALU.is_gt, fill=0.0,
                                         base=0, pattern=[[-1, P]], channel_multiplier=1))
            for c in range(NCH - 1):
                lo, hi = c * CHUNK, (c + 1) * CHUNK
                mask(nc.gpsimd.memset(causal2[lo:hi, :, hi:P], 0.0))
                mask(nc.gpsimd.memset(strict_t[hi:hi + CHUNK, 0:hi], 0.0))
            for s in range(2):
                split_lo(pool, s, s)
            pool.wait_ge(xt_done, KT)
            pool.wait_ge(w_lo, 2)
            for h in range(2):
                other = slice(64 - 64 * h, 128 - 64 * h)
                mask(nc.gpsimd.memset(bz[other, h, :], 0.0))
                mask(nc.gpsimd.memset(kz[other, h, :], 0.0))
            with pool.Fori(1, IN_TILES // 2) as i:
                for s in range(2):
                    split_lo(pool, 2 * i + s, s)
            for s in range(2):
                split_lo(pool, U_OUT + s, s)
            phase_end(pool, 1)
            rwkv_pool(pool)
            phase_end(pool, 2)
            mask(nc.gpsimd.iota(bias[:, 0, :], pattern=[[1, T]], base=-(T - P), channel_multiplier=-1,
                                allow_small_or_imprecise_dtypes=True))
            mask(nc.gpsimd.affine_select(out=bias[:, 0, :], in_=bias[:, 0, :], compare_op=ALU.is_ge, fill=NEG,
                                         base=T - P, pattern=[[-1, T]], channel_multiplier=1))
            mask(nc.gpsimd.memset(small[:, 3:4], SUBLN_EPS))
            phase_end(pool, 3)
            attention_pool(pool, diff, 4)
            phase_end(pool, 4)
            for n in range(U_OUT + 2, U_UP + 2):
                split_lo(pool, n, n % 2)
            post_norm_pool(pool, 0, 8, 16)
            for kt in range(KT):
                pool.wait_ge(added, kt + 1)
                nc.gpsimd.memset(y[:, kt, :], 0.0).then_inc(y_zero, 1)
            with pool.Fori(0, DOWN1) as c:
                for k in range(2, 6):
                    if k == 4:
                        split_down_lo(pool, c)
                    split_lo(pool, U_UP + 4 * c + k, k % 2)
            post_norm_pool(pool, 1, 16, 32)
            split_lo(pool, U_QKV2 + 1, (U_QKV2 + 1) % 2)
            pool.wait_ge(x_lo, 24)
            nc.gpsimd.memset(fa_ones[:, :], 1.0).then_inc(fa_set, 1)
            pool.wait_ge(rel_loaded, 16)
            nc.gpsimd.memset(rel[:, 0:REL - N_REL + 1], 0.0).then_inc(fa_set, 1)
            pool.wait_ge(fa_set, 2)
            first = REL - N_REL + 1
            nc.gpsimd.tensor_scalar(rel[:, 0:first], rel[:, 0:first], rel[:, first:first + 1], None, ALU.add)\
                .then_inc(rel_filled, 1)
            with pool.Fori(0, 20) as i:
                for k in range(2):
                    split_lo(pool, U_QKV2 + 2 + 2 * i + k, (U_QKV2 + k) % 2)
            mask(nc.gpsimd.memset(tri[:, :], 0.0))
            mask(nc.gpsimd.affine_select(out=tri[:, :], in_=tri[:, :], compare_op=ALU.is_ge, fill=NEG,
                                         base=0, pattern=[[-1, P]], channel_multiplier=1))
            phase_end(pool, 5)
            attention_pool(pool, fox, 0)
            phase_end(pool, 6)
            attention_pool(pool, band, 4)
            phase_end(pool, 7)
            for n in range(U_BRANCH + 2, U_UP2 + 2):
                split_lo(pool, n, n % 2)
            with pool.Fori(0, DOWN2 - 1) as c:
                for k in range(2, 4):
                    if k == 3:
                        split_down_lo(pool, DOWN1 + c)
                    split_lo(pool, U_UP2 + 2 * c + k, (U_UP2 + k) % 2)
            split_down_lo(pool, DOWN1 + DOWN2 - 1)

        @block.scalar
        def _(act):
            for steps in (rw_act, pre_act, diff.act, fox.act, band.act, diff.split_act, fox.split_act, band.split_act, ff1_act,
                          ff2_act):
                steps.start(act)
            act.wait_ge(cols_ready, 16)
            for s in range(2):
                split_hi(act, s, s, first=True)
            for kt in range(KT):
                s = kt % 2
                prep_act(act, kt, kt, "ln_attn_pre", (src_ready, kt + 1))
                act.dma_start(residual[kt], src[:, s, :]).then_inc(src_stored[s], 16)
            stat_root_act(act, 0)

            def store_stage(n, s, staged):
                act.wait_ge(staged[0], n + staged[1])
                act.dma_start(proj1[bass.ds(n, 1)].rearrange("a p n -> (a p) n"), stage[:, s, :])\
                    .then_inc(stage_stored[s], 16)

            for lo, hi, staged in ((0, SHIFTED_TILES // 2, (stage_ready, 2)),
                                   (SHIFTED_TILES // 2, IN_TILES // 2, (evac_done, 1))):
                with act.Fori(lo, hi) as i:
                    for s in range(2):
                        split_hi(act, 2 * i + 2 + s, s)
                        store_stage(2 * i + s, s, staged)
            act.wait_ge(lora_ready, 32)
            nc.scalar.activation(wa[0:64, :], wa[0:64, :], ACT.Tanh).then_inc(lora_act, 1)
            nc.scalar.activation(gl[:, :], gl[:, :], ACT.Sigmoid).then_inc(lora_act, 1)
            for s in range(2):
                act.wait_ge(stage_stored[s], 8 * IN_TILES + 1)
            phase_end(act, 1)
            for what in ("lora", "root", "decays"):
                prepare_act(act, 0, what)
            with act.Fori(0, RWKV_TILES - 1) as j:
                rwkv_act(act, j)
            rwkv_act(act, RWKV_TILES - 1, final=True)
            phase_end(act, 2)
            act.wait_ge(lam_dve, 2)
            nc.scalar.activation(lam_dots[:, 0:2], lam_dots[:, 0:2], ACT.Exp).then_inc(lam_act, 1)
            nc.scalar.activation(small[:, 4:5], col("diff_subln", 0), ACT.Copy, scale=1.0 - LAM_INIT)\
                .then_inc(lam_act, 1)
            phase_end(act, 3)
            attention_loop(act, attention_act, attention_split_act, diff, 4)
            phase_end(act, 4)
            for kt in range(KT):
                n = U_OUT + kt
                split_hi(act, n + 2, n % 2)
                act.wait_ge(mm_done, n + 1)
                nc.scalar.activation(y[:, kt, :], bank2(n % 2), ACT.Copy).then_inc(evac_done, 1)
                act.wait_ge(evac_done, n + 1)
                square_act(act, 8 + kt, y[:, kt, :])
            stat_root_act(act, 1, 1)
            post_norm_act(act, 0, 8, 16, "ln_ffn_pre")
            stat_root_act(act, 2)
            ff1_act_chunk(act, 0, 0)
            with act.Fori(0, DOWN1 // 2) as i:
                for h in range(2):
                    c = 2 * i + 1 + h
                    ff1_act_chunk(act, c, (1 + h) % 2)
            y_squares_act(act, DOWN1 - 1, 24)
            stat_root_act(act, 3, 2)
            post_norm_act(act, 1, 16, 32, "norm1_2")
            split_hi(act, U_FA + 2, U_FA % 2)
            stat_root_act(act, 4)
            act.wait_ge(fa_dve, 2)
            nc.scalar.activation(fa_abs[:, :], fa[:, :], ACT.Abs).then_inc(fa_act, 1)
            act.wait_ge(fa_act, 1)
            nc.scalar.activation(fa_abs[:, :], fa_abs[:, :], ACT.Exp, scale=-1.0).then_inc(fa_act, 1)
            act.wait_ge(fa_act, 2)
            nc.scalar.activation(fa_abs[:, :], fa_abs[:, :], ACT.Ln, bias=ones[0:FOX_HEADS, 0:1]).then_inc(fa_act, 1)
            with act.Fori(0, 20) as i:
                for k in range(2):
                    u = 2 * i + k
                    split_hi(act, U_QKV2 + 2 + u, (U_QKV2 + k) % 2)
                    act.wait_ge(evac_done, U_QKV2 + 1 + u)
                    act.dma_start(proj2[bass.ds(u, 1)].rearrange("a p n -> (a p) n"), stage[:, k, :])\
                        .then_inc(stage_stored[k], 16)
            for k in range(2):
                act.wait_ge(stage_stored[k], 16 * (IN_TILES // 2 + 20) + 1)
            phase_end(act, 5)
            attention_loop(act, attention_act, attention_split_act, fox, 0)
            phase_end(act, 6)
            attention_loop(act, attention_act, attention_split_act, band, 4)
            phase_end(act, 7)
            for m in range(KT):
                n = U_BRANCH + m
                act.wait_ge(gate_loaded[m % 2], 32 * (m // 2 + 1))
                nc.scalar.activation(gates[:, m % 2, :, :], gates[:, m % 2, :, :], ACT.Sigmoid)\
                    .then_inc(gate_done, 1)
                split_hi(act, n + 2, n % 2)
                act.wait_ge(merged_done, m + 1)
                nc.scalar.activation(xh2[:, m, :], merged[:, m % 2, :], ACT.Copy).then_inc(m_hi, 1)
            for kt in range(KT):
                n = U_OUT2 + kt
                split_hi(act, n + 2, n % 2)
                prep_act(act, 24 + kt, 40 + kt, "norm2_2", (evac_done, n + 1))
                act.dma_start(residual[kt], src[:, kt % 2, :]).then_inc(src_stored[kt % 2], 16)
            stat_root_act(act, 5, 3)
            ff2_act_chunk(act, 0, 0)
            with act.Fori(0, DOWN2 // 2 - 1) as i:
                for h in range(2):
                    c = 2 * i + 1 + h
                    ff2_act_chunk(act, c, (1 + h) % 2)
            ff2_act_chunk(act, DOWN2 - 1, 1, last=True)
            y_squares_act(act, DOWN1 + DOWN2 - 1, 48)
            act.wait_ge(out_sum, 1)
            nc.scalar.activation(token_rstd[:, :], ps[:, 6, 0:TT], ACT.Sqrt, bias=small[:, 0:1], scale=1.0 / D)\
                .then_inc(out_root, 1)
            act.wait_ge(out_root, 2)
            for t in range(TT):
                s = t % 2
                act.wait_ge(out_turned, t + 1)
                if t >= 2:
                    act.wait_ge(out_stored[s], 16 * (t // 2))
                nc.scalar.activation(out_tile[:, s, :], bank2(s), ACT.Copy, scale=token_rstd[:, t:t + 1])\
                    .then_inc(out_ready, 1)
                act.wait_ge(out_ready, t + 1)
                act.dma_start(out[t * P:(t + 1) * P, :], out_tile[:, s, :]).then_inc(out_stored[s], 16)
            for s in range(2):
                act.wait_ge(out_stored[s], 16 * TT // 2)

        @block.tensor
        def _(pe):
            for steps in (rw_pe, pre_pe, diff.pe, fox.pe, band.pe):
                steps.start(pe)
            pe.sem_inc(down_done, 1)
            pe.wait_ge(consts, 8)
            for s in range(2):
                pe.wait_ge(x_loaded[s], 16 * TT // 2)
            for kt in range(KT):
                s = kt % 2
                if kt >= 2:
                    pe.wait_ge(src_ready, kt - 1)
                for t in range(TT):
                    mm = nc.tensor.transpose(ps[:, 2 * s + t // 4, t % 4 * P:t % 4 * P + P],
                                             xin[:, t, kt * P:(kt + 1) * P], ident[:, :])
                mm.then_inc(xt_done, 1)
                if kt:
                    square_sum_pe(pe, kt - 1)
            square_sum_pe(pe, KT - 1)
            pe.wait_ge(src_ready, KT)
            for s in range(2):
                unit_products(pe, s, s, 0, first=True)
            with pe.Fori(1, IN_TILES // 2) as i:
                for s in range(2):
                    unit_products(pe, 2 * i + s, s, 0)
            phase_end(pe, 1)
            pe.wait_ge(lora_act, 2)
            for what in ("lora", "norm"):
                prepare_pe(pe, 0, what)
            with pe.Fori(0, RWKV_TILES - 1) as j:
                rwkv_pe(pe, j)
            rwkv_pe(pe, RWKV_TILES - 1, final=True)
            phase_end(pe, 2)
            pe.wait_ge(lam_dve, 3)
            nc.tensor.matmul(ps[:, 0, 0:1], ones[0:1, :], lam_dots[:, 2:3], start=True, stop=True).then_inc(lam_pe, 1)
            phase_end(pe, 3)
            with pe.Fori(0, DIFF_HEADS) as j:
                attention_pe(pe, diff, j)
            pe.drain().then_inc(phase, 1)
            for n in range(U_OUT, U_UP):
                unit_products(pe, n, n % 2, before=lambda kt: last_outputs(pe, diff, kt) if n == U_OUT else None)
            stat_products(pe, 16)
            unit_products(pe, U_UP, 0, 8, before=lambda kt: square_sum_pe(pe, 16 + kt))
            for k in range(1, 4):
                unit_products(pe, U_UP + k, k % 2)
            with pe.Fori(0, DOWN1 // 2) as i:
                for h in range(2):
                    c = 2 * i + 1 + h
                    for k in range(4):
                        if k == 2:
                            down_products(pe, ff1_dve, c - 1, c - 1, h)
                        unit_products(pe, U_UP + 4 * c + k, k % 2)
            down_products(pe, ff1_dve, DOWN1 - 1, DOWN1 - 1, (DOWN1 - 1) % 2)
            stat_products(pe, 32)
            unit_products(pe, U_FA, 0, 16, before=lambda kt: square_sum_pe(pe, 32 + kt))
            with pe.Fori(0, 20) as i:
                for k in range(2):
                    unit_products(pe, U_QKV2 + 2 * i + k, (U_QKV2 + k) % 2)
            phase_end(pe, 5)
            with pe.Fori(0, 4) as j:
                attention_pe(pe, fox, j)
            phase_end(pe, 6)
            with pe.Fori(0, 4) as j:
                attention_pe(pe, band, j)
            pe.drain().then_inc(phase, 1)
            for m in range(KT):
                n = U_BRANCH + m
                s = n % 2
                pe.wait_ge(w_lo, n + 1)
                pe.wait_ge(evac_done, n - 1)
                for kt in range(KT):
                    if m == 0:
                        last_outputs(pe, band, kt)
                    b = kt // 4
                    mm = three_products(4 * b + 2 * s, wh[:, s, kt, :], wl[:, s, kt, :], xh[:, kt, :], xl[:, kt, :],
                                        kt % 4 == 0, kt % 4 == 3)
                mm.then_inc(mm_done, 1)
            for n in range(U_OUT2, U_UP2):
                unit_products(pe, n, n % 2, x=(xh2, xl2),
                              before=lambda kt: pe.wait_ge(m_lo, kt + 1) if n == U_OUT2 else None)
            unit_products(pe, U_UP2, U_UP2 % 2, 24)
            stat_products(pe, 48)
            unit_products(pe, U_UP2 + 1, (U_UP2 + 1) % 2)
            with pe.Fori(0, DOWN2 // 2 - 1) as i:
                for h in range(2):
                    c = 2 * i + 1 + h
                    for k in range(2):
                        if k:
                            down_products(pe, ff2_dve, c - 1, DOWN1 - 1 + c, h)
                        unit_products(pe, U_UP2 + 2 * c + k, (U_UP2 + k) % 2)
            c = DOWN2 - 1
            for k in range(2):
                unit_products(pe, U_UP2 + 2 * c + k, (U_UP2 + k) % 2)
                down_products(pe, ff2_dve, c - 1 + k, DOWN1 - 1 + c + k, (c - 1 + k) % 2)
            pe.wait_ge(ss_done, 56)
            for t in range(TT):
                mm = nc.tensor.matmul(ps[:, 6, t:t + 1], ss[:, t * P:(t + 1) * P], ones[:, 0:1], start=True,
                                      stop=True)
            mm.then_inc(out_sum, 1)
            pe.wait_ge(gained, KT)
            for t in range(TT):
                if t >= 2:
                    pe.wait_ge(out_ready, t - 1)
                for kt in range(KT):
                    mm = nc.tensor.transpose(ps[:, 2 * (t % 2) + kt // 4, kt % 4 * P:kt % 4 * P + P],
                                             y[:, kt, t * P:(t + 1) * P], ident[:, :])
                mm.then_inc(out_turned, 1)

        @block.vector
        def _(dve):
            for steps in (rw_dve, pre_dve, diff.dve, fox.dve, band.dve, diff.split_dve, fox.split_dve, band.split_dve, ff1_dve,
                          ff2_dve):
                steps.start(dve)
            for counted in (stage_ready, down_added, *stage_stored):
                dve.sem_inc(counted, 1)
            nc.vector.memset(shifted[:, 0:1], 0.0).then_inc(shift_done, 1)
            dve.wait_ge(cols_ready, 16)
            for kt in range(KT + 1):
                s = kt % 2
                if kt < KT:
                    dve.wait_ge(xt_done, kt + 1)
                    if kt >= 2:
                        dve.wait_ge(x_lo, kt - 1)
                        dve.wait_ge(x_sq, kt - 1)
                        dve.wait_ge(src_stored[s], 16 * (kt // 2))
                    nc.vector.tensor_copy(src[:, s, :], bank2(s)).then_inc(src_ready, 1)
                if kt:
                    prep_dve(dve, kt - 1, kt - 1, "ln_attn_pre")
            stat_reciprocal(dve, 0)

            with dve.Fori(0, SHIFTED_TILES // 2) as i:
                for s in range(2):
                    n = 2 * i + s
                    dve.wait_ge(mm_done, n + 1)
                    dve.wait_ge(stage_ready, n + 1)
                    dve.wait_ge(shift_done, 1)
                    nc.vector.tensor_tensor(shifted[:, 1:T + 1], bank2(s), rstd[:, :], ALU.mult)\
                        .then_inc(evac_done, 1)
                    dve.wait_ge(evac_done, n + 1)
                    nc.vector.tensor_tensor(diff_t[:, :], shifted[:, 0:T], shifted[:, 1:T + 1], ALU.subtract)\
                        .then_inc(shift_done, 1)
                    dve.wait_ge(shift_done, n + 2)
                    dve.wait_ge(stage_stored[s], 16 * i + 1)
                    nc.vector.scalar_tensor_tensor(out=stage[:, s, :], in0=diff_t[:, :],
                                                   scalar=col_at("mu_shift", n), in1=shifted[:, 1:T + 1],
                                                   op0=ALU.mult, op1=ALU.add).then_inc(stage_ready, 1)
            with dve.Fori(SHIFTED_TILES // 2, IN_TILES // 2) as i:
                for s in range(2):
                    n = 2 * i + s
                    dve.wait_ge(mm_done, n + 1)
                    dve.wait_ge(stage_stored[s], 16 * i + 1)
                    nc.vector.tensor_tensor(stage[:, s, :], bank2(s), rstd[:, :], ALU.mult)\
                        .then_inc(evac_done, 1)
            phase_end(dve, 1)
            for what in ("sum", "clamp", "norm0", "norm1", "kk", "km"):
                prepare_dve(dve, 0, what)
            with dve.Fori(0, RWKV_TILES - 1) as j:
                rwkv_dve(dve, j)
            rwkv_dve(dve, RWKV_TILES - 1, final=True)
            phase_end(dve, 2)
            dve.wait_ge(lam_loaded, 16)
            for k in range(2):
                if k:
                    dve.wait_ge(lam_dve, k)
                nc.vector.tensor_tensor_reduce(lam_tmp[:, :], lam_row[:, 128 * k:128 * k + 64],
                                               lam_row[:, 128 * k + 64:128 * k + 128], 1.0, 0.0, ALU.mult, ALU.add,
                                               lam_dots[:, k:k + 1]).then_inc(lam_dve, 1)
            dve.wait_ge(lam_act, 1)
            nc.vector.scalar_tensor_tensor(out=lam_dots[:, 2:3], in0=lam_dots[:, 1:2], scalar=-LAM_INIT,
                                           in1=lam_dots[:, 0:1], op0=ALU.add, op1=ALU.subtract).then_inc(lam_dve, 1)
            dve.wait_ge(lam_pe, 1)
            nc.vector.tensor_copy(small[:, 2:3], ps[:, 0, 0:1]).then_inc(lam_dve, 1)
            phase_end(dve, 3)
            attention_loop(dve, attention_dve, attention_split_dve, diff)
            phase_end(dve, 4)
            for kt in range(KT):
                square_sum_dve(dve, 8 + kt)
            stat_reciprocal(dve, 1)
            post_norm(dve, "ln_attn_post", 8, 16, "ln_ffn_pre")
            stat_reciprocal(dve, 2)
            for s in range(2):
                dve.wait_ge(src_stored[s], 16 * 8)
                nc.vector.memset(ub[:, s, 0:2], 0.0).then_inc(ub_pads, 1)
            dve.wait_ge(ub_pads, 2)
            ff1_dve_chunk(dve, 0, 0)
            dve.wait_ge(y_zero, KT)
            with dve.Fori(0, DOWN1 // 2) as i:
                for h in range(2):
                    c = 2 * i + 1 + h
                    ff1_dve_chunk(dve, c, (1 + h) % 2, c - 1)
            down_add(dve, DOWN1 - 1, 24)
            stat_reciprocal(dve, 3)
            post_norm(dve, "ln_ffn_post", 16, 32, "norm1_2")
            stat_reciprocal(dve, 4)
            dve.wait_ge(mm_done, U_FA + 1)
            for s in range(2):
                dve.wait_ge(src_stored[s], 16 * 12)
            nc.vector.tensor_tensor(fa[:, :], ps[0:FOX_HEADS, 0:2, :].rearrange("p a n -> p (a n)"),
                                    rstd[0:FOX_HEADS, :], ALU.mult).then_inc(evac_done, 1)
            dve.wait_ge(fa_loaded, 16)
            dve.wait_ge(evac_done, U_FA + 1)
            nc.vector.tensor_scalar(fa[:, :], fa[:, :], small[0:FOX_HEADS, 5:6], None, ALU.add).then_inc(fa_dve, 1)
            dve.wait_ge(fa_dve, 1)
            nc.vector.tensor_scalar(cneg[:, :], fa[:, :], 0.0, None, ALU.min).then_inc(fa_dve, 1)
            dve.wait_ge(fa_act, 3)
            dve.wait_ge(fa_dve, 2)
            nc.vector.tensor_tensor(fa[:, :], fa_abs[:, :], cneg[:, :], ALU.subtract).then_inc(fa_dve, 1)
            dve.wait_ge(fa_dve, 3)
            dve.wait_ge(fa_set, 1)
            nc.vector.tensor_tensor_scan(cneg[:, :], fa_ones[:, :], fa[:, :], 0.0, ALU.mult, ALU.add)\
                .then_inc(fa_dve, 1)
            with dve.Fori(0, 20) as i:
                for k in range(2):
                    n = U_QKV2 + 2 * i + k
                    dve.wait_ge(mm_done, n + 1)
                    dve.wait_ge(stage_stored[k], 16 * (IN_TILES // 2) + 16 * i + 1)
                    nc.vector.tensor_tensor(stage[:, k, :], bank2((U_QKV2 + k) % 2), rstd[:, :], ALU.mult)\
                        .then_inc(evac_done, 1)
            phase_end(dve, 5)
            attention_loop(dve, attention_dve, attention_split_dve, fox)
            phase_end(dve, 6)
            attention_loop(dve, attention_dve, attention_split_dve, band)
            phase_end(dve, 7)
            for m in range(KT):
                n = U_BRANCH + m
                s = n % 2
                dve.wait_ge(mm_done, n + 1)
                dve.wait_ge(gate_done, m + 1)
                nc.vector.tensor_tensor(gated[:, m % 2, :], bank2(s), gates[:, m % 2, 0, :], ALU.mult)\
                    .then_inc(gated_a, 1)
                if m >= 2:
                    dve.wait_ge(m_lo, m - 1)
                nc.vector.tensor_tensor(merged[:, m % 2, :], bank2(2 + s), gates[:, m % 2, 1, :], ALU.mult)\
                    .then_inc(gated_b, 1)
                dve.wait_ge(gated_a, m + 1)
                dve.wait_ge(gated_b, m + 1)
                nc.vector.tensor_tensor(merged[:, m % 2, :], merged[:, m % 2, :], gated[:, m % 2, :], ALU.add)\
                    .then_inc(merged_done, 1)
                dve.wait_ge(merged_done, m + 1)
                dve.drain().then_inc(evac_done, 1)
                dve.wait_ge(m_hi, m + 1)
                nc.vector.tensor_tensor(xl2[:, m, :], merged[:, m % 2, :], xh2[:, m, :].bitcast(F32),
                                        ALU.subtract).then_inc(m_lo, 1)
            for kt in range(KT):
                n, r, s = U_OUT2 + kt, 24 + kt, kt % 2
                dve.wait_ge(mm_done, n + 1)
                dve.wait_ge(h2_loaded[s], 16 * (kt // 2 + 1))
                dve.wait_ge(src_stored[s], 16 * (r // 2))
                if kt >= 2:
                    dve.wait_ge(x_sq, 40 + kt - 1)
                    dve.wait_ge(x_lo, r - 1)
                nc.vector.tensor_tensor(src[:, s, :], bank2(n % 2), hres2[:, s, :], ALU.add).then_inc(evac_done, 1)
                prep_dve(dve, r, 40 + kt, "norm2_2", sums=True)
            stat_reciprocal(dve, 5)
            for s in range(2):
                dve.wait_ge(src_stored[s], 16 * 16)
            ff2_dve_chunk(dve, 0, 0)
            dve.wait_ge(y_loaded, 16 * KT)
            with dve.Fori(0, DOWN2 // 2 - 1) as i:
                for h in range(2):
                    c = 2 * i + 1 + h
                    ff2_dve_chunk(dve, c, (1 + h) % 2, DOWN1 - 1 + c)
            ff2_dve_chunk(dve, DOWN2 - 1, 1, DOWN1 + DOWN2 - 2)
            down_add(dve, DOWN1 + DOWN2 - 1, 48)
            dve.wait_ge(out_root, 1)
            nc.vector.reciprocal(token_rstd[:, :], token_rstd[:, :]).then_inc(out_root, 1)
            for kt in range(KT):
                nc.vector.tensor_scalar(y[:, kt, :], y[:, kt, :], col("final_norm_2", kt), None, ALU.mult)\
                    .then_inc(gained, 1)


_NAMES = ["x", "w_in", "w_decay_up", "w_iclr_up", "w_gate_up", "w_out", "w_up", "w_down", "w_in_2",
          "w_out_2", "w_up_2", "w_down_2"]


def kernel(**inputs):
    from concourse import bacc
    from concourse.bass_utils import run_bass_kernel_spmd

    arrays = {}
    for name in _NAMES:
        w = np.asarray(inputs[name])
        arrays[name] = np.ascontiguousarray(w.reshape(w.shape[-2:]))
    packed = [np.asarray(inputs[name]).reshape(tiles, P) for name, tiles in VECTORS]
    arrays["vectors"] = np.ascontiguousarray(np.concatenate(packed).T)
    arrays["lambdas"] = np.stack([np.asarray(inputs[f"lambda_{k}"]).reshape(-1) for k in ("q1", "k1", "q2", "k2")])
    arrays["forget_bias"] = np.asarray(inputs["forget_bias_2"]).reshape(FOX_HEADS, 1)
    arrays["w_branch"] = np.concatenate([np.asarray(inputs[f"w_branch_{k}_2"])[0] for k in "ab"])
    arrays["rel_bias"] = np.ascontiguousarray(np.asarray(inputs["rel_bias_2"])[0, :, ::-1])
    nc = bacc.Bacc("TRN2", target_bir_lowering=False, num_devices=1)
    aps = {n: nc.dram_tensor(f"in_{n}", v.shape, F32, kind="ExternalInput").ap() for n, v in arrays.items()}
    out = nc.dram_tensor("out", (T, D), F32, kind="ExternalOutput").ap()
    build_program(nc, aps, out)
    r = run_bass_kernel_spmd(nc, [{f"in_{n}": v for n, v in arrays.items()}], core_ids=[0])
    return np.asarray(r.results[0]["out"]).reshape(1, T, D)
```
